# Optimizing a Trainium2 kernel written in Bass

```python
import jax, jax.numpy as jnp
from jax import lax
import numpy as np

D_MODEL = 1024
BATCH = 1
SEQ = 1024
DEPTH = 2

GRID_W = 64
CTX_LEN = 256
N_MOD = 6
EPS = 1e-6
ROPE_BASE = 10000.0
QBLK = 128
NEG_INF = -1e30
A_HEADS = 12
A_NOPE = 64
A_ROPE = 32
A_QK = A_NOPE + A_ROPE
A_V = 64
A_Q_LORA = 256
A_KV_LORA = 128
A_IN = A_Q_LORA + A_KV_LORA + A_ROPE
B_GROUPS = 4
B_GDIM = 64
B_WIDTH = B_GROUPS * B_GDIM
EVEN_IN = A_IN + B_WIDTH
EVEN_MIX = A_HEADS * A_V + B_WIDTH
C_HEADS = 12
C_KV_HEADS = 4
C_GROUP = C_HEADS // C_KV_HEADS
C_HDIM = 64
C_WINDOW = 128
C_QW = C_HEADS * C_HDIM
C_KW = C_KV_HEADS * C_HDIM
D_GROUPS = 4
D_GDIM = 64
D_WIDTH = D_GROUPS * D_GDIM
D_WINDOWS = (2, 4, 8, 16)
ODD_IN = C_QW + 2 * C_KW + D_WIDTH
ODD_MIX = C_QW + D_WIDTH
D_FF = 2816
CONV_W = 3
N_EVEN = (DEPTH + 1) // 2
N_ODD = DEPTH // 2

kernel_name = 'hybrid_mla_fnet_swa_pool_dit'

def rmsnorm(x, g):
    xf = x.astype(jnp.float32)
    y = xf * lax.rsqrt(jnp.mean(xf * xf, axis=-1, keepdims=True) + EPS)
    return (y * g.astype(jnp.float32)).astype(x.dtype)

def modulate(u, shift, scale):
    return u * (1 + scale) + shift

def axial_rope_tables(rows, rot_dim, dtype):
    n_freq = rot_dim // 4
    inv = ROPE_BASE ** (-jnp.arange(n_freq, dtype=jnp.float32) / n_freq)
    row = jnp.broadcast_to(jnp.arange(rows, dtype=jnp.float32)[:, None], (rows, GRID_W)).reshape(-1)
    col = jnp.broadcast_to(jnp.arange(GRID_W, dtype=jnp.float32)[None, :], (rows, GRID_W)).reshape(-1)
    ang = jnp.concatenate([row[:, None] * inv, col[:, None] * inv], axis=-1)
    return jnp.cos(ang).astype(dtype), jnp.sin(ang).astype(dtype)

def apply_rope(x, cos, sin):
    h = x.shape[-1] // 2
    x1, x2 = x[..., :h], x[..., h:]
    cs, sn = cos[None, :, None, :], sin[None, :, None, :]
    return jnp.concatenate([x1 * cs - x2 * sn, x1 * sn + x2 * cs], axis=-1)

def attend_grouped(q, k, v, scale, sink=None):
    s = jnp.einsum('bqkgd,bskd->bkgqs', q, k).astype(jnp.float32) * scale
    if sink is not None:
        sk = jnp.broadcast_to(sink.astype(jnp.float32)[None, :, :, None, None], s.shape[:-1] + (1,))
        s = jnp.concatenate([s, sk], axis=-1)
    p = jax.nn.softmax(s, axis=-1)[..., :k.shape[1]].astype(v.dtype)
    return jnp.einsum('bkgqs,bskd->bqkgd', p, v)

def latent_dense_attention(q, k, v, k_ctx, v_ctx, scale):
    B, L, H, dq = q.shape
    nb = L // QBLK
    n_ctx = k_ctx.shape[1]
    qb = jnp.moveaxis(q.reshape(B, nb, QBLK, H, dq), 1, 0)

    def block(qi):
        s = jnp.concatenate([jnp.einsum('bqhd,bchd->bhqc', qi, k_ctx),
                             jnp.einsum('bqhd,bkhd->bhqk', qi, k)], axis=-1).astype(jnp.float32) * scale
        p = jax.nn.softmax(s, axis=-1).astype(v.dtype)
        return (jnp.einsum('bhqc,bchd->bqhd', p[..., :n_ctx], v_ctx)
                + jnp.einsum('bhqk,bkhd->bqhd', p[..., n_ctx:], v))

    o = lax.map(block, qb)
    return jnp.moveaxis(o, 0, 1).reshape(B, L, -1)

def window_attention(q, k, v, k_ctx, v_ctx, sink, scale):
    B, L = q.shape[:2]
    nb = L // QBLK
    n_ctx = k_ctx.shape[1]
    span = 3 * QBLK
    pad = ((0, 0), (QBLK, QBLK), (0, 0), (0, 0))
    k_pad, v_pad = jnp.pad(k, pad), jnp.pad(v, pad)
    qb = jnp.moveaxis(q.reshape((B, nb, QBLK) + q.shape[2:]), 1, 0)
    rel = jnp.arange(span)[None, :] - QBLK - jnp.arange(QBLK)[:, None]
    band = jnp.abs(rel) <= C_WINDOW
    sink_col = jnp.broadcast_to(sink.astype(jnp.float32)[None, :, :, None, None], (B, C_KV_HEADS, C_GROUP, QBLK, 1))

    def block(args):
        i, qi = args
        start = i * QBLK
        ki = lax.dynamic_slice_in_dim(k_pad, start, span, axis=1)
        vi = lax.dynamic_slice_in_dim(v_pad, start, span, axis=1)
        key_pos = start - QBLK + jnp.arange(span)
        valid = band & ((key_pos >= 0) & (key_pos < L))[None, :]
        s_ctx = jnp.einsum('bqkgd,bckd->bkgqc', qi, k_ctx).astype(jnp.float32) * scale
        s_win = jnp.einsum('bqkgd,bskd->bkgqs', qi, ki).astype(jnp.float32) * scale
        s_win = jnp.where(valid, s_win, NEG_INF)
        p = jax.nn.softmax(jnp.concatenate([s_ctx, s_win, sink_col], axis=-1), axis=-1).astype(v.dtype)
        return (jnp.einsum('bkgqc,bckd->bqkgd', p[..., :n_ctx], v_ctx)
                + jnp.einsum('bkgqs,bskd->bqkgd', p[..., n_ctx:n_ctx + span], vi))

    o = lax.map(block, (jnp.arange(nb), qb))
    return jnp.moveaxis(o, 0, 1).reshape(B, L, C_QW)

def fourier_mix(u, w_f):
    B, L, _ = u.shape
    z = u.reshape(B, L, B_GROUPS, B_GDIM).astype(jnp.float32)
    z = jnp.fft.fft2(z, axes=(1, 3), norm='ortho').real.astype(u.dtype)
    return jnp.einsum('blgc,gcd->blgd', z, w_f).reshape(B, L, B_WIDTH)

def multiscale_pool(u, w_p, p_scale):
    B, L, _ = u.shape
    z = u.reshape(B, L, D_GROUPS, D_GDIM).astype(jnp.float32)
    cs = jnp.concatenate([jnp.zeros((B, 1, D_GROUPS, D_GDIM), jnp.float32), jnp.cumsum(z, axis=1)], axis=1)
    t = jnp.arange(L)[:, None]
    half = jnp.asarray(D_WINDOWS, jnp.int32)[None, :] // 2
    lo = jnp.clip(t - half, 0, L)
    hi = jnp.clip(t + half, 0, L)
    grp = jnp.arange(D_GROUPS)[None, :]
    win_sum = cs[:, hi, grp, :] - cs[:, lo, grp, :]
    mean = win_sum / (hi - lo).astype(jnp.float32)[None, :, :, None]
    pooled = (mean - z).astype(u.dtype)
    y = jnp.einsum('blgc,gcd->blgd', pooled, w_p).reshape(B, L, D_WIDTH)
    return y * p_scale

def mla_keys_values(h, ckv_g, w_ukv, k_g):
    B, L, _ = h.shape
    ckv = h[..., A_Q_LORA:A_Q_LORA + A_KV_LORA]
    k_rope = h[..., A_Q_LORA + A_KV_LORA:A_IN]
    kv = (rmsnorm(ckv, ckv_g) @ w_ukv).reshape(B, L, A_HEADS, A_NOPE + A_V)
    k = jnp.concatenate([kv[..., :A_NOPE], jnp.broadcast_to(k_rope[:, :, None, :], (B, L, A_HEADS, A_ROPE))], axis=-1)
    return rmsnorm(k, k_g), kv[..., A_NOPE:]

def mla_queries(h, cq_g, w_uq, q_g):
    B, L, _ = h.shape
    q = (rmsnorm(h[..., :A_Q_LORA], cq_g) @ w_uq).reshape(B, L, A_HEADS, A_QK)
    return rmsnorm(q, q_g)

def rope_tail(x, cos, sin):
    return jnp.concatenate([x[..., :A_NOPE], apply_rope(x[..., A_NOPE:], cos, sin)], axis=-1)

def even_mixer(u_ctx, u_lat, w_in, cq_g, ckv_g, w_uq, w_ukv, q_g, k_g, w_f, w_out, cos, sin, ctx_out):
    scale = A_QK ** -0.5
    B, L, _ = u_lat.shape
    h_ctx = u_ctx @ w_in
    h_lat = u_lat @ w_in
    k_ctx, v_ctx = mla_keys_values(h_ctx, ckv_g, w_ukv, k_g)
    k_lat, v_lat = mla_keys_values(h_lat, ckv_g, w_ukv, k_g)
    q_lat = rope_tail(mla_queries(h_lat, cq_g, w_uq, q_g), cos, sin)
    k_lat = rope_tail(k_lat, cos, sin)
    o_lat = latent_dense_attention(q_lat, k_lat, v_lat, k_ctx, v_ctx, scale)
    y_lat = jnp.concatenate([o_lat, fourier_mix(h_lat[..., A_IN:], w_f)], axis=-1) @ w_out
    y_ctx = None
    if ctx_out:
        Bc, C, _ = u_ctx.shape
        q_ctx = mla_queries(h_ctx, cq_g, w_uq, q_g)[:, :, :, None, :]
        o_ctx = attend_grouped(q_ctx, k_ctx, v_ctx, scale).reshape(Bc, C, -1)
        y_ctx = jnp.concatenate([o_ctx, fourier_mix(h_ctx[..., A_IN:], w_f)], axis=-1) @ w_out
    return y_ctx, y_lat

def gqa_keys_values(h, k_g):
    B, L, _ = h.shape
    k = rmsnorm(h[..., C_QW:C_QW + C_KW].reshape(B, L, C_KV_HEADS, C_HDIM), k_g)
    v = h[..., C_QW + C_KW:C_QW + 2 * C_KW].reshape(B, L, C_KV_HEADS, C_HDIM)
    return k, v

def gqa_queries(h, q_g):
    B, L, _ = h.shape
    return rmsnorm(h[..., :C_QW].reshape(B, L, C_HEADS, C_HDIM), q_g)

def odd_mixer(u_ctx, u_lat, w_in, q_g, k_g, sink, w_p, p_scale, w_out, cos, sin, ctx_out):
    scale = C_HDIM ** -0.5
    B, L, _ = u_lat.shape
    h_ctx = u_ctx @ w_in
    h_lat = u_lat @ w_in
    k_ctx, v_ctx = gqa_keys_values(h_ctx, k_g)
    k_lat, v_lat = gqa_keys_values(h_lat, k_g)
    q_lat = apply_rope(gqa_queries(h_lat, q_g), cos, sin).reshape(B, L, C_KV_HEADS, C_GROUP, C_HDIM)
    k_lat = apply_rope(k_lat, cos, sin)
    o_lat = window_attention(q_lat, k_lat, v_lat, k_ctx, v_ctx, sink, scale)
    y_lat = jnp.concatenate([o_lat, multiscale_pool(h_lat[..., C_QW + 2 * C_KW:], w_p, p_scale)], axis=-1) @ w_out
    y_ctx = None
    if ctx_out:
        Bc, C, _ = u_ctx.shape
        q_ctx = gqa_queries(h_ctx, q_g).reshape(Bc, C, C_KV_HEADS, C_GROUP, C_HDIM)
        o_ctx = attend_grouped(q_ctx, k_ctx, v_ctx, scale, sink).reshape(Bc, C, C_QW)
        y_ctx = jnp.concatenate([o_ctx, multiscale_pool(h_ctx[..., C_QW + 2 * C_KW:], w_p, p_scale)], axis=-1) @ w_out
    return y_ctx, y_lat

def conv_ffn(u, w_up, conv_w, conv_b, w_down):
    h = u @ w_up
    hp = jnp.pad(h, ((0, 0), (1, 1), (0, 0)))
    h = hp[:, :-2] * conv_w[0] + hp[:, 1:-1] * conv_w[1] + hp[:, 2:] * conv_w[2] + conv_b
    return (jax.nn.silu(h[..., :D_FF]) * h[..., D_FF:]) @ w_down

def setup_inputs(seed: int = 0) -> dict:
    key = jax.random.key(seed)
    ks = iter(jax.random.split(key, 32))
    D = D_MODEL

    def nrm(shape, scale):
        return jax.random.normal(next(ks), shape, jnp.float32) * scale

    def gain(shape):
        return 1.0 + nrm(shape, 0.02)

    return {
        'x': nrm((BATCH, SEQ, D), 1.0),
        'c': nrm((BATCH, D), 1.0),
        'ctx': nrm((BATCH, CTX_LEN, D), 1.0),
        'c_ctx': nrm((D,), 1.0),
        'mod_w': nrm((DEPTH, D, N_MOD * D), 0.5 * D ** -0.5),
        'mod_b': nrm((DEPTH, N_MOD * D), 0.01),
        'norm1_g': gain((DEPTH, D)),
        'norm2_g': gain((DEPTH, D)),
        'mla_w_in': nrm((N_EVEN, D, EVEN_IN), D ** -0.5),
        'mla_cq_g': gain((N_EVEN, A_Q_LORA)),
        'mla_ckv_g': gain((N_EVEN, A_KV_LORA)),
        'mla_w_uq': nrm((N_EVEN, A_Q_LORA, A_HEADS * A_QK), A_Q_LORA ** -0.5),
        'mla_w_ukv': nrm((N_EVEN, A_KV_LORA, A_HEADS * (A_NOPE + A_V)), A_KV_LORA ** -0.5),
        'mla_q_g': gain((N_EVEN, A_QK)),
        'mla_k_g': gain((N_EVEN, A_QK)),
        'fnet_w': nrm((N_EVEN, B_GROUPS, B_GDIM, B_GDIM), B_GDIM ** -0.5),
        'even_w_out': nrm((N_EVEN, EVEN_MIX, D), EVEN_MIX ** -0.5),
        'win_w_in': nrm((N_ODD, D, ODD_IN), D ** -0.5),
        'win_q_g': gain((N_ODD, C_HDIM)),
        'win_k_g': gain((N_ODD, C_HDIM)),
        'win_sink': nrm((N_ODD, C_KV_HEADS, C_GROUP), 0.5),
        'pool_w': nrm((N_ODD, D_GROUPS, D_GDIM, D_GDIM), D_GDIM ** -0.5),
        'pool_scale': 0.5 + nrm((N_ODD, D_WIDTH), 0.1),
        'odd_w_out': nrm((N_ODD, ODD_MIX, D), ODD_MIX ** -0.5),
        'ffn_up': nrm((DEPTH, D, 2 * D_FF), D ** -0.5),
        'ffn_conv_w': nrm((DEPTH, CONV_W, 2 * D_FF), CONV_W ** -0.5),
        'ffn_conv_b': nrm((DEPTH, 2 * D_FF), 0.01),
        'ffn_down': nrm((DEPTH, D_FF, D), D_FF ** -0.5),
    }

def reference(x, c, ctx, c_ctx, mod_w, mod_b, norm1_g, norm2_g,
              mla_w_in, mla_cq_g, mla_ckv_g, mla_w_uq, mla_w_ukv, mla_q_g, mla_k_g, fnet_w, even_w_out,
              win_w_in, win_q_g, win_k_g, win_sink, pool_w, pool_scale, odd_w_out,
              ffn_up, ffn_conv_w, ffn_conv_b, ffn_down):
    rows = x.shape[1] // GRID_W
    cos_a, sin_a = axial_rope_tables(rows, A_ROPE, x.dtype)
    cos_w, sin_w = axial_rope_tables(rows, C_HDIM, x.dtype)
    h_ctx = ctx
    for i in range(DEPTH):
        ctx_out = i < DEPTH - 1
        j = i // 2
        m_lat = jnp.split((jax.nn.silu(c) @ mod_w[i] + mod_b[i])[:, None, :], N_MOD, axis=-1)
        m_ctx = jnp.split(jax.nn.silu(c_ctx) @ mod_w[i] + mod_b[i], N_MOD, axis=-1)
        u_lat = modulate(rmsnorm(x, norm1_g[i]), m_lat[0], m_lat[1])
        u_ctx = modulate(rmsnorm(h_ctx, norm1_g[i]), m_ctx[0], m_ctx[1])
        if i % 2 == 0:
            y_ctx, y_lat = even_mixer(u_ctx, u_lat, mla_w_in[j], mla_cq_g[j], mla_ckv_g[j], mla_w_uq[j], mla_w_ukv[j],
                                      mla_q_g[j], mla_k_g[j], fnet_w[j], even_w_out[j], cos_a, sin_a, ctx_out)
        else:
            y_ctx, y_lat = odd_mixer(u_ctx, u_lat, win_w_in[j], win_q_g[j], win_k_g[j], win_sink[j],
                                     pool_w[j], pool_scale[j], odd_w_out[j], cos_w, sin_w, ctx_out)
        x = x + m_lat[2] * y_lat
        x = x + m_lat[5] * conv_ffn(modulate(rmsnorm(x, norm2_g[i]), m_lat[3], m_lat[4]),
                                    ffn_up[i], ffn_conv_w[i], ffn_conv_b[i], ffn_down[i])
        if ctx_out:
            h_ctx = h_ctx + m_ctx[2] * y_ctx
            h_ctx = h_ctx + m_ctx[5] * conv_ffn(modulate(rmsnorm(h_ctx, norm2_g[i]), m_ctx[3], m_ctx[4]),
                                                ffn_up[i], ffn_conv_w[i], ffn_conv_b[i], ffn_down[i])
    return x


_drawn_inputs = setup_inputs


def setup_inputs(seed=0):
    import zlib

    import numpy as np

    out = dict(_drawn_inputs(seed))
    spreads = {}
    factors = {'ctx': 3.727,
     'mod_b': 4.363,
     'norm1_g': 8.0,
     'norm2_g': 6.51,
     'mla_cq_g': 8.0,
     'mla_ckv_g': 8.0,
     'mla_q_g': 8.0,
     'mla_k_g': 8.0,
     'win_q_g': 8.0,
     'win_k_g': 8.0,
     'win_sink': 8.0,
     'pool_scale': 4.642,
     'ffn_conv_b': 8.0}
    for name, (base, spread) in spreads.items():
        noise = np.random.default_rng([zlib.crc32(name.encode()), seed]).standard_normal(out[name].shape)
        drawn = base * np.exp(spread * noise) if base else spread * noise
        out[name] = __import__('jax').numpy.asarray(drawn.astype(out[name].dtype))
    for name, factor in factors.items():
        out[name] = (out[name] * factor).astype(out[name].dtype)
    return out
```

```python
from contextlib import ExitStack

import numpy as np

import concourse.bass as bass
from concourse import mybir

F32 = mybir.dt.float32
BF16 = mybir.dt.bfloat16
ALU = mybir.AluOpType
ACT = mybir.ActivationFunctionType
AX_X = mybir.AxisListType.X
ds = bass.ds

P = 128
D = 1024
KT = D // P
SEQ, CTX = 1024, 256
T = SEQ + CTX
GRID_W = 64
DEPTH = 2
N_MOD = 6
EPS = 1e-6
BANK = 512
CH = [(0, 512), (512, 1024), (1024, 1280)]
STREAMS = [(0, SEQ, 0), (SEQ, T, 1)]

A_HEADS, A_NOPE, A_ROPE, A_V = 12, 64, 32, 64
A_QK = A_NOPE + A_ROPE
A_SCALE = A_QK ** -0.5
C_HEADS, C_KV, C_HD = 12, 4, 64
C_GROUP = C_HEADS // C_KV
C_SCALE = C_HD ** -0.5
D_FF = 2816
FT = D_FF // P
FG = FT // 2
MASKED = -1e30

C_IDENT, C_ONES, C_BONES, C_R0, C_R1, C_SEL, C_GE, C_LE, C_COSC, C_SINC = [i * P for i in range(10)]
N_CONST = 10 * P
(W_MODB, W_NG, W_CQG, W_CKVG, W_G0, W_G1, W_SINK, W_PS, W_FN, W_PW) = np.cumsum(
    [0, 192, 4 * KT * 2, 2, 1, 2, 2, 12, 2, 256]).tolist()

N_SMALL = W_PW + 256


def constants():
    c = np.zeros((P, N_CONST), np.float32)
    i = np.arange(P)
    c[:, C_IDENT:C_IDENT + P] = np.eye(P)
    c[:, C_ONES:C_ONES + P] = 1
    c[:, C_BONES:C_BONES + P] = (i[:, None] // 64) == (i[None, :] // 64)
    for m in range(16):
        c[64 + m + 16, C_R0 + 64 + m] = -1
        c[64 + m, C_R0 + 64 + m + 16] = 1
    for b in (0, 64):
        for m in range(32):
            c[b + m + 32, C_R1 + b + m] = -1
            c[b + m, C_R1 + b + m + 32] = 1
    c[64, C_SEL:C_SEL + 64] = 1
    c[:, C_GE:C_GE + P] = np.where(i[None, :] >= i[:, None], 0, MASKED)
    c[:, C_LE:C_LE + P] = np.where(i[None, :] <= i[:, None], 0, MASKED)
    ang = 2 * np.pi * np.outer(np.arange(64), np.arange(64)) / 64
    for b in (0, 64):
        c[b:b + 64, C_COSC + b:C_COSC + b + 64] = np.cos(ang) / 256
        c[b:b + 64, C_SINC + b:C_SINC + b + 64] = -np.sin(ang) / 256
    t = np.arange(SEQ)

    def rope(dim):
        n = dim // 4
        inv = np.float32(10000.0) ** (-np.arange(n, dtype=np.float32) / np.float32(n))
        row, col = (t // GRID_W).astype(np.float32), (t % GRID_W).astype(np.float32)
        a = np.concatenate([row[:, None] * inv, col[:, None] * inv], axis=-1)
        return np.cos(a).T.astype(np.float32), np.sin(a).T.astype(np.float32)

    rope0 = np.zeros((A_QK, 2, T), np.float32)
    rope0[:, 0] = 1
    cs, sn = rope(A_ROPE)
    for b in (64, 80):
        rope0[b:b + 16, 0, :SEQ], rope0[b:b + 16, 1, :SEQ] = cs, sn
    rope1 = np.zeros((P, 2, T), np.float32)
    rope1[:, 0] = 1
    cs, sn = rope(C_HD)
    for b in (0, 32, 64, 96):
        rope1[b:b + 32, 0, :SEQ], rope1[b:b + 32, 1, :SEQ] = cs, sn

    def dft(n, scale):
        k = np.outer(np.arange(n), np.arange(n)) % n
        a = 2 * np.pi * k / n
        m = np.stack([np.cos(a), np.sin(a)], 1) * scale
        return m.astype(np.float32).reshape(n // P, P, 2, n)

    half = np.array([1, 2, 4, 8])
    cnt = np.clip(t[None] + half[:, None], 0, SEQ) - np.clip(t[None] - half[:, None], 0, SEQ)
    inv = np.repeat(1.0 / cnt, 64, axis=0).reshape(2, P, SEQ).transpose(1, 0, 2).astype(np.float32)
    return {"const": c, "rope0": rope0, "rope1": rope1, "dft": dft(SEQ, 1), "dftc": dft(CTX, 2),
            "pool_inv": np.ascontiguousarray(inv)}


def program(nc, a, out):
    ctx = ExitStack()
    with ctx:
        def sb(name, shape, dt=F32):
            return ctx.enter_context(nc.sbuf_tensor(name, shape, dt))

        held = []

        def sem(name):
            held.append(nc.alloc_semaphore(name))
            return held[-1]

        def recycle():
            nc.clear_and_free_semaphores(list(held))
            held.clear()
            nc.all_engine_barrier()

        X = sb("X", [P, KT, T])
        U = sb("U", [P, KT, T])
        cst = sb("cst", [P, N_CONST])
        sml = sb("sml", [P, N_SMALL])
        mod = sb("mod", [P, DEPTH * N_MOD * KT, 2])
        gsc = sb("gsc", [P, DEPTH * 2 * KT, 2])
        eps = sb("eps", [P, 1])
        identb = sb("identb", [P, P], BF16)
        maskb = sb("maskb", [P, 2, P], BF16)
        rot0 = sb("rot0", [A_QK, 2, A_QK])
        rot1 = sb("rot1", [P, 2, P])
        BIGN = 33200
        BIG = sb("BIG", [P, BIGN])
        PS = ctx.enter_context(nc.psum_tensor("PS", [P, 8 * BANK], F32))

        def big(off, *shape):
            n = int(np.prod(shape))
            assert off + n <= BIGN, (off, n)
            v = BIG[:, off:off + n]
            if len(shape) == 2:
                v = v.rearrange("p (x y) -> p x y", x=shape[0])
            if len(shape) == 3:
                v = v.rearrange("p (x y z) -> p x y z", x=shape[0], y=shape[1])
            return v

        def ps(bank, n, rows=slice(0, P)):
            return PS[rows, bank * BANK:bank * BANK + n]

        ident = cst[:, C_IDENT:C_IDENT + P]
        ones = cst[:, C_ONES:C_ONES + P]
        bones = cst[:, C_BONES:C_BONES + P]

        def moda(layer, which, tile, s, n=1):
            return mod[:, ds((layer * N_MOD + which) * KT + tile, n), s]

        def mods():
            sil = big(0, KT, 2)
            cT = big(16, KT, 2)
            row = big(32, 2, BANK)
            W = [big(2048 + b * KT * BANK, KT, BANK) for b in range(2)]
            NC = DEPTH * N_MOD * D // BANK
            with ExitStack() as c2:
                s = {n: sem("mod_" + n) for n in
                     ("in", "sil", "w0", "w1", "rows0", "rows1", "rowc0", "rowc1", "cols0", "cols1", "out0", "out1",
                      "dve")}
                block = c2.enter_context(nc.Block())

                @block.sync
                def _(sp):
                    sp.dma_start(cT, a["cT"]).then_inc(s["in"], 16)
                    sp.dma_start(sml[:, :], a["small"]).then_inc(s["in"], 16)
                    sp.dma_start(cst[:, :], a["const"]).then_inc(s["in"], 16)
                    sp.dma_start(X[:, :, :], a["xT"]).then_inc(s["in"], 16)
                    with sp.Fori(0, NC // 2) as i:
                        for b in range(2):
                            sp.wait_ge(s[f"rows{b}"], i)
                            sp.dma_start(W[b], a["mod_w"][ds(2 * i + b, 1)].rearrange("o p k n -> (o p) k n"))\
                                .then_inc(s[f"w{b}"], 16)

                @block.scalar
                def _(act):
                    act.wait_ge(s["in"], 64)
                    act.activation(sil, cT, ACT.Silu).then_inc(s["sil"], 1)
                    with act.Fori(0, NC // 2) as i:
                        for b in range(2):
                            act.wait_ge(s[f"rows{b}"], i + 1)
                            act.wait_ge(s[f"cols{b}"], i)
                            act.activation(row[0:2, b, :], ps(b, BANK, slice(0, 2)), ACT.Copy)\
                                .then_inc(s[f"rowc{b}"], 1)

                @block.tensor
                def _(pe):
                    pe.wait_ge(s["sil"], 1)
                    with pe.Fori(0, NC // 2) as i:
                        for b in range(2):
                            pe.wait_ge(s[f"w{b}"], 16 * i + 16)
                            pe.wait_ge(s[f"rowc{b}"], i)
                            for k in range(KT):
                                mm = pe.matmul(ps(b, BANK, slice(0, 2)), sil[:, k, :], W[b][:, k, :],
                                               start=(k == 0), stop=(k == KT - 1))
                            mm.then_inc(s[f"rows{b}"], 1)
                            pe.wait_ge(s[f"rowc{b}"], i + 1)
                            pe.wait_ge(s[f"out{b}"], i)
                            for j in range(4):
                                mm = pe.matmul(ps(2 + b, 8)[:, 2 * j:2 * j + 2], row[0:2, b, j * P:(j + 1) * P],
                                               cst[0:2, C_IDENT:C_IDENT + 2], start=True, stop=True)
                            mm.then_inc(s[f"cols{b}"], 1)

                @block.vector
                def _(dve):
                    dve.memset(eps[:, :], EPS).then_inc(s["dve"], 1)
                    dve.wait_ge(s["in"], 64)
                    dve.tensor_copy(identb[:, :], ident).then_inc(s["dve"], 1)
                    for n, col in enumerate((C_GE, C_LE)):
                        dve.tensor_copy(maskb[:, n, :], cst[:, col:col + P]).then_inc(s["dve"], 1)
                    for n in range(2):
                        dve.tensor_scalar(rot0[:, n, :], cst[0:A_QK, C_R0:C_R0 + A_QK],
                                          sml[0:A_QK, W_G0 + n:W_G0 + n + 1], None, ALU.mult).then_inc(s["dve"], 1)
                        dve.tensor_scalar(rot1[:, n, :], cst[:, C_R1:C_R1 + P],
                                          sml[:, W_G1 + n:W_G1 + n + 1], None, ALU.mult).then_inc(s["dve"], 1)
                    modb = sml[:, W_MODB:W_MODB + 192].rearrange("p (x y) -> p x y", y=2)
                    with dve.Fori(0, NC // 2) as i:
                        for b in range(2):
                            dve.wait_ge(s[f"cols{b}"], i + 1)
                            dve.tensor_tensor(mod[:, ds(8 * i + 4 * b, 4), :],
                                              ps(2 + b, 8).rearrange("p (x y) -> p x y", y=2),
                                              modb[:, ds(8 * i + 4 * b, 4), :], ALU.add).then_inc(s[f"out{b}"], 1)
                    for b in range(2):
                        dve.wait_ge(s[f"out{b}"], NC // 2)
                    for n in range(2 * DEPTH):
                        layer, which = n // 2, 1 + 3 * (n % 2)
                        o = (layer * N_MOD + which) * KT
                        g = sml[:, W_NG + n * 2 * KT:W_NG + (n + 1) * 2 * KT].rearrange("p (x y) -> p x y", y=2)
                        dve.scalar_tensor_tensor(out=gsc[:, n * KT:(n + 1) * KT, :], in0=mod[:, o:o + KT, :],
                                                 scalar=1.0, in1=g, op0=ALU.add, op1=ALU.mult).then_inc(s["dve"], 1)

        def norm(layer, which, tokens):
            tag = f"n{layer}{which}_"
            chunks = [c for c in CH if c[0] < tokens]
            streams = [x for x in STREAMS if x[0] < tokens]
            sq = big(0, 2, T)
            lnb = big(2 * T, T)
            with ExitStack() as c2:
                s = {n: sem(tag + n) for n in
                     ("sq", "acc", "ln", "rinv", "u", "sh")}
                block = c2.enter_context(nc.Block())

                @block.scalar
                def _(act):
                    act.preload_act_table_set("natural_log_exp_and_others")
                    for k in range(KT):
                        if k >= 2:
                            act.wait_ge(s["acc"], k - 1)
                        act.activation(sq[:, k % 2, :tokens], X[:, k, :tokens], ACT.Square).then_inc(s["sq"], 1)
                    act.wait_ge(s["acc"], KT)
                    act.activation(lnb[:, :tokens], PS[:, 0:tokens], ACT.Ln, bias=eps[:, 0:1], scale=1.0 / D)\
                        .then_inc(s["ln"], 1)
                    act.wait_ge(s["ln"], 1)
                    act.activation(PS[:, 0:tokens], lnb[:, :tokens], ACT.Exp, scale=-0.5).then_inc(s["rinv"], 1)
                    for k in range(KT):
                        act.wait_ge(s["u"], k + 1)
                        for lo, hi, v in streams:
                            act.activation(U[:, k, lo:hi], U[:, k, lo:hi], ACT.Identity,
                                           bias=moda(layer, 3 * which, k, v)).then_inc(s["sh"], 1)

                @block.tensor
                def _(pe):
                    for k in range(KT):
                        pe.wait_ge(s["sq"], k + 1)
                        for n, (lo, hi) in enumerate(chunks):
                            mm = pe.matmul(ps(n, hi - lo), ones, sq[:, k % 2, lo:hi],
                                           start=(k == 0), stop=(k == KT - 1))
                        mm.then_inc(s["acc"], 1)

                @block.vector
                def _(dve):
                    dve.wait_ge(s["rinv"], 1)
                    for k in range(KT):
                        for lo, hi, v in streams:
                            g = gsc[:, (2 * layer + which) * KT + k, v:v + 1]
                            op = dve.scalar_tensor_tensor(out=U[:, k, lo:hi], in0=X[:, k, lo:hi], scalar=g,
                                                          in1=PS[:, lo:hi], op0=ALU.mult, op1=ALU.mult)
                        op.then_inc(s["u"], 1)

        def linear(tag, w, rhs, K, tiles, tokens, woff, take, prefetch=None):
            chunks = [c for c in CH if c[0] < tokens]
            W = [big(woff + b * K * P, K, P) for b in range(2)]
            with ExitStack() as c2:
                s = {n: sem(tag + n) for n in ("w0", "w1", "mm0", "mm1", "taken0", "taken1")}
                block = c2.enter_context(nc.Block())

                @block.sync
                def _(sp):
                    with sp.Fori(0, tiles // 2) as i:
                        for b in range(2):
                            sp.wait_ge(s[f"mm{b}"], i)
                            sp.dma_start(W[b], w[ds(2 * i + b, 1)].rearrange("o p (k n) -> (o p) k n", k=K))\
                                .then_inc(s[f"w{b}"], 16)

                @block.tensor
                def _(pe):
                    with pe.Fori(0, tiles // 2) as i:
                        for b in range(2):
                            pe.wait_ge(s[f"w{b}"], 16 * i + 16)
                            pe.wait_ge(s[f"taken{b}"], i)
                            for k in range(K):
                                for n, (lo, hi) in enumerate(chunks):
                                    mm = pe.matmul(ps(3 * b + n, hi - lo), W[b][:, k, :], rhs[:, k, lo:hi],
                                                   start=(k == 0), stop=(k == K - 1))
                            mm.then_inc(s[f"mm{b}"], 1)

                @block.vector
                def _(dve):
                    with dve.Fori(0, tiles // 2) as i:
                        for b in range(2):
                            dve.wait_ge(s[f"mm{b}"], i + 1)
                            take(dve, 2 * i + b, PS[:, 3 * b * BANK:3 * b * BANK + tokens])\
                                .then_inc(s[f"taken{b}"], 1)

        def residual(layer, which, tokens):
            def take(dve, m, y):
                for lo, hi, v in [x for x in STREAMS if x[0] < tokens]:
                    xs = X[:, ds(m, 1), lo:hi].rearrange("p o n -> p (o n)")
                    op = dve.scalar_tensor_tensor(out=xs, in0=y[:, lo:hi], scalar=moda(layer, which, m, v), in1=xs,
                                                  op0=ALU.mult, op1=ALU.add)
                return op
            return take

        def ffn(layer, tokens):
            tag = f"f{layer}_"
            chunks = [c for c in CH if c[0] < tokens]
            streams = [x for x in STREAMS if x[0] < tokens]
            G = big(0, FG, T)
            o = FG * T
            W = [big(o + b * KT * P, KT, P) for b in range(2)]
            WD = [big(o + 2 * KT * P + b * FG * P, FG, P) for b in range(2)]
            o += 2 * KT * P + 2 * FG * P
            tc_ = [big(o + b * T, T) for b in range(2)]
            sg = big(o + 2 * T, T)
            cw = big(o + 3 * T, 2 * FT, 4)
            assert o + 3 * T + 8 * FT <= BIGN
            with ExitStack() as c2:
                s = {n: sem(tag + n) for n in
                     ("cw", "wg", "wv", "wd0", "wd1", "hg", "hv", "tg", "tv", "fg", "fv", "lg", "sg", "g",
                      "y0", "y1", "taken0", "taken1")}
                block = c2.enter_context(nc.Block())
                S = [("hg", "wg", "tg", "fg", "lg"), ("hv", "wv", "tv", "fv", None)]

                @block.sync
                def _(sp):
                    sp.dma_start(cw, a["conv"][layer].rearrange("p (k n) -> p k n", n=4)).then_inc(s["cw"], 16)
                    for half in range(2):
                        with sp.Fori(0, FG) as j:
                            for b in range(2):
                                sp.wait_ge(s[S[b][0]], half * FG + j)
                                sp.dma_start(W[b], a["w_up"][layer][ds(b * FT + half * FG + j, 1)]
                                             .rearrange("o p (k n) -> (o p) k n", k=KT)).then_inc(s[S[b][1]], 16)
                        with sp.Fori(0, KT // 2) as i:
                            for b in range(2):
                                sp.wait_ge(s[f"y{b}"], half * KT // 2 + i)
                                sp.dma_start(WD[b], a["w_down"][layer][half][ds(2 * i + b, 1)]
                                             .rearrange("o p (k n) -> (o p) k n", k=FG)).then_inc(s[f"wd{b}"], 16)

                @block.tensor
                def _(pe):
                    for half in range(2):
                        with pe.Fori(0, FG) as j:
                            for b in range(2):
                                h, wt, _, f, _ = S[b]
                                pe.wait_ge(s[wt], 16 * (half * FG) + 16 * j + 16)
                                pe.wait_ge(s[f], half * FG + j)
                                if b == 0:
                                    for r in range(2):
                                        pe.wait_ge(s[f"taken{r}"], half * KT // 2)
                                for k in range(KT):
                                    for n, (lo, hi) in enumerate(chunks):
                                        mm = pe.matmul(ps(3 * b + n, hi - lo), W[b][:, k, :], U[:, k, lo:hi],
                                                       start=(k == 0), stop=(k == KT - 1))
                                mm.then_inc(s[h], 1)
                        pe.wait_ge(s["g"], (half + 1) * FG)
                        with pe.Fori(0, KT // 2) as i:
                            for b in range(2):
                                pe.wait_ge(s[f"wd{b}"], 16 * (half * KT // 2) + 16 * i + 16)
                                pe.wait_ge(s[f"taken{b}"], half * KT // 2 + i)
                                for k in range(FG):
                                    for n, (lo, hi) in enumerate(chunks):
                                        mm = pe.matmul(ps(3 * b + n, hi - lo), WD[b][:, k, :], G[:, k, lo:hi],
                                                       start=(k == 0), stop=(k == FG - 1))
                                mm.then_inc(s[f"y{b}"], 1)

                @block.scalar
                def _(act):
                    act.preload_act_table_set("silu_and_others")
                    act.wait_ge(s["cw"], 16)
                    for half in range(2):
                        with act.Fori(0, FG) as j:
                            for b in range(2):
                                h, _, t_, _, _ = S[b]
                                act.wait_ge(s[h], half * FG + j + 1)
                                act.wait_ge(s["sg" if b == 0 else "g"], half * FG + j)
                                act.activation(tc_[b][:, :tokens], PS[:, 3 * b * BANK:3 * b * BANK + tokens],
                                               ACT.Identity,
                                               scale=cw[:, ds(b * FT + half * FG + j, 1), 1],
                                               bias=cw[:, ds(b * FT + half * FG + j, 1), 3]).then_inc(s[t_], 1)
                                if b == 0:
                                    act.wait_ge(s["fg"], half * FG + j + 1)
                                    act.wait_ge(s["g"], half * FG + j)
                                    act.activation(sg[:, :tokens], tc_[0][:, :tokens], ACT.Silu).then_inc(s["sg"], 1)

                @block.vector
                def _(dve):
                    dve.wait_ge(s["cw"], 16)
                    for half in range(2):
                        with dve.Fori(0, FG) as j:
                            for b in range(2):
                                _, _, t_, f, _ = S[b]
                                q = b * FT + half * FG + j
                                dve.wait_ge(s[t_], half * FG + j + 1)
                                h = PS[:, 3 * b * BANK:3 * b * BANK + tokens]
                                for lo, hi, v in streams:
                                    op = dve.scalar_tensor_tensor(
                                        out=tc_[b][:, lo + 1:hi], in0=h[:, lo:hi - 1], scalar=cw[:, ds(q, 1), 0],
                                        in1=tc_[b][:, lo + 1:hi], op0=ALU.mult, op1=ALU.add)
                                op.then_inc(s["lg"], 1)
                                dve.wait_ge(s["lg"], 2 * (half * FG) + 2 * j + b + 1)
                                for lo, hi, v in streams:
                                    op = dve.scalar_tensor_tensor(
                                        out=tc_[b][:, lo:hi - 1], in0=h[:, lo + 1:hi], scalar=cw[:, ds(q, 1), 2],
                                        in1=tc_[b][:, lo:hi - 1], op0=ALU.mult, op1=ALU.add)
                                op.then_inc(s[f], 1)
                            dve.wait_ge(s["fv"], half * FG + j + 1)
                            dve.wait_ge(s["sg"], half * FG + j + 1)
                            if half:
                                for r in range(2):
                                    dve.wait_ge(s[f"y{r}"], KT // 2)
                            dve.tensor_tensor(G[:, ds(j, 1), :tokens].rearrange("p o n -> p (o n)"),
                                              sg[:, :tokens], tc_[1][:, :tokens], ALU.mult).then_inc(s["g"], 1)
                        take = residual(layer, 5, tokens)
                        with dve.Fori(0, KT // 2) as i:
                            for b in range(2):
                                dve.wait_ge(s[f"y{b}"], half * KT // 2 + i + 1)
                                dve.wait_ge(s[f"taken{b}"], half * KT // 2 + i)
                                take(dve, 2 * i + b, PS[:, 3 * b * BANK:3 * b * BANK + tokens])\
                                    .then_inc(s[f"taken{b}"], 1)

        O_MIX = 0
        O_H = KT * T
        O_A = O_H + 6 * T
        MIX = big(O_MIX, KT, T)
        H = big(O_H, 6, T)

        def copy_take(dst, tokens):
            def take(dve, m, y):
                return dve.tensor_copy(dst[:, ds(m, 1), :tokens].rearrange("p o n -> p (o n)"), y)
            return take

        V0 = U[:, :, :].rearrange("p k n -> p (k n)")[:, 0:10 * A_HEADS * 65]\
            .rearrange("p (t h d) -> p t h d", t=10, h=A_HEADS)

        def latent_norms():
            sq = big(O_A, 2, T)
            lnb = big(O_A + 2 * T, T)
            wv = big(O_A + 3 * T, A_HEADS * 64)
            parts = [((0, 1), 256, W_CQG), ((2,), 128, W_CKVG)]
            with ExitStack() as c2:
                s = {n: sem("ln_" + n) for n in
                     ("w", "sq", "acc", "ln", "rinv", "u", "v", "vc", "one")}
                block = c2.enter_context(nc.Block())

                @block.sync
                def _(sp):
                    sp.dma_start(wv, a["w_v0"]).then_inc(s["w"], 16)

                @block.gpsimd
                def _(pool):
                    pool.memset(V0[:, :, :, 64], 1.0).then_inc(s["one"], 1)

                @block.scalar
                def _(act):
                    act.preload_act_table_set("natural_log_exp_and_others")
                    n = 0
                    for i, (tiles, width, _) in enumerate(parts):
                        for t_ in tiles:
                            if n >= 2:
                                act.wait_ge(s["acc"], n - 1)
                            act.activation(sq[:, n % 2, :], H[:, t_, :], ACT.Square).then_inc(s["sq"], 1)
                            n += 1
                        act.wait_ge(s["acc"], n)
                        if i:
                            act.wait_ge(s["rinv"], 1)
                        act.activation(lnb, PS[:, 3 * i * BANK:3 * i * BANK + T], ACT.Ln, bias=eps[:, 0:1],
                                       scale=1.0 / width).then_inc(s["ln"], 1)
                        act.wait_ge(s["ln"], i + 1)
                        act.activation(PS[:, 3 * i * BANK:3 * i * BANK + T], lnb, ACT.Exp, scale=-0.5)\
                            .then_inc(s["rinv"], 1)
                    for t_ in range(10):
                        act.wait_ge(s["v"], t_ + 1)
                        for h in range(2):
                            op = act.activation(
                                V0[:, t_, 6 * h:6 * h + 6, 0:64],
                                ps(2 * (t_ % 2) + h, 384).rearrange("p (h d) -> p h d", h=6), ACT.Copy)
                        op.then_inc(s["vc"], 1)

                @block.tensor
                def _(pe):
                    n = 0
                    for i, (tiles, _, _) in enumerate(parts):
                        for t_ in tiles:
                            pe.wait_ge(s["sq"], n + 1)
                            for c, (lo, hi) in enumerate(CH):
                                mm = pe.matmul(ps(3 * i + c, hi - lo), ones, sq[:, n % 2, lo:hi],
                                               start=(t_ == tiles[0]), stop=(t_ == tiles[-1]))
                            mm.then_inc(s["acc"], 1)
                            n += 1
                    pe.wait_ge(s["w"], 16)
                    pe.wait_ge(s["u"], 3)
                    for t_ in range(10):
                        if t_ >= 2:
                            pe.wait_ge(s["vc"], t_ - 1)
                        for h in range(2):
                            mm = pe.matmul(ps(2 * (t_ % 2) + h, 384), H[:, 2, t_ * P:(t_ + 1) * P],
                                           wv[:, 384 * h:384 * h + 384], start=True, stop=True)
                        mm.then_inc(s["v"], 1)

                @block.vector
                def _(dve):
                    for i, (tiles, _, g) in enumerate(parts):
                        dve.wait_ge(s["rinv"], i + 1)
                        for t_ in tiles:
                            dve.scalar_tensor_tensor(out=H[:, t_, :], in0=H[:, t_, :],
                                                     scalar=sml[:, g + t_ % 2:g + t_ % 2 + 1],
                                                     in1=PS[:, 3 * i * BANK:3 * i * BANK + T],
                                                     op0=ALU.mult, op1=ALU.mult).then_inc(s["u"], 1)

        def fourier():
            FW = big(O_A, 2, 2 * P)
            AB = big(O_A + 512, 10, 4 * P)
            DF = [big(O_A + 512 + 5120 + b * 2048, 2, SEQ) for b in range(2)]
            DC = big(O_A + 512 + 5120 + 4096, 2, 2, CTX)
            with ExitStack() as c2:
                s = {n: sem("ff_" + n) for n in
                     ("d0", "d1", "dc", "fw", "fwc", "ab", "abc", "l", "y", "yc")}
                block = c2.enter_context(nc.Block())

                @block.sync
                def _(sp):
                    sp.dma_start(DC, a["dftc"].rearrange("t p s n -> p t s n")).then_inc(s["dc"], 16)
                    for t_ in range(8):
                        if t_ >= 2:
                            sp.wait_ge(s["l"], t_ - 1)
                        sp.dma_start(DF[t_ % 2], a["dft"][t_]).then_inc(s[f"d{t_ % 2}"], 16)

                @block.tensor
                def _(pe):
                    for p in range(2):
                        for n, col in enumerate((C_COSC, C_SINC)):
                            mm = pe.matmul(ps(p, 2 * P)[:, n * P:(n + 1) * P], cst[:, col:col + P],
                                           sml[:, W_FN + p * P:W_FN + (p + 1) * P], start=True, stop=True)
                    mm.then_inc(s["fw"], 1)
                    pe.wait_ge(s["fwc"], 1)
                    for t_ in range(10):
                        if t_ >= 2:
                            pe.wait_ge(s["abc"], t_ - 1)
                        for p in range(2):
                            mm = pe.matmul(ps(2 + t_ % 2, 4 * P)[:, 2 * P * p:2 * P * (p + 1)],
                                           H[:, 4 + p, t_ * P:(t_ + 1) * P], FW[:, p, :], start=True, stop=True)
                        mm.then_inc(s["ab"], 1)
                    pe.wait_ge(s["abc"], 10)
                    for t_ in range(8):
                        pe.wait_ge(s[f"d{t_ % 2}"], 16 * (t_ // 2 + 1))
                        for p in range(2):
                            for n in range(2):
                                for c in range(2):
                                    mm = pe.matmul(ps(4 + 2 * p + c, BANK),
                                                   AB[:, t_, (2 * p + n) * P:(2 * p + n + 1) * P],
                                                   DF[t_ % 2][:, n, c * BANK:(c + 1) * BANK],
                                                   start=(t_ == 0 and n == 0), stop=(t_ == 7 and n == 1))
                        mm.then_inc(s["l"], 1)
                    pe.wait_ge(s["dc"], 16)
                    for p in range(2):
                        for t_ in range(2):
                            for n in range(2):
                                mm = pe.matmul(ps(p, CTX), AB[:, 8 + t_, (2 * p + n) * P:(2 * p + n + 1) * P],
                                               DC[:, t_, n, :], start=(t_ == 0 and n == 0),
                                               stop=(t_ == 1 and n == 1))
                    mm.then_inc(s["y"], 1)

                @block.vector
                def _(dve):
                    dve.wait_ge(s["fw"], 1)
                    dve.tensor_copy(FW, PS[:, 0:2 * BANK].rearrange("p (x y) -> p x y", x=2)[:, :, 0:2 * P])\
                        .then_inc(s["fwc"], 1)
                    for t_ in range(10):
                        dve.wait_ge(s["ab"], t_ + 1)
                        dve.tensor_copy(AB[:, t_, :], ps(2 + t_ % 2, BANK)).then_inc(s["abc"], 1)
                    dve.wait_ge(s["l"], 8)
                    for p in range(2):
                        dve.tensor_copy(MIX[:, 6 + p, 0:SEQ], PS[:, (4 + 2 * p) * BANK:(6 + 2 * p) * BANK])\
                            .then_inc(s["yc"], 1)
                    dve.wait_ge(s["y"], 1)
                    for p in range(2):
                        dve.tensor_copy(MIX[:, 6 + p, SEQ:T], ps(p, CTX)).then_inc(s["yc"], 1)

        def heads0():
            o = O_A

            def take(*shape):
                nonlocal o
                v = big(o, *shape)
                o += int(np.prod(shape))
                return v
            qa = [take(T) for _ in range(2)]
            ka = [take(T) for _ in range(2)]
            vs = [take(10, 65) for _ in range(2)]
            wq = [take(256) for _ in range(2)]
            pr = [take(BANK) for _ in range(2)]
            raw = [take(BANK) for _ in range(2)]
            sq = [take(BANK) for _ in range(2)]
            t1 = take(BANK)
            lnb = take(BANK)
            mc = take(10)
            mcb = take(6).bitcast(BF16)
            rope = H[:, 4:6, :]
            Uf = U[:, :, :].rearrange("p k n -> p (k n)")
            qb = Uf[:, 7800:7800 + T // 2].bitcast(BF16)
            kb = Uf[:, 7800 + T // 2:7800 + T].bitcast(BF16)
            o65 = big(o, T) if o + T <= BIGN else None
            NU = 22
            units = [(kt, c) for kt in range(10) for c in (0, 1)] + [(8, 2), (9, 2)]
            assert o65 is not None
            RB, NB, TB = 5, 6, 7
            with ExitStack() as c2:
                s = {n: sem("h0_" + n) for n in
                     ("tab", "w0", "w1", "one", "S", "P", "PV", "raw", "rawc", "sq", "nt", "ln", "kr", "rinv",
                      "t1", "ts", "ta", "out", "cast", "vs", "mx", "mc", "mn", "mrow", "mr", "o", "bc",
                      "rs", "fin")}
                block = c2.enter_context(nc.Block())

                def at_least(eng, name, value):
                    if not (isinstance(value, int) and value <= 0):
                        eng.wait_ge(s[name], value)

                def step_of(u):
                    if 3 <= u <= 9:
                        return "prep", u - 3
                    if 10 <= u <= 18:
                        return "max", u - 10
                    if u == 19:
                        return "row", 0
                    return None, 0

                @block.sync
                def _(sp):
                    sp.dma_start(rope[0:A_QK], a["rope0"]).then_inc(s["tab"], 16)

                    def load(p, b):
                        sp.dma_start(wq[b], a["wqk0"][ds(p, 1)].rearrange("o p n -> (o p) n")).then_inc(s[f"w{b}"], 16)
                    load(0, 0)
                    load(1, 1)
                    with sp.Fori(0, 5) as i:
                        sp.wait_ge(s["raw"], 12 * i + 6)
                        load(2 * i + 2, 0)
                        sp.wait_ge(s["raw"], 12 * i + 12)
                        load(2 * i + 3, 1)

                @block.gpsimd
                def _(pool):
                    for b in range(2):
                        pool.memset(ka[b][96:97, :], 1.0).then_inc(s["one"], 1)

                    pool.wait_ge(s["one"], 2)

                    def prep(p, b):
                        at_least(pool, "cast", 6 * p)
                        at_least(pool, "PV", NU * (p - 1))
                        pool.tensor_copy(vs[b], V0[:, :, ds(p, 1), :].rearrange("p t o d -> p t (o d)"))\
                            .then_inc(s["vs"], 1)
                        at_least(pool, "mx", 9 * p)
                        for w in range(6):
                            lo, hi = CH[w % 3]
                            src, dst = (ka[b], kb) if w < 3 else (qa[b], qb)
                            pool.wait_ge(s["out"], 6 * p + w + 1)
                            if w == 0:
                                pool.wait_ge(s["vs"], p + 1)
                            pool.tensor_copy(dst[0:A_QK, lo:hi], src[0:A_QK, lo:hi]).then_inc(s["cast"], 1)
                    for p in range(A_HEADS):
                        prep(p, p % 2)

                @block.tensor
                def _(pe):
                    def qk(h, b, u):
                        kt, c = units[u]
                        lo, hi = CH[c]
                        at_least(pe, "P", NU * h + u - 1)
                        if u == 0:
                            pe.wait_ge(s["mr"], h + 1)
                        pe.matmul(ps(u % 2, hi - lo), ka[b][0:97, kt * P:(kt + 1) * P], qa[b][0:97, lo:hi],
                                  start=True, stop=True).then_inc(s["S"], 1)

                    def pv(h, b, u):
                        kt, c = units[u]
                        lo, hi = CH[c]
                        pe.wait_ge(s["P"], NU * h + u + 1)
                        if u == 0:
                            pe.wait_ge(s["vs"], h + 1)
                            at_least(pe, "o", h)
                        pe.matmul(ps(2 + c, hi - lo, slice(0, 65)), vs[b][:, kt, :], pr[u % 2][:, :hi - lo],
                                  start=(kt == (8 if c == 2 else 0)), stop=(kt == 9)).then_inc(s["PV"], 1)

                    def spread(h):
                        pe.wait_ge(s["o"], h + 1)
                        for n, (lo, hi) in enumerate(CH):
                            mm = pe.matmul(ps(RB + n, hi - lo, slice(0, 64)), cst[0:65, C_SEL:C_SEL + 64],
                                           o65[0:65, lo:hi], start=True, stop=True)
                        mm.then_inc(s["bc"], 1)

                    def project(p, b, use, w):
                        lo, hi = CH[w % 3]
                        if w == 0:
                            pe.wait_ge(s[f"w{b}"], 16 * use + 16)
                            at_least(pe, "fin", p - 1)
                        at_least(pe, "rawc", 6 * p + w)
                        if w < 3:
                            mm = pe.matmul(ps(RB, hi - lo, slice(0, 64)), wq[b][:, 192:256], H[:, 2, lo:hi],
                                           start=True, stop=True)
                        else:
                            for k in range(2):
                                mm = pe.matmul(ps(RB, hi - lo, slice(0, A_QK)), wq[b][:, 96 * k:96 * k + 96],
                                               H[:, k, lo:hi], start=(k == 0), stop=(k == 1))
                        mm.then_inc(s["raw"], 1)

                    def squares(p, w):
                        lo, hi = CH[w % 3]
                        pe.wait_ge(s["sq"], 6 * p + w + 1)
                        at_least(pe, "out", 6 * p + w)
                        pe.matmul(ps(NB, hi - lo, slice(0, A_QK)), ones[0:A_QK, 0:A_QK], sq[w % 2][0:A_QK, :hi - lo],
                                  start=True, stop=True)
                        pe.matmul(ps(TB, hi - lo, slice(0, A_QK)), rot0[:, 0 if w >= 3 else 1, :],
                                  raw[w % 2][0:A_QK, :hi - lo], start=True, stop=True).then_inc(s["nt"], 1)

                    def step(kind, n, p, b, use):
                        if kind == "prep":
                            if n < 6:
                                project(p, b, use, n)
                            if n:
                                squares(p, n - 1)
                        if kind == "max" and n < 8:
                            if n == 0:
                                pe.wait_ge(s["cast"], 6 * p + 6)
                            at_least(pe, "mc", 9 * p + n)
                            for c, (lo, hi) in enumerate(CH):
                                mm = pe.matmul(ps(RB + c, hi - lo), qb[0:A_QK, n * P:(n + 1) * P],
                                               kb[0:A_QK, lo:hi], start=True, stop=True)
                            mm.then_inc(s["mx"], 1)
                        if kind == "max" and n == 8:
                            pe.wait_ge(s["mc"], 9 * p + n)
                            for c in range(2):
                                mm = pe.matmul(ps(RB + c, CTX), qb[0:A_QK, SEQ + c * P:SEQ + (c + 1) * P],
                                               kb[0:A_QK, SEQ:T], start=True, stop=True)
                            mm.then_inc(s["mx"], 1)
                        if kind == "row":
                            pe.wait_ge(s["mn"], p + 1)
                            for n in range(10):
                                mm = pe.matmul(ps(RB + n // 4, BANK, slice(96, 97))[:, (n % 4) * P:(n % 4 + 1) * P],
                                               mcb[:, n:n + 1], identb[:, :], start=True, stop=True)
                            mm.then_inc(s["mrow"], 1)

                    def head(h, b, use, prep, before):
                        qk(h, b, 0)
                        for u in range(NU):
                            if u + 1 < NU:
                                qk(h, b, u + 1)
                            if u == 1 and before:
                                spread(h - 1)
                            if prep:
                                step(*step_of(u), h + 1, 1 - b, use)
                            pv(h, b, u)

                    pe.wait_ge(s["tab"], 16)
                    pe.wait_ge(s["one"], 2)
                    for u in range(NU):
                        step(*step_of(u), 0, 0, 0)
                    head(0, 0, 0, True, False)
                    with pe.Fori(0, 5) as i:
                        head(2 * i + 1, 1, i + 1, True, True)
                        head(2 * i + 2, 0, i + 1, True, True)
                    head(11, 1, 0, False, True)
                    spread(11)

                @block.scalar
                def _(act):
                    def project(p, w):
                        lo, hi = CH[w % 3]
                        n = hi - lo
                        act.wait_ge(s["raw"], 6 * p + w + 1)
                        at_least(act, "nt", 6 * p + w - 1)
                        at_least(act, "t1", 6 * p + w - 1)
                        if w < 3:
                            act.activation(raw[w % 2][0:64, :n], ps(RB, n, slice(0, 64)), ACT.Copy).then_inc(s["rawc"], 1)
                            act.activation(raw[w % 2][64:96, :n], H[0:32, 3, lo:hi], ACT.Copy).then_inc(s["kr"], 1)
                        else:
                            act.activation(raw[w % 2][0:96, :n], ps(RB, n, slice(0, 96)), ACT.Copy).then_inc(s["rawc"], 1)
                        act.wait_ge(s["rawc"], 6 * p + w + 1)
                        if w < 3:
                            act.wait_ge(s["kr"], 3 * p + w + 1)
                        act.activation(sq[w % 2][0:96, :n], raw[w % 2][0:96, :n], ACT.Square).then_inc(s["sq"], 1)

                    def inverse(p, w):
                        lo, hi = CH[w % 3]
                        n = hi - lo
                        act.wait_ge(s["nt"], 6 * p + w + 1)
                        at_least(act, "rinv", 6 * p + w)
                        act.activation(lnb[0:96, :n], ps(NB, n, slice(0, 96)), ACT.Ln, bias=eps[0:96, 0:1],
                                       scale=1.0 / A_QK).then_inc(s["ln"], 1)
                        act.wait_ge(s["ln"], 6 * p + w + 1)
                        act.activation(ps(NB, n, slice(0, 96)), lnb[0:96, :n], ACT.Exp, scale=-0.5)\
                            .then_inc(s["rinv"], 1)

                    def step(kind, n, p, b):
                        if kind == "prep":
                            if n < 6:
                                project(p, n)
                            if n:
                                inverse(p, n - 1)
                        if kind == "row":
                            act.wait_ge(s["mrow"], p + 1)
                            act.activation(qa[b][96:97, :], PS[96:97, RB * BANK:RB * BANK + T], ACT.Copy)\
                                .then_inc(s["mr"], 1)

                    def head(h, b, prep):
                        for u in range(NU):
                            lo, hi = CH[units[u][1]]
                            act.wait_ge(s["S"], NU * h + u + 1)
                            at_least(act, "PV", NU * h + u - 1)
                            act.activation(pr[u % 2][:, :hi - lo], ps(u % 2, hi - lo), ACT.Exp, scale=A_SCALE)\
                                .then_inc(s["P"], 1)
                            if prep:
                                step(*step_of(u), h + 1, 1 - b)
                        act.wait_ge(s["PV"], NU * h + NU)
                        at_least(act, "fin", h)
                        act.activation(o65[0:65, :], PS[0:65, 2 * BANK:2 * BANK + T], ACT.Copy).then_inc(s["o"], 1)

                    for u in range(NU):
                        step(*step_of(u), 0, 0)
                    head(0, 0, True)
                    with act.Fori(0, 5) as i:
                        head(2 * i + 1, 1, True)
                        head(2 * i + 2, 0, True)
                    head(11, 1, False)

                @block.vector
                def _(dve):
                    def finish(h, tile, half):
                        dve.wait_ge(s["bc"], h + 1)
                        r = PS[0:64, RB * BANK:RB * BANK + T]
                        dve.reciprocal(r, r).then_inc(s["rs"], 1)
                        dve.wait_ge(s["rs"], h + 1)
                        dve.tensor_tensor(MIX[64 * half:64 * half + 64, ds(tile, 1), :].rearrange("p o n -> p (o n)"),
                                          o65[0:64, :], r, ALU.mult).then_inc(s["fin"], 1)

                    def unit(p, b, w):
                        lo, hi = CH[w % 3]
                        n = hi - lo
                        g = sml[0:96, W_G0 + (0 if w >= 3 else 1):W_G0 + (1 if w >= 3 else 2)]
                        dst = qa[b] if w >= 3 else ka[b]
                        dve.wait_ge(s["sq"], 6 * p + w + 1)
                        at_least(dve, "out", 6 * p + w)
                        dve.scalar_tensor_tensor(out=t1[0:96, :n], in0=raw[w % 2][0:96, :n], scalar=g,
                                                 in1=rope[0:96, 0, lo:hi], op0=ALU.mult, op1=ALU.mult)\
                            .then_inc(s["t1"], 1)
                        dve.wait_ge(s["nt"], 6 * p + w + 1)
                        T_ = ps(TB, n, slice(0, 96))
                        dve.tensor_tensor(T_, T_, rope[0:96, 1, lo:hi], ALU.mult).then_inc(s["ts"], 1)
                        dve.wait_ge(s["ts"], 6 * p + w + 1)
                        dve.tensor_tensor(t1[0:96, :n], t1[0:96, :n], T_, ALU.add).then_inc(s["ta"], 1)
                        dve.wait_ge(s["ta"], 6 * p + w + 1)
                        dve.wait_ge(s["rinv"], 6 * p + w + 1)
                        dve.tensor_tensor(dst[0:96, lo:hi], t1[0:96, :n], ps(NB, n, slice(0, 96)), ALU.mult)\
                            .then_inc(s["out"], 1)

                    def step(kind, n, p, b):
                        if kind == "prep" and n:
                            unit(p, b, n - 1)
                        if kind == "max":
                            dve.wait_ge(s["mx"], 9 * p + n + 1)
                            if n == 0:
                                at_least(dve, "mn", p)
                            if n < 8:
                                op = dve.reduce_max(mc[:, n:n + 1], PS[:, RB * BANK:RB * BANK + T], AX_X)
                            else:
                                op = dve.reduce_max(
                                    mc[:, 8:10], PS[:, RB * BANK:(RB + 2) * BANK].rearrange("p (x y) -> p x y", x=2)
                                    [:, :, 0:CTX], AX_X)
                            op.then_inc(s["mc"], 1)
                        if kind == "row":
                            dve.wait_ge(s["mc"], 9 * p + 9)
                            at_least(dve, "mrow", p)
                            dve.tensor_scalar(mcb[:, 0:10], mc, -1.0, None, ALU.mult).then_inc(s["mn"], 1)

                    dve.wait_ge(s["tab"], 16)
                    for u in range(NU):
                        step(*step_of(u), 0, 0)
                    for u in range(NU):
                        step(*step_of(u), 1, 1)
                    with dve.Fori(0, 5) as i:
                        finish(2 * i, i, 0)
                        for u in range(NU):
                            step(*step_of(u), 2 * i + 2, 0)
                        finish(2 * i + 1, i, 1)
                        for u in range(NU):
                            step(*step_of(u), 2 * i + 3, 1)
                    finish(10, 5, 0)
                    finish(11, 5, 1)

        MIX1 = big(0, KT, SEQ)
        O_V1 = KT * SEQ
        V1 = big(O_V1, 10, C_KV, 65)
        O_B = O_V1 + 10 * C_KV * 65

        def values1():
            wv = big(O_B, KT, 256)
            with ExitStack() as c2:
                s = {n: sem("v1_" + n) for n in ("w", "v", "vc", "one")}
                block = c2.enter_context(nc.Block())

                @block.sync
                def _(sp):
                    sp.dma_start(wv, a["w_v1"]).then_inc(s["w"], 16)

                @block.gpsimd
                def _(pool):
                    pool.memset(V1[:, :, :, 64], 1.0).then_inc(s["one"], 1)

                @block.tensor
                def _(pe):
                    pe.wait_ge(s["w"], 16)
                    for t_ in range(10):
                        if t_ >= 2:
                            pe.wait_ge(s["vc"], t_ - 1)
                        for k in range(KT):
                            mm = pe.matmul(ps(t_ % 2, 256), U[:, k, t_ * P:(t_ + 1) * P], wv[:, k, :],
                                           start=(k == 0), stop=(k == KT - 1))
                        mm.then_inc(s["v"], 1)

                @block.vector
                def _(dve):
                    for t_ in range(10):
                        dve.wait_ge(s["v"], t_ + 1)
                        dve.tensor_copy(V1[:, t_, :, 0:64], ps(t_ % 2, 256).rearrange("p (h d) -> p h d", h=C_KV))\
                            .then_inc(s["vc"], 1)

        PAD = 8
        ZW = SEQ + 2 * PAD
        Z = big(O_B + 2048, 2, ZW)

        def pool_take(dve, m, y):
            return dve.tensor_copy(Z[:, ds(m, 1), PAD:PAD + SEQ].rearrange("p o n -> p (o n)"), y)

        def pooling():
            o = O_B + 2048 + 2 * ZW
            Wd = [big(o + n * ZW, ZW) for n in range(3)]
            Pm = big(o + 3 * ZW, 2, SEQ)
            inv = big(o + 3 * ZW + 2 * SEQ, 2, SEQ)
            with ExitStack() as c2:
                s = {n: sem("po_" + n) for n in ("inv", "pad", "d", "mm", "out")}
                block = c2.enter_context(nc.Block())

                @block.sync
                def _(sp):
                    sp.dma_start(inv, a["pool_inv"]).then_inc(s["inv"], 16)

                @block.vector
                def _(dve):
                    n = 0

                    def chained(op):
                        nonlocal n
                        n += 1
                        op.then_inc(s["d"], 1)
                        dve.wait_ge(s["d"], n)

                    for t_ in range(2):
                        for e in (0, PAD + SEQ):
                            chained(dve.memset(Z[:, t_, e:e + PAD], 0.0))
                    dve.wait_ge(s["inv"], 16)
                    for t_ in range(2):
                        z = Z[:, t_, :]
                        chained(dve.tensor_tensor(Wd[0][:, 1:ZW], z[:, 0:ZW - 1], z[:, 1:ZW], ALU.add))
                        chained(dve.tensor_tensor(Wd[1][:, 2:ZW - 1], Wd[0][:, 1:ZW - 2], Wd[0][:, 3:ZW], ALU.add))
                        lo, hi = Wd[0], Wd[1]
                        if t_ == 1:
                            chained(dve.tensor_tensor(Wd[2][:, 4:ZW - 3], Wd[1][:, 2:ZW - 5], Wd[1][:, 6:ZW - 1],
                                                      ALU.add))
                            chained(dve.tensor_tensor(Wd[0][:, PAD:PAD + SEQ], Wd[2][:, PAD - 4:PAD + SEQ - 4],
                                                      Wd[2][:, PAD + 4:PAD + SEQ + 4], ALU.add))
                            lo, hi = Wd[2], Wd[0]
                        for r, src in ((0, lo), (64, hi)):
                            chained(dve.tensor_tensor(Pm[r:r + 64, t_, :], src[r:r + 64, PAD:PAD + SEQ],
                                                      inv[r:r + 64, t_, :], ALU.mult))
                        chained(dve.tensor_tensor(Pm[:, t_, :], Pm[:, t_, :], z[:, PAD:PAD + SEQ], ALU.subtract))
                    for t_ in range(2):
                        dve.wait_ge(s["mm"], t_ + 1)
                        dve.tensor_scalar(MIX1[:, 6 + t_, :], PS[:, 2 * t_ * BANK:(2 * t_ + 2) * BANK],
                                          sml[:, W_PS + t_:W_PS + t_ + 1], None, ALU.mult).then_inc(s["out"], 1)

                @block.tensor
                def _(pe):
                    pe.wait_ge(s["d"], 4 + 5 + 7)
                    for t_ in range(2):
                        for c in range(2):
                            mm = pe.matmul(ps(2 * t_ + c, BANK), sml[:, W_PW + t_ * P:W_PW + (t_ + 1) * P],
                                           Pm[:, t_, c * BANK:(c + 1) * BANK], start=True, stop=True)
                        mm.then_inc(s["mm"], 1)

        def heads1():
            o = O_B

            def take(*shape):
                nonlocal o
                v = big(o, *shape)
                o += int(np.prod(shape))
                return v
            qa = [[take(SEQ) for _ in range(C_GROUP)] for _ in range(2)]
            ka = [take(T) for _ in range(2)]
            wt = [take(KT, P) for _ in range(2)]
            pr = [take(BANK) for _ in range(2)]
            raw = [take(BANK) for _ in range(2)]
            sq = [take(BANK) for _ in range(2)]
            t1 = take(BANK)
            lnb = take(BANK)
            rope = take(2, T)
            qb = [take(SEQ // 2).bitcast(BF16) for _ in range(C_GROUP)]
            kb = take(T // 2).bitcast(BF16)
            mc = take(C_GROUP * 8)
            mcb = take(C_GROUP * 4).bitcast(BF16)
            s8 = take(C_HEADS)
            o65 = take(SEQ)
            es = X[64:65, 0:4, SEQ:T]
            RB, NB, TB = 5, 6, 7
            WIN = [(max(t - 1, 0), min(t + 2, 8)) for t in range(8)]
            units = [(8, 0, 4), (8, 4, 8), (9, 0, 4), (9, 4, 8)] + [(t, *WIN[t]) for t in range(8)]
            NU = len(units)
            NS = 6 + 8 * C_GROUP + C_GROUP
            places = [(j, u) for j in range(C_GROUP) for u in range(NU) if u != 2]
            assert len(places) == NS
            step_at = {pl: n for n, pl in enumerate(places)}
            prods = [(0, 0), (0, 1), (0, 2), (1, 0), (1, 1)]
            NW = len(prods)
            with ExitStack() as c2:
                s = {n: sem("h1_" + n) for n in
                     ("tab", "w0", "w1", "one", "s8", "S", "P", "PV", "raw", "rawc", "sq", "nt", "ln", "rinv",
                      "t1", "ts", "ta", "out", "cast", "mx", "mc", "mn", "mrow", "mr", "o", "es", "os", "bc",
                      "rs", "fin")}
                block = c2.enter_context(nc.Block())

                def at_least(eng, name, value):
                    if value > 0:
                        eng.wait_ge(s[name], value)

                def everywhere(stepper, attend, begin, end):
                    for n in range(NS):
                        stepper(n, 0)
                    for g in range(C_KV):
                        for j in range(C_GROUP):
                            for u in range(NU):
                                begin(g, j, u)
                                if g + 1 < C_KV and (j, u) in step_at:
                                    stepper(step_at[j, u], g + 1)
                                attend(g, j, u)
                            end(g, j)

                @block.sync
                def _(sp):
                    sp.dma_start(rope, a["rope1"]).then_inc(s["tab"], 16)
                    for g in range(C_KV):
                        for n in range(2):
                            at_least(sp, "raw", NW * (g - 1) + (3 if n == 0 else 5) if g else 0)
                            sp.dma_start(wt[n], a["wqk1"][2 * g + n].rearrange("p (k n) -> p k n", k=KT))\
                                .then_inc(s[f"w{n}"], 16)

                @block.gpsimd
                def _(pool):
                    for b in range(2):
                        pool.memset(ka[b][64:65, :], 1.0).then_inc(s["one"], 1)
                    pool.wait_ge(s["one"], 2)
                    for g in range(C_KV):
                        b = g % 2
                        at_least(pool, "mx", 8 * C_GROUP * g)
                        for w, (n, c) in enumerate(prods):
                            lo, hi = CH[c]
                            pool.wait_ge(s["out"], NW * g + w + 1)
                            if n == 0:
                                if c < 2:
                                    pool.tensor_copy(qb[2][0:64, lo:hi], qa[b][2][0:64, lo:hi])
                                op = pool.tensor_copy(kb[0:64, lo:hi], ka[b][0:64, lo:hi])
                            else:
                                pool.tensor_copy(qb[0][0:64, lo:hi], qa[b][0][0:64, lo:hi])
                                op = pool.tensor_copy(qb[1][0:64, lo:hi], qa[b][1][0:64, lo:hi])
                            op.then_inc(s["cast"], 1)

                @block.tensor
                def _(pe):
                    spreads = 0

                    def qk(g, j, u):
                        kt, q0, q1 = units[u]
                        n = (q1 - q0) * P
                        U_ = NU * (C_GROUP * g + j) + u
                        at_least(pe, "P", U_ - 1)
                        if u == 0:
                            pe.wait_ge(s["mr"], C_GROUP * g + j + 1)
                        ends = [(kt - 1 >= q0 and kt < 8, 0, 0), (kt + 1 < q1 and kt < 8, n - P, 1)]
                        last = [e for e in ends if e[0]]
                        mm = pe.matmul(ps(u % 2, n), ka[g % 2][0:65, kt * P:(kt + 1) * P],
                                       qa[g % 2][j][0:65, q0 * P:q1 * P], start=True, stop=not last)
                        for e in last:
                            mm = pe.matmul(ps(u % 2, n)[:, e[1]:e[1] + P], identb[:, :], maskb[:, e[2], :],
                                           start=False, stop=(e is last[-1]))
                        mm.then_inc(s["S"], 1)

                    def pv(g, j, u):
                        kt, q0, q1 = units[u]
                        U_ = NU * (C_GROUP * g + j) + u
                        pe.wait_ge(s["P"], U_ + 1)
                        if u == 0:
                            at_least(pe, "o", C_GROUP * g + j)
                        for c in range(2):
                            lo, hi = max(q0, 4 * c), min(q1, 4 * c + 4)
                            if lo < hi:
                                mm = pe.matmul(ps(2 + c, BANK, slice(0, 65))[:, (lo - 4 * c) * P:(hi - 4 * c) * P],
                                               V1[:, kt, g, :], pr[u % 2][:, (lo - q0) * P:(hi - q0) * P],
                                               start=(kt == 8), stop=(kt == (4 if c == 0 else 7)))
                        mm.then_inc(s["PV"], 1)

                    def spread(idx, G):
                        nonlocal spreads
                        at_least(pe, "rawc", NW * G + min(idx, NW))
                        at_least(pe, "out", NW * G + min(max(idx - 1, 0), NW))
                        at_least(pe, "mc", 8 * C_GROUP * G + min(max(idx - 6, 0), 8 * C_GROUP))
                        at_least(pe, "mr", C_GROUP * G + max(idx - 6 - 8 * C_GROUP, 0))
                        pe.wait_ge(s["os"], spreads + 1)
                        for c in range(2):
                            mm = pe.matmul(ps(RB + c, BANK, slice(0, 64)), cst[0:65, C_SEL:C_SEL + 64],
                                           o65[0:65, c * BANK:(c + 1) * BANK], start=True, stop=True)
                        mm.then_inc(s["bc"], 1)
                        spreads += 1

                    def step(n, G):
                        at_least(pe, "fin", spreads)
                        if n < NW:
                            t_, c = prods[n]
                            lo, hi = CH[c]
                            pe.wait_ge(s[f"w{t_}"], 16 * (G + 1))
                            at_least(pe, "rawc", NW * G + n)
                            at_least(pe, "mr", C_GROUP * G)
                            for k in range(KT):
                                mm = pe.matmul(ps(RB, hi - lo), wt[t_][:, k, :], U[:, k, lo:hi],
                                               start=(k == 0), stop=(k == KT - 1))
                            mm.then_inc(s["raw"], 1)
                        if 0 < n < NW + 1:
                            w = n - 1
                            lo, hi = CH[prods[w][1]]
                            pe.wait_ge(s["sq"], NW * G + w + 1)
                            at_least(pe, "out", NW * G + w)
                            pe.matmul(ps(NB, hi - lo), bones, sq[w % 2][:, :hi - lo], start=True, stop=True)
                            pe.matmul(ps(TB, hi - lo), rot1[:, 1 - prods[w][0], :], raw[w % 2][:, :hi - lo],
                                      start=True, stop=True).then_inc(s["nt"], 1)
                        if 6 <= n < 6 + 8 * C_GROUP:
                            j, qt = divmod(n - 6, 8)
                            if n == 6:
                                pe.wait_ge(s["cast"], NW * (G + 1))
                            at_least(pe, "mc", 8 * C_GROUP * G + n - 6)
                            q = qb[j][0:64, qt * P:(qt + 1) * P]
                            lo, hi = WIN[qt]
                            pe.matmul(ps(RB, BANK)[:, CTX:BANK], q, kb[0:64, SEQ:T], start=True, stop=True)
                            nk = (hi - lo) * P
                            pe.matmul(ps(NB, nk), q, kb[0:64, lo * P:hi * P], start=True, stop=False)
                            if qt > 0:
                                mm = pe.matmul(ps(NB, P), identb[:, :], maskb[:, 0, :], start=False, stop=(qt == 7))
                            if qt < 7:
                                mm = pe.matmul(ps(NB, nk)[:, nk - P:nk], identb[:, :], maskb[:, 1, :],
                                               start=False, stop=True)
                            mm.then_inc(s["mx"], 1)
                        if n >= 6 + 8 * C_GROUP:
                            j = n - 6 - 8 * C_GROUP
                            pe.wait_ge(s["mn"], C_GROUP * G + j + 1)
                            at_least(pe, "mr", C_GROUP * G + j)
                            for m in range(8):
                                mm = pe.matmul(ps(RB + m // 4, BANK, slice(64, 65))[:, (m % 4) * P:(m % 4 + 1) * P],
                                               mcb[:, 8 * j + m:8 * j + m + 1], identb[:, :], start=True, stop=True)
                            mm.then_inc(s["mrow"], 1)

                    def begin(g, j, u):
                        if u == 0:
                            qk(g, j, 0)
                        if u + 1 < NU:
                            qk(g, j, u + 1)
                        if u == 2 and (g or j):
                            G = g + 1
                            spread(sum(pl < (j, u) for pl in places) if G < C_KV else 0, G)

                    pe.wait_ge(s["tab"], 16)
                    pe.wait_ge(s["one"], 2)
                    everywhere(step, pv, begin, lambda g, j: None)
                    spread(0, C_KV)

                @block.scalar
                def _(act):
                    def step(n, G):
                        if n < NW:
                            lo, hi = CH[prods[n][1]]
                            m = hi - lo
                            act.wait_ge(s["raw"], NW * G + n + 1)
                            at_least(act, "nt", NW * G + n - 1)
                            at_least(act, "t1", NW * G + n - 1)
                            act.activation(raw[n % 2][:, :m], ps(RB, m), ACT.Copy).then_inc(s["rawc"], 1)
                            act.wait_ge(s["rawc"], NW * G + n + 1)
                            act.activation(sq[n % 2][:, :m], raw[n % 2][:, :m], ACT.Square).then_inc(s["sq"], 1)
                        if 0 < n < NW + 1:
                            w = n - 1
                            lo, hi = CH[prods[w][1]]
                            m = hi - lo
                            act.wait_ge(s["nt"], NW * G + w + 1)
                            at_least(act, "rinv", NW * G + w)
                            act.activation(lnb[:, :m], ps(NB, m), ACT.Ln, bias=eps[:, 0:1], scale=1.0 / C_HD)\
                                .then_inc(s["ln"], 1)
                            act.wait_ge(s["ln"], NW * G + w + 1)
                            act.activation(ps(NB, m), lnb[:, :m], ACT.Exp, scale=-0.5).then_inc(s["rinv"], 1)
                        if n >= 6 + 8 * C_GROUP:
                            j = n - 6 - 8 * C_GROUP
                            act.wait_ge(s["mrow"], C_GROUP * G + j + 1)
                            act.activation(qa[G % 2][j][64:65, :], PS[64:65, RB * BANK:RB * BANK + SEQ], ACT.Copy)\
                                .then_inc(s["mr"], 1)

                    def attend(g, j, u):
                        _, q0, q1 = units[u]
                        n = (q1 - q0) * P
                        U_ = NU * (C_GROUP * g + j) + u
                        act.wait_ge(s["S"], U_ + 1)
                        at_least(act, "PV", U_ - 1)
                        act.activation(pr[u % 2][:, :n], ps(u % 2, n), ACT.Exp, scale=C_SCALE).then_inc(s["P"], 1)

                    def end(g, j):
                        h = C_GROUP * g + j
                        act.wait_ge(s["PV"], NU * (h + 1))
                        at_least(act, "fin", h)
                        act.activation(o65[0:65, :], PS[0:65, 2 * BANK:2 * BANK + SEQ], ACT.Copy).then_inc(s["o"], 1)
                        act.activation(es, qa[g % 2][j][64:65, :].rearrange("p (x y) -> p x y", x=4), ACT.Exp,
                                       scale=C_SCALE, bias=sml[64:65, W_SINK + h:W_SINK + h + 1]).then_inc(s["es"], 1)

                    everywhere(step, attend, lambda g, j, u: None, end)

                @block.vector
                def _(dve):
                    heads = 0

                    def finish():
                        nonlocal heads
                        h = heads
                        heads += 1
                        dve.wait_ge(s["o"], h + 1)
                        dve.wait_ge(s["es"], h + 1)
                        row = o65[64:65, :].rearrange("p (x y) -> p x y", x=4)
                        dve.tensor_tensor(row, row, es, ALU.add).then_inc(s["os"], 1)
                        dve.wait_ge(s["bc"], h + 1)
                        r = PS[0:64, RB * BANK:RB * BANK + SEQ]
                        dve.reciprocal(r, r).then_inc(s["rs"], 1)
                        dve.wait_ge(s["rs"], h + 1)
                        half = 64 * (h % 2)
                        dve.tensor_tensor(MIX1[half:half + 64, h // 2, :], o65[0:64, :], r, ALU.mult)\
                            .then_inc(s["fin"], 1)

                    def step(n, G):
                        b = G % 2
                        if 0 < n < NW + 1:
                            w = n - 1
                            t_, c = prods[w]
                            lo, hi = CH[c]
                            m = hi - lo
                            q = NW * G + w
                            dve.wait_ge(s["sq"], q + 1)
                            at_least(dve, "out", q)
                            dve.scalar_tensor_tensor(out=t1[:, :m], in0=raw[w % 2][:, :m],
                                                     scalar=sml[:, W_G1 + 1 - t_:W_G1 + 2 - t_],
                                                     in1=rope[:, 0, lo:hi], op0=ALU.mult, op1=ALU.mult)\
                                .then_inc(s["t1"], 1)
                            dve.wait_ge(s["nt"], q + 1)
                            T_ = ps(TB, m)
                            dve.tensor_tensor(T_, T_, rope[:, 1, lo:hi], ALU.mult).then_inc(s["ts"], 1)
                            dve.wait_ge(s["ts"], q + 1)
                            dve.tensor_tensor(t1[:, :m], t1[:, :m], T_, ALU.add).then_inc(s["ta"], 1)
                            dve.wait_ge(s["ta"], q + 1)
                            dve.wait_ge(s["rinv"], q + 1)
                            dsts = [qa[b][2] if c < 2 else None, ka[b]] if t_ == 0 else [qa[b][0], qa[b][1]]
                            for r, dst in enumerate(dsts):
                                if dst is not None:
                                    op = dve.tensor_tensor(dst[0:64, lo:hi], t1[64 * r:64 * r + 64, :m],
                                                           ps(NB, m, slice(64 * r, 64 * r + 64)), ALU.mult)
                            op.then_inc(s["out"], 1)
                        if 6 <= n < 6 + 8 * C_GROUP:
                            m = n - 6
                            dve.wait_ge(s["mx"], 8 * C_GROUP * G + m + 1)
                            if m == 0:
                                at_least(dve, "mn", C_GROUP * G)
                            lo, hi = WIN[m % 8]
                            dve.reduce_max(mc[:, m:m + 1],
                                           PS[:, RB * BANK + CTX:NB * BANK + (hi - lo) * P], AX_X)\
                                .then_inc(s["mc"], 1)
                        if n >= 6 + 8 * C_GROUP:
                            j = n - 6 - 8 * C_GROUP
                            h = C_GROUP * G + j
                            dve.wait_ge(s["mc"], 8 * C_GROUP * (G + 1))
                            at_least(dve, "mrow", C_GROUP * G)
                            dve.tensor_scalar(mcb[:, 8 * j:8 * j + 8], mc[:, 8 * j:8 * j + 8], s8[:, h:h + 1], -1.0,
                                              ALU.max, ALU.mult).then_inc(s["mn"], 1)

                    dve.tensor_scalar(s8, sml[:, W_SINK:W_SINK + C_HEADS], 1 / C_SCALE, None, ALU.mult)\
                        .then_inc(s["s8"], 1)
                    dve.wait_ge(s["s8"], 1)
                    dve.wait_ge(s["tab"], 16)

                    def begin(g, j, u):
                        if u == 2 and (g or j):
                            finish()
                    everywhere(step, lambda g, j, u: None, begin, lambda g, j: None)
                    finish()

        mods()
        norm(0, 0, T)
        linear("in0_", a["w_in0"], U, KT, 6, T, O_A, copy_take(H, T))
        latent_norms()
        fourier()
        heads0()
        recycle()
        linear("out0_", a["w_out0"], MIX, KT, KT, T, O_A, residual(0, 2, T))
        norm(0, 1, T)
        ffn(0, T)
        recycle()
        norm(1, 0, T)
        linear("pool_", a["w_pool"], U, KT, 2, SEQ, O_B, pool_take)
        pooling()
        values1()
        heads1()
        linear("out1_", a["w_out1"], MIX1, KT, KT, SEQ, O_B, residual(1, 2, SEQ))
        norm(1, 1, SEQ)
        ffn(1, SEQ)
        stored = sem("stored")
        with nc.Block() as block:
            @block.sync
            def _(sp):
                sp.dma_start(out, X[:, :, 0:SEQ]).then_inc(stored, 16)
                sp.wait_ge(stored, 16)


def kernel(**inputs):
    import concourse.bacc as bacc
    from concourse.bass_utils import run_bass_kernel_spmd

    f = {k: np.asarray(v) for k, v in inputs.items()}

    def cols(v):
        return v.reshape(-1, P).T

    def rows(m):
        return m.reshape(-1, P, m.shape[-1]).transpose(1, 0, 2)

    def tiles(m, width=P):
        k, n = m.shape
        return m.reshape(k // P, P, n // width, width).transpose(2, 1, 0, 3).reshape(n // width, P, -1)

    def twice(v):
        return np.repeat(v[..., None], 2, axis=-1).reshape(v.shape[0], -1)

    z = {"xT": rows(np.concatenate([f["x"][0], f["ctx"][0]], 0).T),
         "cT": np.stack([cols(f["c"][0]), cols(f["c_ctx"])], -1)}
    z["mod_w"] = f["mod_w"].reshape(DEPTH, KT, P, -1, BANK).transpose(0, 3, 2, 1, 4).reshape(-1, P, KT, BANK)
    small = np.zeros((P, N_SMALL), np.float32)

    def put(col, v, r=0):
        small[r:r + v.shape[0], col:col + v.shape[1]] = v
    put(W_MODB, twice(cols(f["mod_b"].reshape(-1))))
    for layer in range(DEPTH):
        for n, g in enumerate((f["norm1_g"], f["norm2_g"])):
            put(W_NG + (2 * layer + n) * 2 * KT, twice(cols(g[layer])))
    put(W_CQG, cols(f["mla_cq_g"][0]))
    put(W_CKVG, cols(f["mla_ckv_g"][0]))
    put(W_G0, f["mla_q_g"].T)
    put(W_G0 + 1, f["mla_k_g"].T)
    q, k = f["win_q_g"].T, f["win_k_g"].T
    put(W_G1, np.concatenate([q, q]))
    put(W_G1 + 1, np.concatenate([q, k]))
    put(W_SINK, np.tile(f["win_sink"].reshape(1, -1), (P, 1)))
    put(W_PS, cols(f["pool_scale"][0]))
    for p in range(2):
        for i in range(2):
            put(W_FN + p * P + 64 * i, f["fnet_w"][0, 2 * p + i], 64 * i)
            put(W_PW + p * P + 64 * i, f["pool_w"][0, 2 * p + i], 64 * i)
    z["small"] = small
    w = f["mla_w_in"][0]
    pad = np.zeros((D, 96), np.float32)
    z["w_in0"] = tiles(np.concatenate([w[:, :416], pad, w[:, 416:]], 1))
    uq = f["mla_w_uq"][0].reshape(2, P, A_HEADS, A_QK).transpose(2, 1, 0, 3).reshape(A_HEADS, P, -1)
    ukv = f["mla_w_ukv"][0].reshape(P, A_HEADS, 128)
    z["wqk0"] = np.concatenate([uq, ukv[:, :, :64].transpose(1, 0, 2)], -1)
    z["w_v0"] = ukv[:, :, 64:].reshape(P, -1)
    z["w_out0"] = tiles(f["even_w_out"][0])
    w = f["win_w_in"][0]
    qs = w[:, :768].reshape(D, C_KV, C_GROUP, 64)
    ks = w[:, 768:1024].reshape(D, C_KV, 64)
    z["wqk1"] = np.concatenate([t for g in range(C_KV) for t in (
        tiles(np.concatenate([qs[:, g, 2], ks[:, g]], 1)), tiles(np.concatenate([qs[:, g, 0], qs[:, g, 1]], 1)))])
    z["w_v1"] = rows(w[:, 1024:1280])
    z["w_pool"] = tiles(w[:, 1280:])
    z["w_out1"] = tiles(f["odd_w_out"][0])
    z["w_up"] = np.stack([tiles(m) for m in f["ffn_up"]])
    z["w_down"] = np.stack([np.stack([tiles(h) for h in (m[:FG * P], m[FG * P:])]) for m in f["ffn_down"]])
    conv = np.concatenate([f["ffn_conv_w"], f["ffn_conv_b"][:, None]], 1)
    z["conv"] = conv.reshape(DEPTH, 4, 2 * FT, P).transpose(0, 3, 2, 1).reshape(DEPTH, P, -1)
    z.update(constants())

    nc = bacc.Bacc("TRN2", target_bir_lowering=False, num_devices=1,
                   dynamic_dma_scratch_size=1024)
    arrays, args = {}, {}
    for name, v in z.items():
        v = np.ascontiguousarray(v)
        arrays["in_" + name] = v
        args[name] = nc.dram_tensor("in_" + name, v.shape, F32, kind="ExternalInput").ap()
    out = nc.dram_tensor("out", (P, KT, SEQ), F32, kind="ExternalOutput").ap()
    program(nc, args, out)
    r = run_bass_kernel_spmd(nc, [arrays], core_ids=[0])
    y = np.asarray(r.results[0]["out"])
    return y.transpose(2, 1, 0).reshape(1, SEQ, D)
```

```python
from contextlib import ExitStack

import numpy as np

import concourse.bass as bass
from concourse import mybir

F32 = mybir.dt.float32
BF16 = mybir.dt.bfloat16
F32R = mybir.dt.float32r
ALU = mybir.AluOpType
ACT = mybir.ActivationFunctionType
AX_X = mybir.AxisListType.X
ds = bass.ds

P = 128
D = 1024
KT = D // P
SEQ, CTX = 1024, 256
T = SEQ + CTX
GRID_W = 64
DEPTH = 2
N_MOD = 6
EPS = 1e-6
BANK = 512
CH = [(0, 512), (512, 1024), (1024, 1280)]
STREAMS = [(0, SEQ, 0), (SEQ, T, 1)]

A_HEADS, A_NOPE, A_ROPE, A_V = 12, 64, 32, 64
A_QK = A_NOPE + A_ROPE
A_SCALE = A_QK ** -0.5
C_HEADS, C_KV, C_HD = 12, 4, 64
C_GROUP = C_HEADS // C_KV
C_SCALE = C_HD ** -0.5
D_FF = 2816
FT = D_FF // P
MASKED = -1e30

C_IDENT, C_ONES, C_BONES, C_R0, C_R1, C_SEL, C_GE, C_LE, C_COSC, C_SINC = [i * P for i in range(10)]
N_CONST = 10 * P
(W_MODB, W_NG, W_CQG, W_CKVG, W_G0, W_G1, W_SINK, W_PS, W_FN, W_PW) = np.cumsum(
    [0, 192, 4 * KT * 2, 2, 1, 2, 2, 12, 2, 256]).tolist()

N_SMALL = W_PW + 256


def constants():
    c = np.zeros((P, N_CONST), np.float32)
    i = np.arange(P)
    c[:, C_IDENT:C_IDENT + P] = np.eye(P)
    c[:, C_ONES:C_ONES + P] = 1
    c[:, C_BONES:C_BONES + P] = (i[:, None] // 64) == (i[None, :] // 64)
    for m in range(16):
        c[64 + m + 16, C_R0 + 64 + m] = -1
        c[64 + m, C_R0 + 64 + m + 16] = 1
    for b in (0, 64):
        for m in range(32):
            c[b + m + 32, C_R1 + b + m] = -1
            c[b + m, C_R1 + b + m + 32] = 1
    c[64, C_SEL:C_SEL + 64] = c[96, C_SEL:C_SEL + 64] = 1
    c[:, C_GE:C_GE + P] = np.where(i[None, :] >= i[:, None], 0, MASKED)
    c[:, C_LE:C_LE + P] = np.where(i[None, :] <= i[:, None], 0, MASKED)
    ang = 2 * np.pi * np.outer(np.arange(64), np.arange(64)) / 64
    for b in (0, 64):
        c[b:b + 64, C_COSC + b:C_COSC + b + 64] = np.cos(ang) / 256
        c[b:b + 64, C_SINC + b:C_SINC + b + 64] = -np.sin(ang) / 256
    t = np.arange(SEQ)

    def rope(dim):
        n = dim // 4
        inv = np.float32(10000.0) ** (-np.arange(n, dtype=np.float32) / np.float32(n))
        row, col = (t // GRID_W).astype(np.float32), (t % GRID_W).astype(np.float32)
        a = np.concatenate([row[:, None] * inv, col[:, None] * inv], axis=-1)
        return np.cos(a).T.astype(np.float32), np.sin(a).T.astype(np.float32)

    rope0 = np.zeros((A_QK, 2, T), np.float32)
    rope0[:, 0] = 1
    cs, sn = rope(A_ROPE)
    for b in (64, 80):
        rope0[b:b + 16, 0, :SEQ], rope0[b:b + 16, 1, :SEQ] = cs, sn
    rope1 = np.zeros((P, 2, T), np.float32)
    rope1[:, 0] = 1
    cs, sn = rope(C_HD)
    for b in (0, 32, 64, 96):
        rope1[b:b + 32, 0, :SEQ], rope1[b:b + 32, 1, :SEQ] = cs, sn

    def dft(n, scale):
        k = np.outer(np.arange(n), np.arange(n)) % n
        a = 2 * np.pi * k / n
        m = np.stack([np.cos(a), np.sin(a)], 1) * scale
        return m.astype(np.float32).reshape(n // P, P, 2, n)

    half = np.array([1, 2, 4, 8])
    cnt = np.clip(t[None] + half[:, None], 0, SEQ) - np.clip(t[None] - half[:, None], 0, SEQ)
    inv = np.repeat(1.0 / cnt, 64, axis=0).reshape(2, P, SEQ).transpose(1, 0, 2).astype(np.float32)
    return {"const": c, "rope0": rope0, "rope1": rope1, "dft": dft(SEQ, 1), "dftc": dft(CTX, 2),
            "pool_inv": np.ascontiguousarray(inv)}


def program(nc, a, out):
    ctx = ExitStack()
    with ctx:
        def sb(name, shape, dt=F32):
            return ctx.enter_context(nc.sbuf_tensor(name, shape, dt))

        held = []

        def sem(name):
            held.append(nc.alloc_semaphore(name))
            return held[-1]

        def recycle():
            nc.clear_and_free_semaphores(list(held))
            held.clear()
            nc.all_engine_barrier()

        X = sb("X", [P, KT, T])
        cst = sb("cst", [P, N_CONST])
        sml = sb("sml", [P, N_SMALL])
        mod = sb("mod", [P, DEPTH * N_MOD * KT, 2])
        gsc = sb("gsc", [P, DEPTH * 2 * KT, 2])
        eps = sb("eps", [P, 1])
        identb = sb("identb", [P, P], BF16)
        maskb = sb("maskb", [P, 2, P], BF16)
        rot0 = sb("rot0", [A_QK, 2, A_QK])
        rot1 = sb("rot1", [P, 2, P])
        BIGN = 33590
        PS = ctx.enter_context(nc.psum_tensor("PS", [P, 8 * BANK], F32))

        def big(off, *shape):
            n = int(np.prod(shape))
            assert off + n <= BIGN, (off, n)
            v = BIG[:, off:off + n]
            if len(shape) == 2:
                v = v.rearrange("p (x y) -> p x y", x=shape[0])
            if len(shape) == 3:
                v = v.rearrange("p (x y z) -> p x y z", x=shape[0], y=shape[1])
            return v

        def ps(bank, n, rows=slice(0, P)):
            return PS[rows, bank * BANK:bank * BANK + n]

        ident = cst[:, C_IDENT:C_IDENT + P]
        ones = cst[:, C_ONES:C_ONES + P]
        bones = cst[:, C_BONES:C_BONES + P]

        def moda(layer, which, tile, s, n=1):
            return mod[:, ds((layer * N_MOD + which) * KT + tile, n), s]

        def workspace(tag):
            stack = ExitStack()
            return (stack, stack.enter_context(nc.sbuf_tensor("U" + tag, [P, KT, T], F32)),
                    stack.enter_context(nc.sbuf_tensor("BIG" + tag, [P, BIGN], F32)))

        def mods():
            sil = big(0, KT, 2)
            cT = big(16, KT, 2)
            row = big(32, 2, BANK)
            W = [big(2048 + b * KT * BANK, KT, BANK) for b in range(2)]
            NC = DEPTH * N_MOD * D // BANK
            with ExitStack() as c2:
                s = {n: sem("mod_" + n) for n in
                     ("in", "sil", "w0", "w1", "rows0", "rows1", "rowc0", "rowc1", "cols0", "cols1", "out0", "out1",
                      "dve")}
                block = c2.enter_context(nc.Block())

                @block.sync
                def _(sp):
                    sp.dma_start(cT, a["cT"]).then_inc(s["in"], 16)
                    sp.dma_start(sml[:, :], a["small"]).then_inc(s["in"], 16)
                    sp.dma_start(cst[:, :], a["const"]).then_inc(s["in"], 16)
                    sp.dma_start(X[:, :, :], a["xT"]).then_inc(s["in"], 16)
                    with sp.Fori(0, NC // 2) as i:
                        for b in range(2):
                            sp.wait_ge(s[f"rows{b}"], i)
                            sp.dma_start(W[b], a["mod_w"][ds(2 * i + b, 1)].rearrange("o p k n -> (o p) k n"))\
                                .then_inc(s[f"w{b}"], 16)

                @block.scalar
                def _(act):
                    act.wait_ge(s["in"], 64)
                    act.activation(sil, cT, ACT.Silu).then_inc(s["sil"], 1)
                    with act.Fori(0, NC // 2) as i:
                        for b in range(2):
                            act.wait_ge(s[f"rows{b}"], i + 1)
                            act.wait_ge(s[f"cols{b}"], i)
                            act.activation(row[0:2, b, :], ps(b, BANK, slice(0, 2)), ACT.Copy)\
                                .then_inc(s[f"rowc{b}"], 1)

                @block.tensor
                def _(pe):
                    pe.wait_ge(s["sil"], 1)
                    with pe.Fori(0, NC // 2) as i:
                        for b in range(2):
                            pe.wait_ge(s[f"w{b}"], 16 * i + 16)
                            pe.wait_ge(s[f"rowc{b}"], i)
                            for k in range(KT):
                                mm = pe.matmul(ps(b, BANK, slice(0, 2)), sil[:, k, :], W[b][:, k, :],
                                               start=(k == 0), stop=(k == KT - 1))
                            mm.then_inc(s[f"rows{b}"], 1)
                            pe.wait_ge(s[f"rowc{b}"], i + 1)
                            pe.wait_ge(s[f"out{b}"], i)
                            for j in range(4):
                                mm = pe.matmul(ps(2 + b, 8)[:, 2 * j:2 * j + 2], row[0:2, b, j * P:(j + 1) * P],
                                               cst[0:2, C_IDENT:C_IDENT + 2], start=True, stop=True)
                            mm.then_inc(s[f"cols{b}"], 1)

                @block.vector
                def _(dve):
                    dve.memset(eps[:, :], EPS).then_inc(s["dve"], 1)
                    dve.wait_ge(s["in"], 64)
                    dve.tensor_copy(identb[:, :], ident).then_inc(s["dve"], 1)
                    for n, col in enumerate((C_GE, C_LE)):
                        dve.tensor_copy(maskb[:, n, :], cst[:, col:col + P]).then_inc(s["dve"], 1)
                    for n in range(2):
                        dve.tensor_scalar(rot0[:, n, :], cst[0:A_QK, C_R0:C_R0 + A_QK],
                                          sml[0:A_QK, W_G0 + n:W_G0 + n + 1], None, ALU.mult).then_inc(s["dve"], 1)
                        dve.tensor_scalar(rot1[:, n, :], cst[:, C_R1:C_R1 + P],
                                          sml[:, W_G1 + n:W_G1 + n + 1], None, ALU.mult).then_inc(s["dve"], 1)
                    modb = sml[:, W_MODB:W_MODB + 192].rearrange("p (x y) -> p x y", y=2)
                    with dve.Fori(0, NC // 2) as i:
                        for b in range(2):
                            dve.wait_ge(s[f"cols{b}"], i + 1)
                            dve.tensor_tensor(mod[:, ds(8 * i + 4 * b, 4), :],
                                              ps(2 + b, 8).rearrange("p (x y) -> p x y", y=2),
                                              modb[:, ds(8 * i + 4 * b, 4), :], ALU.add).then_inc(s[f"out{b}"], 1)
                    for b in range(2):
                        dve.wait_ge(s[f"out{b}"], NC // 2)
                    for n in range(2 * DEPTH):
                        layer, which = n // 2, 1 + 3 * (n % 2)
                        o = (layer * N_MOD + which) * KT
                        g = sml[:, W_NG + n * 2 * KT:W_NG + (n + 1) * 2 * KT].rearrange("p (x y) -> p x y", y=2)
                        dve.scalar_tensor_tensor(out=gsc[:, n * KT:(n + 1) * KT, :], in0=mod[:, o:o + KT, :],
                                                 scalar=1.0, in1=g, op0=ALU.add, op1=ALU.mult).then_inc(s["dve"], 1)

        def norm(layer, which, tokens):
            tag = f"n{layer}{which}_"
            chunks = [c for c in CH if c[0] < tokens]
            streams = [x for x in STREAMS if x[0] < tokens]
            sq = big(0, 2, T)
            lnb = big(2 * T, T)
            with ExitStack() as c2:
                s = {n: sem(tag + n) for n in
                     ("sq", "acc", "ln", "rinv", "u", "sh")}
                block = c2.enter_context(nc.Block())

                @block.scalar
                def _(act):
                    act.preload_act_table_set("natural_log_exp_and_others")
                    for k in range(KT):
                        if k >= 2:
                            act.wait_ge(s["acc"], k - 1)
                        act.activation(sq[:, k % 2, :tokens], X[:, k, :tokens], ACT.Square).then_inc(s["sq"], 1)
                    act.wait_ge(s["acc"], KT)
                    act.activation(lnb[:, :tokens], PS[:, 0:tokens], ACT.Ln, bias=eps[:, 0:1], scale=1.0 / D)\
                        .then_inc(s["ln"], 1)
                    act.wait_ge(s["ln"], 1)
                    act.activation(PS[:, 0:tokens], lnb[:, :tokens], ACT.Exp, scale=-0.5).then_inc(s["rinv"], 1)
                    for k in range(KT):
                        act.wait_ge(s["u"], k + 1)
                        for lo, hi, v in streams:
                            act.activation(U[:, k, lo:hi], U[:, k, lo:hi], ACT.Identity,
                                           bias=moda(layer, 3 * which, k, v)).then_inc(s["sh"], 1)

                @block.tensor
                def _(pe):
                    for k in range(KT):
                        pe.wait_ge(s["sq"], k + 1)
                        for n, (lo, hi) in enumerate(chunks):
                            mm = pe.matmul(ps(n, hi - lo), ones, sq[:, k % 2, lo:hi],
                                           start=(k == 0), stop=(k == KT - 1))
                        mm.then_inc(s["acc"], 1)

                @block.vector
                def _(dve):
                    dve.wait_ge(s["rinv"], 1)
                    for k in range(KT):
                        for lo, hi, v in streams:
                            g = gsc[:, (2 * layer + which) * KT + k, v:v + 1]
                            op = dve.scalar_tensor_tensor(out=U[:, k, lo:hi], in0=X[:, k, lo:hi], scalar=g,
                                                          in1=PS[:, lo:hi], op0=ALU.mult, op1=ALU.mult)
                        op.then_inc(s["u"], 1)

        def linear(tag, w, rhs, K, tiles, tokens, woff, take, prefetch=None):
            chunks = [c for c in CH if c[0] < tokens]
            W = [big(woff + b * K * P, K, P) for b in range(2)]
            with ExitStack() as c2:
                s = {n: sem(tag + n) for n in ("w0", "w1", "mm0", "mm1", "taken0", "taken1")}
                block = c2.enter_context(nc.Block())

                @block.sync
                def _(sp):
                    with sp.Fori(0, tiles // 2) as i:
                        for b in range(2):
                            sp.wait_ge(s[f"mm{b}"], i)
                            sp.dma_start(W[b], w[ds(2 * i + b, 1)].rearrange("o p (k n) -> (o p) k n", k=K))\
                                .then_inc(s[f"w{b}"], 16)

                @block.tensor
                def _(pe):
                    with pe.Fori(0, tiles // 2) as i:
                        for b in range(2):
                            pe.wait_ge(s[f"w{b}"], 16 * i + 16)
                            pe.wait_ge(s[f"taken{b}"], i)
                            for k in range(K):
                                for n, (lo, hi) in enumerate(chunks):
                                    mm = pe.matmul(ps(3 * b + n, hi - lo), W[b][:, k, :], rhs[:, k, lo:hi],
                                                   start=(k == 0), stop=(k == K - 1))
                            mm.then_inc(s[f"mm{b}"], 1)

                @block.vector
                def _(dve):
                    with dve.Fori(0, tiles // 2) as i:
                        for b in range(2):
                            dve.wait_ge(s[f"mm{b}"], i + 1)
                            take(dve, 2 * i + b, PS[:, 3 * b * BANK:3 * b * BANK + tokens])\
                                .then_inc(s[f"taken{b}"], 1)

        def residual(layer, which, tokens):
            def take(dve, m, y):
                for lo, hi, v in [x for x in STREAMS if x[0] < tokens]:
                    xs = X[:, ds(m, 1), lo:hi].rearrange("p o n -> p (o n)")
                    op = dve.scalar_tensor_tensor(out=xs, in0=y[:, lo:hi], scalar=moda(layer, which, m, v), in1=xs,
                                                  op0=ALU.mult, op1=ALU.add)
                return op
            return take

        def split_norm(layer, which, n, uh, ul):
            tag = f"s{layer}{which}_"
            chunks = [c for c in CH if c[0] < n]
            streams = [x for x in STREAMS if x[0] < n]
            with ExitStack() as c2:
                sq = c2.enter_context(nc.sbuf_tensor(tag + "sq", [P, 2, n], F32))
                lnb = c2.enter_context(nc.sbuf_tensor(tag + "lnb", [P, n], F32))
                tt = c2.enter_context(nc.sbuf_tensor(tag + "tt", [P, 2, n], F32))
                s = {n_: sem(tag + n_) for n_ in ("sq", "acc", "ln", "rinv", "t", "uh", "ul")}
                block = c2.enter_context(nc.Block())

                @block.scalar
                def _(act):
                    act.preload_act_table_set("natural_log_exp_and_others")
                    for k in range(KT):
                        if k >= 2:
                            act.wait_ge(s["acc"], k - 1)
                        act.activation(sq[:, k % 2, :], X[:, k, 0:n], ACT.Square).then_inc(s["sq"], 1)
                    act.wait_ge(s["acc"], KT)
                    act.activation(lnb[:, :], PS[:, 0:n], ACT.Ln, bias=eps[:, 0:1], scale=1.0 / D)\
                        .then_inc(s["ln"], 1)
                    act.wait_ge(s["ln"], 1)
                    act.activation(PS[:, 0:n], lnb[:, :], ACT.Exp, scale=-0.5).then_inc(s["rinv"], 1)
                    for k in range(KT):
                        act.wait_ge(s["t"], k + 1)
                        for lo, hi, v in streams:
                            op = act.activation(uh[:, k, lo:hi], tt[:, k % 2, lo:hi], ACT.Identity,
                                                bias=moda(layer, 3 * which, k, v))
                        op.then_inc(s["uh"], 1)

                @block.tensor
                def _(pe):
                    for k in range(KT):
                        pe.wait_ge(s["sq"], k + 1)
                        for c0, c1 in chunks:
                            mm = pe.matmul(PS[:, c0:c1], ones, sq[:, k % 2, c0:c1], start=(k == 0), stop=(k == KT - 1))
                        mm.then_inc(s["acc"], 1)

                @block.vector
                def _(dve):
                    dve.wait_ge(s["rinv"], 1)

                    def rest(k):
                        dve.wait_ge(s["uh"], k + 1)
                        for lo, hi, v in streams:
                            op = dve.scalar_tensor_tensor(
                                out=ul[:, k, lo:hi], in0=tt[:, k % 2, lo:hi], scalar=moda(layer, 3 * which, k, v),
                                in1=uh[:, k, lo:hi].bitcast(F32), op0=ALU.add, op1=ALU.subtract)
                        op.then_inc(s["ul"], 1)
                    for k in range(KT):
                        if k >= 2:
                            dve.wait_ge(s["ul"], k - 1)
                        for lo, hi, v in streams:
                            g = gsc[:, (2 * layer + which) * KT + k, v:v + 1]
                            op = dve.scalar_tensor_tensor(out=tt[:, k % 2, lo:hi], in0=X[:, k, lo:hi], scalar=g,
                                                          in1=PS[:, lo:hi], op0=ALU.mult, op1=ALU.mult)
                        op.then_inc(s["t"], 1)
                        if k:
                            rest(k - 1)
                    rest(KT - 1)

        def ffn(layer, n):
            tag = f"f{layer}_"
            chunks = [c for c in CH if c[0] < n]
            streams = [x for x in STREAMS if x[0] < n]
            NG = FT // 2
            with ExitStack() as c2:
                def buf(name, shape, dt=F32):
                    return c2.enter_context(nc.sbuf_tensor(tag + name, shape, dt))
                uh = buf("uh", [P, KT, n], F32R)
                ul = buf("ul", [P, KT, n], F32R)
                split_norm(layer, 1, n, uh, ul)
                gh = buf("gh", [P, 2, n], F32R)
                gl = buf("gl", [P, 2, n], F32R)
                W = [buf(f"W{b}", [P, KT, P]) for b in range(2)]
                Wh = [buf(f"Wh{b}", [P, KT, P], F32R) for b in range(2)]
                Wl = [buf(f"Wl{b}", [P, KT, P], F32R) for b in range(2)]
                WD = buf("WD", [P, 2, D])
                WDh = buf("WDh", [P, 2, D], F32R)
                WDl = buf("WDl", [P, 2, D], F32R)
                cg = buf("cg", [P, n])
                cv = buf("cv", [P, n])
                sg = buf("sg", [P, n])
                gp = buf("gp", [P, n])
                cw = buf("cw", [P, 2 * FT, 4])
                s = {n_: sem(tag + n_) for n_ in
                     ("cw", "w0", "w1", "wd", "hi", "lo", "up", "cen", "left", "conv", "silu", "mul", "gh", "gl",
                      "dhi", "dlo", "y", "acc")}
                block = c2.enter_context(nc.Block())
                PLACES = [(0, 0), (0, 1), (1, 0), (1, 1)]
                UPB = [0, 3]
                DNB = [6, 7]
                outs = [(m, c) for m in range(KT) for c in range(len(chunks))]
                NO = len(outs)

                def at_least(eng, name, value):
                    if not (isinstance(value, int) and value <= 0):
                        eng.wait_ge(s[name], value)

                def psv(bank):
                    return PS[:, bank * BANK:bank * BANK + n]

                def groups(eng, group, last):
                    group(0, False, True)
                    with eng.Fori(1, NG - 1) as g:
                        group(g, True, True)
                    group(NG - 1, True, False)
                    last()

                @block.sync
                def _(sp):
                    def load(g, place):
                        t_, kind = PLACES[place % 4]
                        g = g + place // 4
                        at_least(sp, "lo", 4 * g + place % 4 - 1)
                        sp.dma_start(W[place % 2][:, :, :], a["w_up"][layer][ds(kind * FT + 2 * g + t_, 1)]
                                     .rearrange("o p (k n) -> (o p) k n", k=KT)).then_inc(s[f"w{place % 2}"], 16)

                    def group(g, before, after):
                        for place in (1, 2, 3, 4):
                            if place == 3:
                                at_least(sp, "dlo", g)
                                sp.dma_start(WD[:, :, :], a["w_down"][layer][ds(g, 1)]
                                             .rearrange("o p k n -> (o p) k n")).then_inc(s["wd"], 16)
                            if place < 4 or after:
                                load(g, place)
                    sp.dma_start(cw[:, :, :], a["conv"][layer].rearrange("p (k n) -> p k n", n=4)).then_inc(s["cw"], 16)
                    load(0, 0)
                    groups(sp, group, lambda: None)

                @block.tensor
                def _(pe):
                    def three(bank, cs, wh, wl, xh, xl, first, final):
                        for w_, x_, f_, l_ in ((wh, xh, first, False), (wh, xl, False, False), (wl, xh, False, final)):
                            for c, (lo, hi) in enumerate(cs):
                                mm = pe.matmul(ps(bank + c, hi - lo), w_, x_[:, lo:hi], start=f_, stop=l_)
                        return mm

                    def up(g, place):
                        t_, kind = PLACES[place]
                        q = 4 * g + place
                        pe.wait_ge(s["hi"], q + 1)
                        pe.wait_ge(s["lo"], q + 1)
                        at_least(pe, "conv", q - 1)
                        for k in range(KT):
                            mm = three(UPB[kind], chunks, Wh[place % 2][:, k, :], Wl[place % 2][:, k, :], uh[:, k, :], ul[:, k, :],
                                       k == 0, k == KT - 1)
                        mm.then_inc(s["up"], 1)

                    def down(g):
                        pe.wait_ge(s["dhi"], g + 1)
                        pe.wait_ge(s["dlo"], g + 1)
                        pe.wait_ge(s["gh"], 2 * g + 2)
                        pe.wait_ge(s["gl"], 2 * g + 2)
                        for r, (m, c) in enumerate(outs):
                            at_least(pe, "acc", NO * g + max(r - 1, 0))
                            for k in range(2):
                                mm = three(DNB[r % 2], chunks[c:c + 1], WDh[:, k, m * P:(m + 1) * P], WDl[:, k, m * P:(m + 1) * P],
                                           gh[:, k, :], gl[:, k, :], k == 0, k == 1)
                            mm.then_inc(s["y"], 1)

                    def group(g, before, after):
                        up(g, 0)
                        if before:
                            down(g - 1)
                        for place in (1, 2, 3):
                            up(g, place)
                    groups(pe, group, lambda: down(NG - 1))

                @block.scalar
                def _(act):
                    def high(g, place):
                        g, place = g + place // 4, place % 4
                        q = 4 * g + place
                        act.wait_ge(s[f"w{place % 2}"], 16 * (2 * g + place // 2 + 1))
                        at_least(act, "up", q - 1)
                        act.activation(Wh[place % 2][:, :, :], W[place % 2][:, :, :], ACT.Copy).then_inc(s["hi"], 1)

                    def centre(g, place):
                        t_, kind = PLACES[place]
                        q = 4 * g + place
                        act.wait_ge(s["up"], q + 1)
                        at_least(act, "silu" if kind == 0 else "mul", 2 * g + t_)
                        f = kind * FT + 2 * g + t_
                        act.activation((cg, cv)[kind][:, :], psv(UPB[kind]), ACT.Identity,
                                       scale=cw[:, ds(f, 1), 1], bias=cw[:, ds(f, 1), 3]).then_inc(s["cen"], 1)

                    def silu(g, t_):
                        act.wait_ge(s["conv"], 4 * g + 2 * t_ + 1)
                        at_least(act, "mul", 2 * g + t_)
                        act.activation(sg[:, :], cg[:, :], ACT.Silu).then_inc(s["silu"], 1)

                    def gated_high(g, t_):
                        act.wait_ge(s["mul"], 2 * g + t_ + 1)
                        at_least(act, "y", NO * g)
                        act.activation(gh[:, t_, :], gp[:, :], ACT.Copy).then_inc(s["gh"], 1)

                    def down_high(g):
                        act.wait_ge(s["wd"], 16 * (g + 1))
                        at_least(act, "y", NO * g)
                        act.activation(WDh[:, :, :], WD[:, :, :], ACT.Copy).then_inc(s["dhi"], 1)

                    def group(g, before, after):
                        high(g, 1)
                        centre(g, 0)
                        silu(g, 0)
                        high(g, 2)
                        centre(g, 1)
                        gated_high(g, 0)
                        high(g, 3)
                        down_high(g)
                        centre(g, 2)
                        silu(g, 1)
                        if after:
                            high(g, 4)
                        centre(g, 3)
                        gated_high(g, 1)
                    act.preload_act_table_set("silu_and_others")
                    act.wait_ge(s["cw"], 16)
                    high(0, 0)
                    groups(act, group, lambda: None)

                @block.vector
                def _(dve):
                    def low(g, place):
                        g, place = g + place // 4, place % 4
                        dve.wait_ge(s["hi"], 4 * g + place + 1)
                        dve.tensor_tensor(Wl[place % 2][:, :, :], W[place % 2][:, :, :],
                                          Wh[place % 2][:, :, :].bitcast(F32), ALU.subtract).then_inc(s["lo"], 1)

                    def sides(g, place):
                        t_, kind = PLACES[place]
                        q = 4 * g + place
                        x = (cg, cv)[kind]
                        h = psv(UPB[kind])
                        f = kind * FT + 2 * g + t_
                        dve.wait_ge(s["cen"], q + 1)
                        for lo, hi, _ in streams:
                            op = dve.scalar_tensor_tensor(out=x[:, lo + 1:hi], in0=h[:, lo:hi - 1],
                                                          scalar=cw[:, ds(f, 1), 0], in1=x[:, lo + 1:hi],
                                                          op0=ALU.mult, op1=ALU.add)
                        op.then_inc(s["left"], 1)
                        dve.wait_ge(s["left"], q + 1)
                        for lo, hi, _ in streams:
                            op = dve.scalar_tensor_tensor(out=x[:, lo:hi - 1], in0=h[:, lo + 1:hi],
                                                          scalar=cw[:, ds(f, 1), 2], in1=x[:, lo:hi - 1],
                                                          op0=ALU.mult, op1=ALU.add)
                        op.then_inc(s["conv"], 1)

                    def product(g, t_):
                        dve.wait_ge(s["conv"], 4 * g + 2 * t_ + 2)
                        dve.wait_ge(s["silu"], 2 * g + t_ + 1)
                        at_least(dve, "gl", 2 * g + t_)
                        dve.tensor_tensor(gp[:, :], sg[:, :], cv[:, :], ALU.mult).then_inc(s["mul"], 1)
                        dve.wait_ge(s["gh"], 2 * g + t_ + 1)
                        dve.tensor_tensor(gl[:, t_, :], gp[:, :], gh[:, t_, :].bitcast(F32), ALU.subtract)\
                            .then_inc(s["gl"], 1)

                    def down_low(g):
                        dve.wait_ge(s["dhi"], g + 1)
                        dve.tensor_tensor(WDl[:, :, :], WD[:, :, :], WDh[:, :, :].bitcast(F32), ALU.subtract)\
                            .then_inc(s["dlo"], 1)

                    def add(g):
                        at_least(dve, "acc", NO * g)
                        for r, (m, c) in enumerate(outs):
                            lo, hi = chunks[c]
                            dve.wait_ge(s["y"], NO * g + r + 1)
                            dve.scalar_tensor_tensor(out=X[:, m, lo:hi], in0=ps(DNB[r % 2], hi - lo),
                                                     scalar=moda(layer, 5, m, 0 if lo < SEQ else 1), in1=X[:, m, lo:hi],
                                                     op0=ALU.mult, op1=ALU.add).then_inc(s["acc"], 1)

                    def group(g, before, after):
                        low(g, 1)
                        if before:
                            add(g - 1)
                        sides(g, 0)
                        low(g, 2)
                        sides(g, 1)
                        product(g, 0)
                        low(g, 3)
                        down_low(g)
                        sides(g, 2)
                        if after:
                            low(g, 4)
                        sides(g, 3)
                        product(g, 1)
                    dve.wait_ge(s["cw"], 16)
                    low(0, 0)
                    groups(dve, group, lambda: add(NG - 1))

        work, U, BIG = workspace("0")
        O_MIX = 0
        O_H = KT * T
        O_A = O_H + 6 * T
        MIX = big(O_MIX, KT, T)
        H = big(O_H, 6, T)

        def copy_take(dst, tokens):
            def take(dve, m, y):
                return dve.tensor_copy(dst[:, ds(m, 1), :tokens].rearrange("p o n -> p (o n)"), y)
            return take

        V0 = U[:, :, :].rearrange("p k n -> p (k n)")[:, 0:10 * A_HEADS * 65]\
            .rearrange("p (t h d) -> p t h d", t=10, h=A_HEADS)

        def latent_norms():
            sq = big(O_A, 2, T)
            lnb = big(O_A + 2 * T, T)
            wv = big(O_A + 3 * T, A_HEADS * 64)
            parts = [((0, 1), 256, W_CQG), ((2,), 128, W_CKVG)]
            with ExitStack() as c2:
                s = {n: sem("ln_" + n) for n in
                     ("w", "sq", "acc", "ln", "rinv", "u", "v", "vc", "one")}
                block = c2.enter_context(nc.Block())

                @block.sync
                def _(sp):
                    sp.dma_start(wv, a["w_v0"]).then_inc(s["w"], 16)

                @block.gpsimd
                def _(pool):
                    pool.memset(V0[:, :, :, 64], 1.0).then_inc(s["one"], 1)

                @block.scalar
                def _(act):
                    act.preload_act_table_set("natural_log_exp_and_others")
                    n = 0
                    for i, (tiles, width, _) in enumerate(parts):
                        for t_ in tiles:
                            if n >= 2:
                                act.wait_ge(s["acc"], n - 1)
                            act.activation(sq[:, n % 2, :], H[:, t_, :], ACT.Square).then_inc(s["sq"], 1)
                            n += 1
                        act.wait_ge(s["acc"], n)
                        if i:
                            act.wait_ge(s["rinv"], 1)
                        act.activation(lnb, PS[:, 3 * i * BANK:3 * i * BANK + T], ACT.Ln, bias=eps[:, 0:1],
                                       scale=1.0 / width).then_inc(s["ln"], 1)
                        act.wait_ge(s["ln"], i + 1)
                        act.activation(PS[:, 3 * i * BANK:3 * i * BANK + T], lnb, ACT.Exp, scale=-0.5)\
                            .then_inc(s["rinv"], 1)
                    for t_ in range(10):
                        act.wait_ge(s["v"], t_ + 1)
                        for h in range(2):
                            op = act.activation(
                                V0[:, t_, 6 * h:6 * h + 6, 0:64],
                                ps(2 * (t_ % 2) + h, 384).rearrange("p (h d) -> p h d", h=6), ACT.Copy)
                        op.then_inc(s["vc"], 1)

                @block.tensor
                def _(pe):
                    n = 0
                    for i, (tiles, _, _) in enumerate(parts):
                        for t_ in tiles:
                            pe.wait_ge(s["sq"], n + 1)
                            for c, (lo, hi) in enumerate(CH):
                                mm = pe.matmul(ps(3 * i + c, hi - lo), ones, sq[:, n % 2, lo:hi],
                                               start=(t_ == tiles[0]), stop=(t_ == tiles[-1]))
                            mm.then_inc(s["acc"], 1)
                            n += 1
                    pe.wait_ge(s["w"], 16)
                    pe.wait_ge(s["u"], 3)
                    for t_ in range(10):
                        if t_ >= 2:
                            pe.wait_ge(s["vc"], t_ - 1)
                        for h in range(2):
                            mm = pe.matmul(ps(2 * (t_ % 2) + h, 384), H[:, 2, t_ * P:(t_ + 1) * P],
                                           wv[:, 384 * h:384 * h + 384], start=True, stop=True)
                        mm.then_inc(s["v"], 1)

                @block.vector
                def _(dve):
                    for i, (tiles, _, g) in enumerate(parts):
                        dve.wait_ge(s["rinv"], i + 1)
                        for t_ in tiles:
                            dve.scalar_tensor_tensor(out=H[:, t_, :], in0=H[:, t_, :],
                                                     scalar=sml[:, g + t_ % 2:g + t_ % 2 + 1],
                                                     in1=PS[:, 3 * i * BANK:3 * i * BANK + T],
                                                     op0=ALU.mult, op1=ALU.mult).then_inc(s["u"], 1)

        def fourier():
            FW = big(O_A, 2, 2 * P)
            AB = big(O_A + 512, 10, 4 * P)
            DF = [big(O_A + 512 + 5120 + b * 2048, 2, SEQ) for b in range(2)]
            DC = big(O_A + 512 + 5120 + 4096, 2, 2, CTX)
            with ExitStack() as c2:
                s = {n: sem("ff_" + n) for n in
                     ("d0", "d1", "dc", "fw", "fwc", "ab", "abc", "l", "y", "yc")}
                block = c2.enter_context(nc.Block())

                @block.sync
                def _(sp):
                    sp.dma_start(DC, a["dftc"].rearrange("t p s n -> p t s n")).then_inc(s["dc"], 16)
                    for t_ in range(8):
                        if t_ >= 2:
                            sp.wait_ge(s["l"], t_ - 1)
                        sp.dma_start(DF[t_ % 2], a["dft"][t_]).then_inc(s[f"d{t_ % 2}"], 16)

                @block.tensor
                def _(pe):
                    for p in range(2):
                        for n, col in enumerate((C_COSC, C_SINC)):
                            mm = pe.matmul(ps(p, 2 * P)[:, n * P:(n + 1) * P], cst[:, col:col + P],
                                           sml[:, W_FN + p * P:W_FN + (p + 1) * P], start=True, stop=True)
                    mm.then_inc(s["fw"], 1)
                    pe.wait_ge(s["fwc"], 1)
                    for t_ in range(10):
                        if t_ >= 2:
                            pe.wait_ge(s["abc"], t_ - 1)
                        for p in range(2):
                            mm = pe.matmul(ps(2 + t_ % 2, 4 * P)[:, 2 * P * p:2 * P * (p + 1)],
                                           H[:, 4 + p, t_ * P:(t_ + 1) * P], FW[:, p, :], start=True, stop=True)
                        mm.then_inc(s["ab"], 1)
                    pe.wait_ge(s["abc"], 10)
                    for t_ in range(8):
                        pe.wait_ge(s[f"d{t_ % 2}"], 16 * (t_ // 2 + 1))
                        for p in range(2):
                            for n in range(2):
                                for c in range(2):
                                    mm = pe.matmul(ps(4 + 2 * p + c, BANK),
                                                   AB[:, t_, (2 * p + n) * P:(2 * p + n + 1) * P],
                                                   DF[t_ % 2][:, n, c * BANK:(c + 1) * BANK],
                                                   start=(t_ == 0 and n == 0), stop=(t_ == 7 and n == 1))
                        mm.then_inc(s["l"], 1)
                    pe.wait_ge(s["dc"], 16)
                    for p in range(2):
                        for t_ in range(2):
                            for n in range(2):
                                mm = pe.matmul(ps(p, CTX), AB[:, 8 + t_, (2 * p + n) * P:(2 * p + n + 1) * P],
                                               DC[:, t_, n, :], start=(t_ == 0 and n == 0),
                                               stop=(t_ == 1 and n == 1))
                    mm.then_inc(s["y"], 1)

                @block.vector
                def _(dve):
                    dve.wait_ge(s["fw"], 1)
                    dve.tensor_copy(FW, PS[:, 0:2 * BANK].rearrange("p (x y) -> p x y", x=2)[:, :, 0:2 * P])\
                        .then_inc(s["fwc"], 1)
                    for t_ in range(10):
                        dve.wait_ge(s["ab"], t_ + 1)
                        dve.tensor_copy(AB[:, t_, :], ps(2 + t_ % 2, BANK)).then_inc(s["abc"], 1)
                    dve.wait_ge(s["l"], 8)
                    for p in range(2):
                        dve.tensor_copy(MIX[:, 6 + p, 0:SEQ], PS[:, (4 + 2 * p) * BANK:(6 + 2 * p) * BANK])\
                            .then_inc(s["yc"], 1)
                    dve.wait_ge(s["y"], 1)
                    for p in range(2):
                        dve.tensor_copy(MIX[:, 6 + p, SEQ:T], ps(p, CTX)).then_inc(s["yc"], 1)

        def heads0():
            o = O_A

            def take(*shape):
                nonlocal o
                v = big(o, *shape)
                o += int(np.prod(shape))
                return v
            qa = [take(T) for _ in range(2)]
            ka = [take(T) for _ in range(2)]
            vs = [take(10, 65) for _ in range(2)]
            wq = [take(256) for _ in range(2)]
            pr = [take(BANK) for _ in range(2)]
            raw = [take(BANK) for _ in range(2)]
            sq = [take(BANK) for _ in range(2)]
            kx = take(T)
            sk = take(T)
            t1 = take(BANK)
            lnb = take(BANK)
            mc = take(26)
            mcb = take(6).bitcast(BF16)
            o65 = take(T)
            rope = H[:, 4:6, :]
            lnr = H[:, 3, :]
            Uf = U[:, :, :].rearrange("p k n -> p (k n)")
            qb = Uf[:, 7800:7800 + T // 2].bitcast(BF16)
            kb = Uf[:, 7800 + T // 2:7800 + T].bitcast(BF16)
            NU = 22
            units = [(kt, c) for kt in range(10) for c in (0, 1)] + [(8, 2), (9, 2)]
            NM = 26
            LAST = A_HEADS - 1
            RB, NB, TB = 5, 6, 7
            with ExitStack() as c2:
                s = {n: sem("h0_" + n) for n in
                     ("tab", "w0", "w1", "one", "zero", "kr", "krc", "krt", "krm", "krp", "krs", "S", "P", "PV", "raw", "rawc",
                      "sq", "nt", "ln", "rinv", "t1", "ts", "ta", "out", "cast", "vs", "mx", "mc", "mn", "mrow",
                      "mr", "o", "bc", "lnr", "rs", "fin")}
                block = c2.enter_context(nc.Block())

                def at_least(eng, name, value):
                    if not (isinstance(value, int) and value <= 0):
                        eng.wait_ge(s[name], value)

                def step_of(u):
                    if 3 <= u <= 9:
                        return "prep", u - 3
                    if 10 <= u <= 18:
                        return "max", u - 10
                    if u == 19:
                        return "row", 0
                    return None, 0

                @block.sync
                def _(sp):
                    sp.dma_start(rope[0:A_QK], a["rope0"]).then_inc(s["tab"], 16)

                    def load(p, b):
                        sp.dma_start(wq[b], a["wqk0"][ds(p, 1)].rearrange("o p n -> (o p) n")).then_inc(s[f"w{b}"], 16)
                    load(0, 0)
                    load(1, 1)
                    with sp.Fori(0, 5) as i:
                        sp.wait_ge(s["raw"], 12 * i + 6)
                        load(2 * i + 2, 0)
                        sp.wait_ge(s["raw"], 12 * i + 12)
                        load(2 * i + 3, 1)

                @block.gpsimd
                def _(pool):
                    pool.memset(sk[0:64, :], 0.0).then_inc(s["zero"], 1)
                    pool.wait_ge(s["zero"], 1)
                    for b in range(2):
                        pool.memset(ka[b][96:97, :], 1.0).then_inc(s["one"], 1)
                    pool.wait_ge(s["one"], 2)
                    for p in range(A_HEADS):
                        b = p % 2
                        at_least(pool, "cast", 6 * p)
                        at_least(pool, "PV", NU * (p - 1))
                        pool.tensor_copy(vs[b], V0[:, :, p, :]).then_inc(s["vs"], 1)
                        at_least(pool, "mx", NM * p)
                        for w in range(6):
                            lo, hi = CH[w % 3]
                            src, dst = (ka[b], kb) if w < 3 else (qa[b], qb)
                            pool.wait_ge(s["out"], 6 * p + w + 1)
                            if w == 0:
                                pool.wait_ge(s["vs"], p + 1)
                            pool.tensor_copy(dst[0:A_QK, lo:hi], src[0:A_QK, lo:hi]).then_inc(s["cast"], 1)

                @block.tensor
                def _(pe):
                    def qk(h, b, u):
                        kt, c = units[u]
                        lo, hi = CH[c]
                        at_least(pe, "P", NU * h + u - 1)
                        if u == 0:
                            pe.wait_ge(s["mr"], h + 1)
                        pe.matmul(ps(u % 2, hi - lo), ka[b][0:97, kt * P:(kt + 1) * P], qa[b][0:97, lo:hi],
                                  start=True, stop=True).then_inc(s["S"], 1)

                    def pv(h, b, u):
                        kt, c = units[u]
                        lo, hi = CH[c]
                        pe.wait_ge(s["P"], NU * h + u + 1)
                        if u == 0:
                            pe.wait_ge(s["vs"], h + 1)
                        if u in (0, 1, 20):
                            at_least(pe, "o", 3 * h - 2 + c)
                        pe.matmul(ps(2 + c, hi - lo, slice(0, 65)), vs[b][:, kt, :], pr[u % 2][:, :hi - lo],
                                  start=(kt == (8 if c == 2 else 0)), stop=(kt == 9)).then_inc(s["PV"], 1)

                    def spread(h):
                        pe.wait_ge(s["o"], 3 * h + 3)
                        for n, (lo, hi) in enumerate(CH):
                            mm = pe.matmul(ps(RB + n, hi - lo, slice(0, 64)), cst[0:65, C_SEL:C_SEL + 64],
                                           o65[0:65, lo:hi], start=True, stop=True)
                        mm.then_inc(s["bc"], 1)

                    def project(p, b, use, w):
                        lo, hi = CH[w % 3]
                        if w == 0:
                            pe.wait_ge(s[f"w{b}"], 16 * use + 16)
                            at_least(pe, "fin", p - 1)
                        at_least(pe, "sq", 6 * p + w)
                        if w < 3:
                            mm = pe.matmul(ps(RB, hi - lo, slice(0, 64)), wq[b][:, 192:256], H[:, 2, lo:hi],
                                           start=True, stop=True)
                        else:
                            for k in range(2):
                                mm = pe.matmul(ps(RB, hi - lo, slice(0, A_QK)), wq[b][:, 96 * k:96 * k + 96],
                                               H[:, k, lo:hi], start=(k == 0), stop=(k == 1))
                        mm.then_inc(s["raw"], 1)

                    def squares(p, w):
                        lo, hi = CH[w % 3]
                        pe.wait_ge(s["sq"], 6 * p + w + 1)
                        at_least(pe, "out", 6 * p + w)
                        src = sk[0:A_QK, lo:hi] if w < 3 else sq[w % 2][0:A_QK, :hi - lo]
                        mm = pe.matmul(ps(NB, hi - lo, slice(0, A_QK)), ones[0:A_QK, 0:A_QK], src,
                                       start=True, stop=True)
                        if 3 <= w < 5:
                            mm = pe.matmul(ps(TB, hi - lo, slice(0, A_QK)), rot0[:, 0, :],
                                           raw[w % 2][0:A_QK, :hi - lo], start=True, stop=True)
                        mm.then_inc(s["nt"], 1)

                    def step(kind, n, p, b, use):
                        if kind == "prep":
                            if n < 6:
                                project(p, b, use, n)
                            if n:
                                squares(p, n - 1)
                        if kind == "max" and n < 8:
                            if n == 0:
                                pe.wait_ge(s["cast"], 6 * p + 6)
                            for c, (lo, hi) in enumerate(CH):
                                at_least(pe, "mc", NM * p + max(3 * n + c - 2, 0))
                                pe.matmul(ps(RB + c, hi - lo), qb[0:A_QK, n * P:(n + 1) * P],
                                          kb[0:A_QK, lo:hi], start=True, stop=True).then_inc(s["mx"], 1)
                        if kind == "max" and n == 8:
                            for c in range(2):
                                pe.wait_ge(s["mc"], NM * p + 3 * n + c - 2)
                                pe.matmul(ps(RB + c, CTX), qb[0:A_QK, SEQ + c * P:SEQ + (c + 1) * P],
                                          kb[0:A_QK, SEQ:T], start=True, stop=True).then_inc(s["mx"], 1)
                        if kind == "row":
                            pe.wait_ge(s["mn"], p + 1)
                            for n in range(10):
                                mm = pe.matmul(ps(RB + n // 4, BANK, slice(96, 97))[:, (n % 4) * P:(n % 4 + 1) * P],
                                               mcb[:, n:n + 1], identb[:, :], start=True, stop=True)
                            mm.then_inc(s["mrow"], 1)

                    def head(h, b, use, prep, before):
                        for u in range(NU):
                            if u + 1 < NU:
                                qk(h, b, u + 1)
                            elif prep:
                                qk(h + 1, 1 - b, 0)
                            if u == 1 and before:
                                spread(h - 1)
                            if prep:
                                step(*step_of(u), h + 1, 1 - b, use)
                            pv(h, b, u)

                    pe.wait_ge(s["tab"], 16)
                    pe.wait_ge(s["one"], 2)
                    for c, (lo, hi) in enumerate(CH):
                        pe.wait_ge(s["kr"], 1)
                        pe.wait_ge(s["zero"], 1)
                        mm = pe.matmul(ps(RB + c, hi - lo, slice(0, A_QK)), rot0[:, 1, :], sk[0:A_QK, lo:hi],
                                       start=True, stop=True)
                    mm.then_inc(s["krm"], 1)
                    pe.wait_ge(s["krc"], 1)
                    pe.wait_ge(s["krs"], 1)
                    for u in range(NU):
                        step(*step_of(u), 0, 0, 0)
                    qk(0, 0, 0)
                    head(0, 0, 0, True, False)
                    with pe.Fori(0, 5) as i:
                        head(2 * i + 1, 1, i + 1, True, True)
                        head(2 * i + 2, 0, i + 1, True, True)
                    head(LAST, 1, 0, False, True)
                    spread(LAST)

                @block.scalar
                def _(act):
                    def project(p, w):
                        lo, hi = CH[w % 3]
                        n = hi - lo
                        act.wait_ge(s["raw"], 6 * p + w + 1)
                        if w < 3:
                            at_least(act, "out", 6 * p)
                            act.activation(kx[0:64, lo:hi], ps(RB, n, slice(0, 64)), ACT.Copy,
                                           scale=sml[0:64, W_G0 + 1:W_G0 + 2]).then_inc(s["rawc"], 1)
                            act.activation(sk[0:64, lo:hi], ps(RB, n, slice(0, 64)), ACT.Square).then_inc(s["sq"], 1)
                        else:
                            at_least(act, "nt", 6 * p + w - 1)
                            if w == 3:
                                at_least(act, "out", 6 * p)
                            if w == 5:
                                act.wait_ge(s["t1"], 2 * p + 1)
                            act.activation(raw[w % 2][0:96, :n], ps(RB, n, slice(0, 96)), ACT.Copy)\
                                .then_inc(s["rawc"], 1)
                            act.activation(sq[w % 2][0:96, :n], ps(RB, n, slice(0, 96)), ACT.Square)\
                                .then_inc(s["sq"], 1)

                    def inverse(p, w):
                        lo, hi = CH[w % 3]
                        n = hi - lo
                        act.wait_ge(s["nt"], 6 * p + w + 1)
                        at_least(act, "rinv", 6 * p + w)
                        act.activation(lnb[0:96, :n], ps(NB, n, slice(0, 96)), ACT.Ln, bias=eps[0:96, 0:1],
                                       scale=1.0 / A_QK).then_inc(s["ln"], 1)
                        act.wait_ge(s["ln"], 6 * p + w + 1)
                        act.activation(ps(NB, n, slice(0, 96)), lnb[0:96, :n], ACT.Exp, scale=-0.5)\
                            .then_inc(s["rinv"], 1)

                    def step(kind, n, p, b):
                        if kind == "prep":
                            if n < 6:
                                project(p, n)
                            if n:
                                inverse(p, n - 1)
                        if kind == "row":
                            act.wait_ge(s["mrow"], p + 1)
                            act.activation(qa[b][96:97, :], PS[96:97, RB * BANK:RB * BANK + T], ACT.Copy)\
                                .then_inc(s["mr"], 1)

                    def exps(h, u):
                        lo, hi = CH[units[u][1]]
                        act.wait_ge(s["S"], NU * h + u + 1)
                        at_least(act, "PV", NU * h + u - 1)
                        act.activation(pr[u % 2][:, :hi - lo], ps(u % 2, hi - lo), ACT.Exp, scale=A_SCALE)\
                            .then_inc(s["P"], 1)

                    def inverse_sum(h):
                        act.wait_ge(s["bc"], h + 1)
                        at_least(act, "rs", h)
                        r = PS[0:64, RB * BANK:RB * BANK + T]
                        act.activation(lnr[0:64, :], r, ACT.Ln).then_inc(s["lnr"], 1)
                        act.wait_ge(s["lnr"], h + 1)
                        act.activation(r, lnr[0:64, :], ACT.Exp, scale=-1.0).then_inc(s["rs"], 1)

                    def head(h, b, prep, before):
                        for u in range(NU):
                            if u + 1 < NU:
                                exps(h, u + 1)
                            elif prep:
                                exps(h + 1, 0)
                            if u == 1 and before:
                                inverse_sum(h - 1)
                            if prep:
                                step(*step_of(u), h + 1, 1 - b)
                        act.wait_ge(s["PV"], NU * h + NU)
                        at_least(act, "fin", h)
                        for c, (lo, hi) in enumerate(CH):
                            act.activation(o65[0:65, lo:hi], ps(2 + c, hi - lo, slice(0, 65)), ACT.Copy)\
                                .then_inc(s["o"], 1)

                    act.wait_ge(s["zero"], 1)
                    act.activation(sk[64:96, :], H[0:32, 3, :], ACT.Copy).then_inc(s["kr"], 1)
                    act.wait_ge(s["krm"], 1)
                    act.wait_ge(s["krt"], 1)
                    act.activation(sk[64:96, :], H[0:32, 3, :], ACT.Square).then_inc(s["krs"], 1)
                    act.wait_ge(s["krs"], 1)
                    for u in range(NU):
                        step(*step_of(u), 0, 0)
                    exps(0, 0)
                    head(0, 0, True, False)
                    with act.Fori(0, 5) as i:
                        head(2 * i + 1, 1, True, True)
                        head(2 * i + 2, 0, True, True)
                    head(LAST, 1, False, True)
                    inverse_sum(LAST)

                @block.vector
                def _(dve):
                    def finish(h, tile, half):
                        dve.wait_ge(s["rs"], h + 1)
                        dve.tensor_tensor(MIX[64 * half:64 * half + 64, ds(tile, 1), :].rearrange("p o n -> p (o n)"),
                                          o65[0:64, :], PS[0:64, RB * BANK:RB * BANK + T], ALU.mult)\
                            .then_inc(s["fin"], 1)

                    def unit(p, b, w):
                        lo, hi = CH[w % 3]
                        n = hi - lo
                        g = sml[0:96, W_G0:W_G0 + 1]
                        norm_ = ps(NB, n, slice(0, 96))
                        if w < 3:
                            dve.wait_ge(s["rinv"], 6 * p + w + 1)
                            dve.tensor_tensor(ka[b][0:96, lo:hi], kx[0:96, lo:hi], norm_, ALU.mult)\
                                .then_inc(s["out"], 1)
                            return
                        x = raw[w % 2][0:96, :n]
                        if w == 5:
                            dve.wait_ge(s["rinv"], 6 * p + w + 1)
                            dve.scalar_tensor_tensor(out=qa[b][0:96, lo:hi], in0=x, scalar=g, in1=norm_,
                                                     op0=ALU.mult, op1=ALU.mult).then_inc(s["out"], 1)
                            return
                        v = 2 * p + w - 3
                        dve.wait_ge(s["sq"], 6 * p + w + 1)
                        at_least(dve, "out", 6 * p + w)
                        dve.scalar_tensor_tensor(out=t1[0:96, :n], in0=x, scalar=g,
                                                 in1=rope[0:96, 0, lo:hi], op0=ALU.mult, op1=ALU.mult)\
                            .then_inc(s["t1"], 1)
                        dve.wait_ge(s["nt"], 6 * p + w + 1)
                        T_ = ps(TB, n, slice(0, 96))
                        dve.tensor_tensor(T_, T_, rope[0:96, 1, lo:hi], ALU.mult).then_inc(s["ts"], 1)
                        dve.wait_ge(s["ts"], v + 1)
                        dve.tensor_tensor(t1[0:96, :n], t1[0:96, :n], T_, ALU.add).then_inc(s["ta"], 1)
                        dve.wait_ge(s["ta"], v + 1)
                        dve.wait_ge(s["rinv"], 6 * p + w + 1)
                        dve.tensor_tensor(qa[b][0:96, lo:hi], t1[0:96, :n], norm_, ALU.mult).then_inc(s["out"], 1)

                    def step(kind, n, p, b):
                        if kind == "prep" and n:
                            unit(p, b, n - 1)
                        if kind == "max":
                            for c, (lo, hi) in enumerate(CH if n < 8 else CH[2:] * 2):
                                r = 3 * n + c
                                dve.wait_ge(s["mx"], NM * p + r + 1)
                                if r == 0:
                                    at_least(dve, "mn", p)
                                dve.reduce_max(mc[:, r:r + 1], ps(RB + c, hi - lo), AX_X).then_inc(s["mc"], 1)
                        if kind == "row":
                            dve.wait_ge(s["mc"], NM * p + NM)
                            at_least(dve, "mrow", p)
                            dve.tensor_reduce(mcb[:, 0:8], mc[:, 0:24].rearrange("p (x y) -> p x y", y=3), AX_X,
                                              ALU.max, negate=True)
                            dve.tensor_scalar(mcb[:, 8:10], mc[:, 24:26], -1.0, None, ALU.mult).then_inc(s["mn"], 1)

                    dve.wait_ge(s["tab"], 16)
                    dve.wait_ge(s["kr"], 1)
                    dve.scalar_tensor_tensor(out=kx[64:96, :], in0=sk[64:96, :], scalar=sml[64:96, W_G0 + 1:W_G0 + 2],
                                             in1=rope[64:96, 0, :], op0=ALU.mult, op1=ALU.mult).then_inc(s["krt"], 1)
                    dve.wait_ge(s["krm"], 1)
                    T_ = PS[64:96, RB * BANK:RB * BANK + T]
                    dve.tensor_tensor(T_, T_, rope[64:96, 1, :], ALU.mult).then_inc(s["krp"], 1)
                    dve.wait_ge(s["krt"], 1)
                    dve.wait_ge(s["krp"], 1)
                    dve.tensor_tensor(kx[64:96, :], kx[64:96, :], T_, ALU.add).then_inc(s["krc"], 1)
                    dve.wait_ge(s["krc"], 1)
                    for u in range(NU):
                        step(*step_of(u), 0, 0)
                    for u in range(NU):
                        step(*step_of(u), 1, 1)
                    with dve.Fori(0, 5) as i:
                        finish(2 * i, i, 0)
                        for u in range(NU):
                            step(*step_of(u), 2 * i + 2, 0)
                        finish(2 * i + 1, i, 1)
                        for u in range(NU):
                            step(*step_of(u), 2 * i + 3, 1)
                    finish(10, 5, 0)
                    finish(LAST, 5, 1)

        mods()
        norm(0, 0, T)
        linear("in0_", a["w_in0"], U, KT, 6, T, O_A, copy_take(H, T))
        latent_norms()
        fourier()
        heads0()
        recycle()
        linear("out0_", a["w_out0"], MIX, KT, KT, T, O_A, residual(0, 2, T))
        work.close()
        ffn(0, T)
        recycle()

        work, U, BIG = workspace("1")
        MIX1 = big(0, KT, SEQ)
        O_V1 = KT * SEQ
        V1 = big(O_V1, 10, C_KV, 65)
        O_B = O_V1 + 10 * C_KV * 65

        def values1():
            wv = big(O_B, KT, 256)
            with ExitStack() as c2:
                s = {n: sem("v1_" + n) for n in ("w", "v", "vc", "one")}
                block = c2.enter_context(nc.Block())

                @block.sync
                def _(sp):
                    sp.dma_start(wv, a["w_v1"]).then_inc(s["w"], 16)

                @block.gpsimd
                def _(pool):
                    pool.memset(V1[:, :, :, 64], 1.0).then_inc(s["one"], 1)

                @block.tensor
                def _(pe):
                    pe.wait_ge(s["w"], 16)
                    for t_ in range(10):
                        if t_ >= 2:
                            pe.wait_ge(s["vc"], t_ - 1)
                        for k in range(KT):
                            mm = pe.matmul(ps(t_ % 2, 256), U[:, k, t_ * P:(t_ + 1) * P], wv[:, k, :],
                                           start=(k == 0), stop=(k == KT - 1))
                        mm.then_inc(s["v"], 1)

                @block.vector
                def _(dve):
                    for t_ in range(10):
                        dve.wait_ge(s["v"], t_ + 1)
                        dve.tensor_copy(V1[:, t_, :, 0:64], ps(t_ % 2, 256).rearrange("p (h d) -> p h d", h=C_KV))\
                            .then_inc(s["vc"], 1)

        PAD = 8
        ZW = SEQ + 2 * PAD
        Z = big(O_B + 2048, 2, ZW)

        def pool_take(dve, m, y):
            return dve.tensor_copy(Z[:, ds(m, 1), PAD:PAD + SEQ].rearrange("p o n -> p (o n)"), y)

        def pooling():
            o = O_B + 2048 + 2 * ZW
            Wd = [big(o + n * ZW, ZW) for n in range(3)]
            Pm = big(o + 3 * ZW, 2, SEQ)
            inv = big(o + 3 * ZW + 2 * SEQ, 2, SEQ)
            with ExitStack() as c2:
                s = {n: sem("po_" + n) for n in ("inv", "pad", "d", "mm", "out")}
                block = c2.enter_context(nc.Block())

                @block.sync
                def _(sp):
                    sp.dma_start(inv, a["pool_inv"]).then_inc(s["inv"], 16)

                @block.vector
                def _(dve):
                    n = 0

                    def chained(op):
                        nonlocal n
                        n += 1
                        op.then_inc(s["d"], 1)
                        dve.wait_ge(s["d"], n)

                    for t_ in range(2):
                        for e in (0, PAD + SEQ):
                            chained(dve.memset(Z[:, t_, e:e + PAD], 0.0))
                    dve.wait_ge(s["inv"], 16)
                    for t_ in range(2):
                        z = Z[:, t_, :]
                        chained(dve.tensor_tensor(Wd[0][:, 1:ZW], z[:, 0:ZW - 1], z[:, 1:ZW], ALU.add))
                        chained(dve.tensor_tensor(Wd[1][:, 2:ZW - 1], Wd[0][:, 1:ZW - 2], Wd[0][:, 3:ZW], ALU.add))
                        lo, hi = Wd[0], Wd[1]
                        if t_ == 1:
                            chained(dve.tensor_tensor(Wd[2][:, 4:ZW - 3], Wd[1][:, 2:ZW - 5], Wd[1][:, 6:ZW - 1],
                                                      ALU.add))
                            chained(dve.tensor_tensor(Wd[0][:, PAD:PAD + SEQ], Wd[2][:, PAD - 4:PAD + SEQ - 4],
                                                      Wd[2][:, PAD + 4:PAD + SEQ + 4], ALU.add))
                            lo, hi = Wd[2], Wd[0]
                        for r, src in ((0, lo), (64, hi)):
                            chained(dve.tensor_tensor(Pm[r:r + 64, t_, :], src[r:r + 64, PAD:PAD + SEQ],
                                                      inv[r:r + 64, t_, :], ALU.mult))
                        chained(dve.tensor_tensor(Pm[:, t_, :], Pm[:, t_, :], z[:, PAD:PAD + SEQ], ALU.subtract))
                    for t_ in range(2):
                        dve.wait_ge(s["mm"], t_ + 1)
                        dve.tensor_scalar(MIX1[:, 6 + t_, :], PS[:, 2 * t_ * BANK:(2 * t_ + 2) * BANK],
                                          sml[:, W_PS + t_:W_PS + t_ + 1], None, ALU.mult).then_inc(s["out"], 1)

                @block.tensor
                def _(pe):
                    pe.wait_ge(s["d"], 4 + 5 + 7)
                    for t_ in range(2):
                        for c in range(2):
                            mm = pe.matmul(ps(2 * t_ + c, BANK), sml[:, W_PW + t_ * P:W_PW + (t_ + 1) * P],
                                           Pm[:, t_, c * BANK:(c + 1) * BANK], start=True, stop=True)
                        mm.then_inc(s["mm"], 1)

        def heads1():
            o = O_B

            def take(*shape):
                nonlocal o
                v = big(o, *shape)
                o += int(np.prod(shape))
                return v
            qa = [[take(SEQ) for _ in range(C_GROUP)] for _ in range(2)]
            ka = [take(T) for _ in range(2)]
            wt = [take(KT, P) for _ in range(2)]
            pr = [take(BANK) for _ in range(2)]
            raw = [take(BANK) for _ in range(2)]
            sq = [take(BANK) for _ in range(2)]
            t1 = take(BANK)
            lnb = take(BANK)
            rope = take(2, T)
            qb = [take(SEQ // 2).bitcast(BF16) for _ in range(C_GROUP)]
            kb = take(T // 2).bitcast(BF16)
            mc = take(C_GROUP * 8)
            mcb = take(C_GROUP * 4).bitcast(BF16)
            s8 = take(C_HEADS)
            o97 = take(SEQ)
            lnr = take(SEQ)
            RB, NB, TB = 5, 6, 7
            WIN = [(max(t - 1, 0), min(t + 2, 8)) for t in range(8)]
            units = [(8, 0, 4), (8, 4, 8), (9, 0, 4), (9, 4, 8)] + [(t, *WIN[t]) for t in range(8)]
            NU = len(units)
            NS = 6 + 8 * C_GROUP + C_GROUP
            places = [(j, u) for j in range(C_GROUP) for u in range(NU) if u != 2]
            assert len(places) == NS
            step_at = {pl: n for n, pl in enumerate(places)}
            prods = [(0, 0), (0, 1), (0, 2), (1, 0), (1, 1)]
            NW = len(prods)
            with ExitStack() as c2:
                s = {n: sem("h1_" + n) for n in
                     ("tab", "w0", "w1", "one", "s8", "S", "P", "PV", "raw", "rawc", "sq", "nt", "ln", "rinv",
                      "t1", "ts", "ta", "out", "cast", "mx", "mc", "mn", "mrow", "mr", "o", "es", "zero",
                      "bc", "lnr", "rs", "fin")}
                block = c2.enter_context(nc.Block())

                def at_least(eng, name, value):
                    if value > 0:
                        eng.wait_ge(s[name], value)

                def everywhere(stepper, attend, begin, end):
                    for n in range(NS):
                        stepper(n, 0)
                    for g in range(C_KV):
                        for j in range(C_GROUP):
                            for u in range(NU):
                                begin(g, j, u)
                                if g + 1 < C_KV and (j, u) in step_at:
                                    stepper(step_at[j, u], g + 1)
                                attend(g, j, u)
                            end(g, j)

                def following(g, j, u):
                    n = NU * (C_GROUP * g + j) + u + 1
                    return (n // NU // C_GROUP, n // NU % C_GROUP, n % NU) if n < NU * C_HEADS else None

                @block.sync
                def _(sp):
                    sp.dma_start(rope, a["rope1"]).then_inc(s["tab"], 16)
                    for g in range(C_KV):
                        for n in range(2):
                            at_least(sp, "raw", NW * (g - 1) + (3 if n == 0 else 5) if g else 0)
                            sp.dma_start(wt[n], a["wqk1"][2 * g + n].rearrange("p (k n) -> p k n", k=KT))\
                                .then_inc(s[f"w{n}"], 16)

                @block.gpsimd
                def _(pool):
                    pool.memset(o97[64:97, :], 0.0).then_inc(s["zero"], 1)
                    pool.wait_ge(s["zero"], 1)
                    for b in range(2):
                        pool.memset(ka[b][64:65, :], 1.0).then_inc(s["one"], 1)
                    pool.wait_ge(s["one"], 2)
                    for g in range(C_KV):
                        b = g % 2
                        at_least(pool, "mx", 8 * C_GROUP * g)
                        for w, (n, c) in enumerate(prods):
                            lo, hi = CH[c]
                            pool.wait_ge(s["out"], NW * g + w + 1)
                            if n == 0:
                                if c < 2:
                                    pool.tensor_copy(qb[2][0:64, lo:hi], qa[b][2][0:64, lo:hi])
                                op = pool.tensor_copy(kb[0:64, lo:hi], ka[b][0:64, lo:hi])
                            else:
                                pool.tensor_copy(qb[0][0:64, lo:hi], qa[b][0][0:64, lo:hi])
                                op = pool.tensor_copy(qb[1][0:64, lo:hi], qa[b][1][0:64, lo:hi])
                            op.then_inc(s["cast"], 1)

                @block.tensor
                def _(pe):
                    spreads = 0

                    def qk(g, j, u):
                        kt, q0, q1 = units[u]
                        n = (q1 - q0) * P
                        U_ = NU * (C_GROUP * g + j) + u
                        at_least(pe, "P", U_ - 1)
                        if u == 0:
                            pe.wait_ge(s["mr"], C_GROUP * g + j + 1)
                        ends = [(kt - 1 >= q0 and kt < 8, 0, 0), (kt + 1 < q1 and kt < 8, n - P, 1)]
                        last = [e for e in ends if e[0]]
                        mm = pe.matmul(ps(u % 2, n), ka[g % 2][0:65, kt * P:(kt + 1) * P],
                                       qa[g % 2][j][0:65, q0 * P:q1 * P], start=True, stop=not last)
                        for e in last:
                            mm = pe.matmul(ps(u % 2, n)[:, e[1]:e[1] + P], identb[:, :], maskb[:, e[2], :],
                                           start=False, stop=(e is last[-1]))
                        mm.then_inc(s["S"], 1)

                    def pv(g, j, u):
                        kt, q0, q1 = units[u]
                        U_ = NU * (C_GROUP * g + j) + u
                        pe.wait_ge(s["P"], U_ + 1)
                        if u < 2:
                            at_least(pe, "o", 2 * (C_GROUP * g + j) - 1 + u)
                        for c in range(2):
                            lo, hi = max(q0, 4 * c), min(q1, 4 * c + 4)
                            if lo < hi:
                                mm = pe.matmul(ps(2 + c, BANK, slice(0, 65))[:, (lo - 4 * c) * P:(hi - 4 * c) * P],
                                               V1[:, kt, g, :], pr[u % 2][:, (lo - q0) * P:(hi - q0) * P],
                                               start=(kt == 8), stop=(kt == (4 if c == 0 else 7)))
                        mm.then_inc(s["PV"], 1)

                    def spread(idx, G):
                        nonlocal spreads
                        at_least(pe, "rawc", NW * G + min(idx, NW))
                        at_least(pe, "out", NW * G + min(max(idx - 1, 0), NW))
                        at_least(pe, "mc", 8 * C_GROUP * G + min(max(idx - 6, 0), 8 * C_GROUP))
                        at_least(pe, "mr", C_GROUP * G + max(idx - 6 - 8 * C_GROUP, 0))
                        pe.wait_ge(s["o"], 2 * spreads + 2)
                        pe.wait_ge(s["es"], spreads + 1)
                        for c in range(2):
                            mm = pe.matmul(ps(RB + c, BANK, slice(0, 64)), cst[0:97, C_SEL:C_SEL + 64],
                                           o97[0:97, c * BANK:(c + 1) * BANK], start=True, stop=True)
                        mm.then_inc(s["bc"], 1)
                        spreads += 1

                    def step(n, G):
                        at_least(pe, "fin", spreads)
                        if n < NW:
                            t_, c = prods[n]
                            lo, hi = CH[c]
                            pe.wait_ge(s[f"w{t_}"], 16 * (G + 1))
                            at_least(pe, "rawc", NW * G + n)
                            at_least(pe, "mr", C_GROUP * G)
                            for k in range(KT):
                                mm = pe.matmul(ps(RB, hi - lo), wt[t_][:, k, :], U[:, k, lo:hi],
                                               start=(k == 0), stop=(k == KT - 1))
                            mm.then_inc(s["raw"], 1)
                        if 0 < n < NW + 1:
                            w = n - 1
                            lo, hi = CH[prods[w][1]]
                            pe.wait_ge(s["sq"], NW * G + w + 1)
                            at_least(pe, "out", NW * G + w)
                            pe.matmul(ps(NB, hi - lo), bones, sq[w % 2][:, :hi - lo], start=True, stop=True)
                            pe.matmul(ps(TB, hi - lo), rot1[:, 1 - prods[w][0], :], raw[w % 2][:, :hi - lo],
                                      start=True, stop=True).then_inc(s["nt"], 1)
                        if 6 <= n < 6 + 8 * C_GROUP:
                            j, qt = divmod(n - 6, 8)
                            if n == 6:
                                pe.wait_ge(s["cast"], NW * (G + 1))
                            at_least(pe, "mc", 8 * C_GROUP * G + n - 6)
                            q = qb[j][0:64, qt * P:(qt + 1) * P]
                            lo, hi = WIN[qt]
                            pe.matmul(ps(RB, BANK)[:, CTX:BANK], q, kb[0:64, SEQ:T], start=True, stop=True)
                            nk = (hi - lo) * P
                            pe.matmul(ps(NB, nk), q, kb[0:64, lo * P:hi * P], start=True, stop=False)
                            if qt > 0:
                                mm = pe.matmul(ps(NB, P), identb[:, :], maskb[:, 0, :], start=False, stop=(qt == 7))
                            if qt < 7:
                                mm = pe.matmul(ps(NB, nk)[:, nk - P:nk], identb[:, :], maskb[:, 1, :],
                                               start=False, stop=True)
                            mm.then_inc(s["mx"], 1)
                        if n >= 6 + 8 * C_GROUP:
                            j = n - 6 - 8 * C_GROUP
                            pe.wait_ge(s["mn"], C_GROUP * G + j + 1)
                            at_least(pe, "mr", C_GROUP * G + j)
                            for m in range(8):
                                mm = pe.matmul(ps(RB + m // 4, BANK, slice(64, 65))[:, (m % 4) * P:(m % 4 + 1) * P],
                                               mcb[:, 8 * j + m:8 * j + m + 1], identb[:, :], start=True, stop=True)
                            mm.then_inc(s["mrow"], 1)

                    def begin(g, j, u):
                        if (g, j, u) == (0, 0, 0):
                            qk(0, 0, 0)
                        if following(g, j, u):
                            qk(*following(g, j, u))
                        if u == 2 and (g or j):
                            G = g + 1
                            spread(sum(pl < (j, u) for pl in places) if G < C_KV else 0, G)

                    pe.wait_ge(s["tab"], 16)
                    pe.wait_ge(s["one"], 2)
                    everywhere(step, pv, begin, lambda g, j: None)
                    spread(0, C_KV)

                @block.scalar
                def _(act):
                    def step(n, G):
                        if n < NW:
                            lo, hi = CH[prods[n][1]]
                            m = hi - lo
                            act.wait_ge(s["raw"], NW * G + n + 1)
                            at_least(act, "nt", NW * G + n - 1)
                            at_least(act, "t1", NW * G + n - 1)
                            act.activation(raw[n % 2][:, :m], ps(RB, m), ACT.Copy).then_inc(s["rawc"], 1)
                            act.wait_ge(s["rawc"], NW * G + n + 1)
                            act.activation(sq[n % 2][:, :m], raw[n % 2][:, :m], ACT.Square).then_inc(s["sq"], 1)
                        if 0 < n < NW + 1:
                            w = n - 1
                            lo, hi = CH[prods[w][1]]
                            m = hi - lo
                            act.wait_ge(s["nt"], NW * G + w + 1)
                            at_least(act, "rinv", NW * G + w)
                            act.activation(lnb[:, :m], ps(NB, m), ACT.Ln, bias=eps[:, 0:1], scale=1.0 / C_HD)\
                                .then_inc(s["ln"], 1)
                            act.wait_ge(s["ln"], NW * G + w + 1)
                            act.activation(ps(NB, m), lnb[:, :m], ACT.Exp, scale=-0.5).then_inc(s["rinv"], 1)
                        if n >= 6 + 8 * C_GROUP:
                            j = n - 6 - 8 * C_GROUP
                            act.wait_ge(s["mrow"], C_GROUP * G + j + 1)
                            act.activation(qa[G % 2][j][64:65, :], PS[64:65, RB * BANK:RB * BANK + SEQ], ACT.Copy)\
                                .then_inc(s["mr"], 1)

                    def attend(g, j, u):
                        _, q0, q1 = units[u]
                        n = (q1 - q0) * P
                        U_ = NU * (C_GROUP * g + j) + u
                        act.wait_ge(s["S"], U_ + 1)
                        at_least(act, "PV", U_ - 1)
                        act.activation(pr[u % 2][:, :n], ps(u % 2, n), ACT.Exp, scale=C_SCALE).then_inc(s["P"], 1)

                    def begin(g, j, u):
                        if (g, j, u) == (0, 0, 0):
                            attend(0, 0, 0)
                        if following(g, j, u):
                            attend(*following(g, j, u))
                        if u == 2 and (g or j):
                            inverse_sum(C_GROUP * g + j - 1)

                    def inverse_sum(h):
                        act.wait_ge(s["bc"], h + 1)
                        at_least(act, "rs", h)
                        r = PS[0:64, RB * BANK:RB * BANK + SEQ]
                        act.activation(lnr[0:64, :], r, ACT.Ln).then_inc(s["lnr"], 1)
                        act.wait_ge(s["lnr"], h + 1)
                        act.activation(r, lnr[0:64, :], ACT.Exp, scale=-1.0).then_inc(s["rs"], 1)

                    def end(g, j):
                        h = C_GROUP * g + j
                        act.wait_ge(s["PV"], NU * (h + 1))
                        at_least(act, "fin", h)
                        for c in range(2):
                            act.activation(o97[0:65, c * BANK:(c + 1) * BANK], ps(2 + c, BANK, slice(0, 65)), ACT.Copy)\
                                .then_inc(s["o"], 1)
                        act.activation(o97[96:97, :], qa[g % 2][j][64:65, :], ACT.Exp, scale=C_SCALE,
                                       bias=sml[64:65, W_SINK + h:W_SINK + h + 1]).then_inc(s["es"], 1)

                    act.wait_ge(s["zero"], 1)
                    everywhere(step, lambda g, j, u: None, begin, end)
                    inverse_sum(C_HEADS - 1)

                @block.vector
                def _(dve):
                    heads = 0

                    def finish():
                        nonlocal heads
                        h = heads
                        heads += 1
                        dve.wait_ge(s["rs"], h + 1)
                        half = 64 * (h % 2)
                        dve.tensor_tensor(MIX1[half:half + 64, h // 2, :], o97[0:64, :],
                                          PS[0:64, RB * BANK:RB * BANK + SEQ], ALU.mult).then_inc(s["fin"], 1)

                    def step(n, G):
                        b = G % 2
                        if 0 < n < NW + 1:
                            w = n - 1
                            t_, c = prods[w]
                            lo, hi = CH[c]
                            m = hi - lo
                            q = NW * G + w
                            dve.wait_ge(s["sq"], q + 1)
                            at_least(dve, "out", q)
                            dve.scalar_tensor_tensor(out=t1[:, :m], in0=raw[w % 2][:, :m],
                                                     scalar=sml[:, W_G1 + 1 - t_:W_G1 + 2 - t_],
                                                     in1=rope[:, 0, lo:hi], op0=ALU.mult, op1=ALU.mult)\
                                .then_inc(s["t1"], 1)
                            dve.wait_ge(s["nt"], q + 1)
                            T_ = ps(TB, m)
                            dve.tensor_tensor(T_, T_, rope[:, 1, lo:hi], ALU.mult).then_inc(s["ts"], 1)
                            dve.wait_ge(s["ts"], q + 1)
                            dve.tensor_tensor(t1[:, :m], t1[:, :m], T_, ALU.add).then_inc(s["ta"], 1)
                            dve.wait_ge(s["ta"], q + 1)
                            dve.wait_ge(s["rinv"], q + 1)
                            dsts = [qa[b][2] if c < 2 else None, ka[b]] if t_ == 0 else [qa[b][0], qa[b][1]]
                            for r, dst in enumerate(dsts):
                                if dst is not None:
                                    op = dve.tensor_tensor(dst[0:64, lo:hi], t1[64 * r:64 * r + 64, :m],
                                                           ps(NB, m, slice(64 * r, 64 * r + 64)), ALU.mult)
                            op.then_inc(s["out"], 1)
                        if 6 <= n < 6 + 8 * C_GROUP:
                            m = n - 6
                            dve.wait_ge(s["mx"], 8 * C_GROUP * G + m + 1)
                            if m == 0:
                                at_least(dve, "mn", C_GROUP * G)
                            lo, hi = WIN[m % 8]
                            dve.reduce_max(mc[:, m:m + 1],
                                           PS[:, RB * BANK + CTX:NB * BANK + (hi - lo) * P], AX_X)\
                                .then_inc(s["mc"], 1)
                        if n >= 6 + 8 * C_GROUP:
                            j = n - 6 - 8 * C_GROUP
                            h = C_GROUP * G + j
                            dve.wait_ge(s["mc"], 8 * C_GROUP * (G + 1))
                            at_least(dve, "mrow", C_GROUP * G)
                            dve.tensor_scalar(mcb[:, 8 * j:8 * j + 8], mc[:, 8 * j:8 * j + 8], s8[:, h:h + 1], -1.0,
                                              ALU.max, ALU.mult).then_inc(s["mn"], 1)

                    dve.tensor_scalar(s8, sml[:, W_SINK:W_SINK + C_HEADS], 1 / C_SCALE, None, ALU.mult)\
                        .then_inc(s["s8"], 1)
                    dve.wait_ge(s["s8"], 1)
                    dve.wait_ge(s["tab"], 16)

                    def begin(g, j, u):
                        if u == 2 and (g or j):
                            finish()
                    everywhere(step, lambda g, j, u: None, begin, lambda g, j: None)
                    finish()

        norm(1, 0, T)
        linear("pool_", a["w_pool"], U, KT, 2, SEQ, O_B, pool_take)
        pooling()
        values1()
        heads1()
        linear("out1_", a["w_out1"], MIX1, KT, KT, SEQ, O_B, residual(1, 2, SEQ))
        work.close()
        recycle()
        ffn(1, SEQ)
        stored = sem("stored")
        with nc.Block() as block:
            @block.sync
            def _(sp):
                sp.dma_start(out, X[:, :, 0:SEQ]).then_inc(stored, 16)
                sp.wait_ge(stored, 16)


def kernel(**inputs):
    import concourse.bacc as bacc
    from concourse.bass_utils import run_bass_kernel_spmd

    f = {k: np.asarray(v) for k, v in inputs.items()}

    def cols(v):
        return v.reshape(-1, P).T

    def rows(m):
        return m.reshape(-1, P, m.shape[-1]).transpose(1, 0, 2)

    def tiles(m, width=P):
        k, n = m.shape
        return m.reshape(k // P, P, n // width, width).transpose(2, 1, 0, 3).reshape(n // width, P, -1)

    def twice(v):
        return np.repeat(v[..., None], 2, axis=-1).reshape(v.shape[0], -1)

    z = {"xT": rows(np.concatenate([f["x"][0], f["ctx"][0]], 0).T),
         "cT": np.stack([cols(f["c"][0]), cols(f["c_ctx"])], -1)}
    z["mod_w"] = f["mod_w"].reshape(DEPTH, KT, P, -1, BANK).transpose(0, 3, 2, 1, 4).reshape(-1, P, KT, BANK)
    small = np.zeros((P, N_SMALL), np.float32)

    def put(col, v, r=0):
        small[r:r + v.shape[0], col:col + v.shape[1]] = v
    put(W_MODB, twice(cols(f["mod_b"].reshape(-1))))
    for layer in range(DEPTH):
        for n, g in enumerate((f["norm1_g"], f["norm2_g"])):
            put(W_NG + (2 * layer + n) * 2 * KT, twice(cols(g[layer])))
    put(W_CQG, cols(f["mla_cq_g"][0]))
    put(W_CKVG, cols(f["mla_ckv_g"][0]))
    put(W_G0, f["mla_q_g"].T)
    put(W_G0 + 1, f["mla_k_g"].T)
    q, k = f["win_q_g"].T, f["win_k_g"].T
    put(W_G1, np.concatenate([q, q]))
    put(W_G1 + 1, np.concatenate([q, k]))
    put(W_SINK, np.tile(f["win_sink"].reshape(1, -1), (P, 1)))
    put(W_PS, cols(f["pool_scale"][0]))
    for p in range(2):
        for i in range(2):
            put(W_FN + p * P + 64 * i, f["fnet_w"][0, 2 * p + i], 64 * i)
            put(W_PW + p * P + 64 * i, f["pool_w"][0, 2 * p + i], 64 * i)
    z["small"] = small
    w = f["mla_w_in"][0]
    pad = np.zeros((D, 96), np.float32)
    z["w_in0"] = tiles(np.concatenate([w[:, :416], pad, w[:, 416:]], 1))
    uq = f["mla_w_uq"][0].reshape(2, P, A_HEADS, A_QK).transpose(2, 1, 0, 3).reshape(A_HEADS, P, -1)
    ukv = f["mla_w_ukv"][0].reshape(P, A_HEADS, 128)
    z["wqk0"] = np.concatenate([uq, ukv[:, :, :64].transpose(1, 0, 2)], -1)
    z["w_v0"] = ukv[:, :, 64:].reshape(P, -1)
    z["w_out0"] = tiles(f["even_w_out"][0])
    w = f["win_w_in"][0]
    qs = w[:, :768].reshape(D, C_KV, C_GROUP, 64)
    ks = w[:, 768:1024].reshape(D, C_KV, 64)
    z["wqk1"] = np.concatenate([t for g in range(C_KV) for t in (
        tiles(np.concatenate([qs[:, g, 2], ks[:, g]], 1)), tiles(np.concatenate([qs[:, g, 0], qs[:, g, 1]], 1)))])
    z["w_v1"] = rows(w[:, 1024:1280])
    z["w_pool"] = tiles(w[:, 1280:])
    z["w_out1"] = tiles(f["odd_w_out"][0])
    z["w_up"] = np.stack([tiles(m) for m in f["ffn_up"]])
    z["w_down"] = f["ffn_down"].reshape(DEPTH, FT // 2, 2, P, D).transpose(0, 1, 3, 2, 4)
    conv = np.concatenate([f["ffn_conv_w"], f["ffn_conv_b"][:, None]], 1)
    z["conv"] = conv.reshape(DEPTH, 4, 2 * FT, P).transpose(0, 3, 2, 1).reshape(DEPTH, P, -1)
    z.update(constants())

    nc = bacc.Bacc("TRN2", target_bir_lowering=False, num_devices=1,
                   dynamic_dma_scratch_size=1024)
    arrays, args = {}, {}
    for name, v in z.items():
        v = np.ascontiguousarray(v)
        arrays["in_" + name] = v
        args[name] = nc.dram_tensor("in_" + name, v.shape, F32, kind="ExternalInput").ap()
    out = nc.dram_tensor("out", (P, KT, SEQ), F32, kind="ExternalOutput").ap()
    program(nc, args, out)
    r = run_bass_kernel_spmd(nc, [arrays], core_ids=[0])
    y = np.asarray(r.results[0]["out"])
    return y.transpose(2, 1, 0).reshape(1, SEQ, D)
```

```python
from contextlib import ExitStack, contextmanager
from itertools import count

import numpy as np

import concourse.bass as bass
from concourse import mybir

F32 = mybir.dt.float32
BF16 = mybir.dt.bfloat16
F32R = mybir.dt.float32r
ALU = mybir.AluOpType
ACT = mybir.ActivationFunctionType
AX_X = mybir.AxisListType.X
ds = bass.ds

P = 128
D = 1024
KT = D // P
SEQ, CTX = 1024, 256
T = SEQ + CTX
GRID_W = 64
DEPTH = 2
N_MOD = 6
EPS = 1e-6
BANK = 512
CH = [(0, 512), (512, 1024), (1024, 1280)]
STREAMS = [(0, SEQ, 0), (SEQ, T, 1)]

A_HEADS, A_NOPE, A_ROPE, A_V = 12, 64, 32, 64
A_QK = A_NOPE + A_ROPE
A_SCALE = A_QK ** -0.5
C_HEADS, C_KV, C_HD = 12, 4, 64
C_GROUP = C_HEADS // C_KV
C_SCALE = C_HD ** -0.5
D_FF = 2816
FT = D_FF // P
MASKED = -1e30

C_IDENT, C_ONES, C_BONES, C_R0, C_R1, C_SEL, C_GE, C_LE, C_COSC, C_SINC = [i * P for i in range(10)]
N_CONST = 10 * P
(W_MODB, W_NG, W_CQG, W_CKVG, W_G0, W_G1, W_SINK, W_PS, W_FN, W_PW) = np.cumsum(
    [0, 192, 4 * KT * 2, 2, 1, 2, 2, 12, 2, 256]).tolist()

N_SMALL = W_PW + 256


def constants():
    c = np.zeros((P, N_CONST), np.float32)
    i = np.arange(P)
    c[:, C_IDENT:C_IDENT + P] = np.eye(P)
    c[:, C_ONES:C_ONES + P] = 1
    c[:, C_BONES:C_BONES + P] = (i[:, None] // 64) == (i[None, :] // 64)
    for m in range(16):
        c[64 + m + 16, C_R0 + 64 + m] = -1
        c[64 + m, C_R0 + 64 + m + 16] = 1
    for b in (0, 64):
        for m in range(32):
            c[b + m + 32, C_R1 + b + m] = -1
            c[b + m, C_R1 + b + m + 32] = 1
    c[64, C_SEL:C_SEL + 64] = c[96, C_SEL:C_SEL + 64] = 1
    c[0:4, C_SEL + 64:C_SEL + 66] = np.eye(4, 2) + np.eye(4, 2, -2)
    c[:, C_GE:C_GE + P] = np.where(i[None, :] >= i[:, None], 0, MASKED)
    c[:, C_LE:C_LE + P] = np.where(i[None, :] <= i[:, None], 0, MASKED)
    ang = 2 * np.pi * np.outer(np.arange(64), np.arange(64)) / 64
    for b in (0, 64):
        c[b:b + 64, C_COSC + b:C_COSC + b + 64] = np.cos(ang) / 256
        c[b:b + 64, C_SINC + b:C_SINC + b + 64] = -np.sin(ang) / 256
    t = np.arange(SEQ)

    def rope(dim):
        n = dim // 4
        inv = np.float32(10000.0) ** (-np.arange(n, dtype=np.float32) / np.float32(n))
        row, col = (t // GRID_W).astype(np.float32), (t % GRID_W).astype(np.float32)
        a = np.concatenate([row[:, None] * inv, col[:, None] * inv], axis=-1)
        return np.cos(a).T.astype(np.float32), np.sin(a).T.astype(np.float32)

    rope0 = np.zeros((A_QK, 2, T), np.float32)
    rope0[:, 0] = 1
    cs, sn = rope(A_ROPE)
    for b in (64, 80):
        rope0[b:b + 16, 0, :SEQ], rope0[b:b + 16, 1, :SEQ] = cs, sn
    rope1 = np.zeros((P, 2, T), np.float32)
    rope1[:, 0] = 1
    cs, sn = rope(C_HD)
    for b in (0, 32, 64, 96):
        rope1[b:b + 32, 0, :SEQ], rope1[b:b + 32, 1, :SEQ] = cs, sn

    def dft(n, scale):
        k = np.outer(np.arange(n), np.arange(n)) % n
        a = 2 * np.pi * k / n
        m = np.stack([np.cos(a), np.sin(a)], 1) * scale
        return m.astype(np.float32).reshape(n // P, P, 2, n)

    half = np.array([1, 2, 4, 8])
    cnt = np.clip(t[None] + half[:, None], 0, SEQ) - np.clip(t[None] - half[:, None], 0, SEQ)
    inv = np.repeat(1.0 / cnt, 64, axis=0).reshape(2, P, SEQ).transpose(1, 0, 2).astype(np.float32)
    return {"const": c, "rope0": rope0, "rope1": rope1, "dft": dft(SEQ, 1), "dftc": dft(CTX, 2),
            "pool_inv": np.ascontiguousarray(inv)}


def program(nc, a, out):
    ctx = ExitStack()
    with ctx:
        def sb(name, shape, dt=F32):
            return ctx.enter_context(nc.sbuf_tensor(name, shape, dt))

        held = []

        def sem(name):
            held.append(nc.alloc_semaphore(name))
            return held[-1]

        def recycle():
            nc.clear_and_free_semaphores(list(held))
            held.clear()
            nc.all_engine_barrier()

        X = sb("X", [P, KT, T])
        cst = sb("cst", [P, N_CONST])
        sml = sb("sml", [P, N_SMALL])
        mod = sb("mod", [P, DEPTH * N_MOD * KT, 2])
        gsc = sb("gsc", [P, DEPTH * 2 * KT, 2])
        eps = sb("eps", [P, 1])
        identb = sb("identb", [P, P], BF16)
        maskb = sb("maskb", [P, 2, P], BF16)
        rot0 = sb("rot0", [A_QK, 2, A_QK])
        rot1 = sb("rot1", [P, 2, P])
        PS = ctx.enter_context(nc.psum_tensor("PS", [P, 8 * BANK], F32))

        BASE = -(-nc.sbuf_base // 32) * 32
        ARENA = (nc.sbuf_usable_end - BASE) // 4
        parts = count()

        O_ACC = ARENA - T
        O_SQ = ARENA - 4 * T

        def big(off, *shape):
            assert off + int(np.prod(shape)) <= ARENA, (off, shape, ARENA)
            t = nc.alloc_sbuf_tensor_at(f"part{next(parts)}", [P, *shape], F32, offset=BASE + 4 * off, align_bytes=4)
            return t[(slice(None),) * (1 + len(shape))]

        def place(name, off, *shape):
            assert off + int(np.prod(shape)) <= ARENA, (name, off, ARENA)
            return nc.alloc_sbuf_tensor_at(name, [P, *shape], F32R, offset=BASE + 4 * off)

        def ps(bank, n, rows=slice(0, P)):
            return PS[rows, bank * BANK:bank * BANK + n]

        ident = cst[:, C_IDENT:C_IDENT + P]
        ones = cst[:, C_ONES:C_ONES + P]
        bones = cst[:, C_BONES:C_BONES + P]

        def moda(layer, which, tile, s, n=1):
            return mod[:, ds((layer * N_MOD + which) * KT + tile, n), s]

        def mods():
            NC = DEPTH * N_MOD * D // BANK
            with ExitStack() as c2:
                def tensor(name, shape, dt=F32):
                    return c2.enter_context(nc.sbuf_tensor("mod_" + name, shape, dt))
                cT = tensor("cT", [P, KT, 2])
                sil = tensor("silu", [P, KT, 2])
                sil4 = tensor("silu4", [P, KT, 4], F32R)
                row = tensor("row", [4, 2, BANK])
                W = [tensor(f"w{b}", [P, KT, BANK]) for b in range(4)]
                Wh = [tensor(f"wh{b}", [P, KT, BANK], F32R) for b in range(2)]
                Wl = [tensor(f"wl{b}", [P, KT, BANK], F32R) for b in range(2)]
                s = {n: sem("mod_" + n) for n in
                     ("in", "x", "sil", "silh", "sill", "dve", "w0", "w1", "w2", "w3",
                      "high", "low", "rows", "rowc", "cols", "out")}
                block = c2.enter_context(nc.Block())
                TRIPS = NC // 4

                def at_least(eng, name, value):
                    if not (isinstance(value, int) and value <= 0):
                        eng.wait_ge(s[name], value)

                def lagged(eng, ahead, behind, lag):
                    def trip(i, last=False):
                        for j in range(4):
                            if j < 4 - lag:
                                ahead(i, j + lag)
                            elif not last:
                                ahead(i + 1, j + lag - 4)
                            behind(i, j)
                    for j in range(lag):
                        ahead(0, j)
                    trip(0)
                    with eng.Fori(1, TRIPS - 1) as i:
                        trip(i)
                    trip(TRIPS - 1, last=True)

                @block.sync
                def _(sp):
                    sp.dma_start(cT[:, :, :], a["cT"]).then_inc(s["in"], 16)
                    sp.dma_start(sml[:, :], a["small"]).then_inc(s["in"], 16)
                    sp.dma_start(cst[:, :], a["const"]).then_inc(s["in"], 16)

                    def load(i, j):
                        at_least(sp, "low", 4 * i + j - 3)
                        sp.dma_start(W[j][:, :, :], a["mod_w"][ds(4 * i + j, 1)].rearrange("o p k n -> (o p) k n"))\
                            .then_inc(s[f"w{j}"], 16)
                    for j in range(4):
                        load(0, j)
                    sp.dma_start(X[:, :, :], a["xT"]).then_inc(s["x"], 16)
                    with sp.Fori(1, TRIPS) as i:
                        for j in range(4):
                            load(i, j)
                    sp.wait_ge(s["x"], 16)

                @block.scalar
                def _(act):
                    act.wait_ge(s["in"], 48)
                    act.activation(sil[:, :, :], cT[:, :, :], ACT.Silu).then_inc(s["sil"], 1)
                    act.wait_ge(s["sil"], 1)
                    act.activation(sil4[:, :, 0:2], sil[:, :, :], ACT.Copy).then_inc(s["silh"], 1)

                    def high(i, j):
                        act.wait_ge(s[f"w{j}"], 16 * i + 16)
                        at_least(act, "rows", 4 * i + j - 1)
                        act.activation(Wh[j % 2][:, :, :], W[j][:, :, :], ACT.Copy).then_inc(s["high"], 1)

                    def rows(i, j):
                        act.wait_ge(s["rows"], 4 * i + j + 1)
                        at_least(act, "cols", 4 * i + j - 1)
                        act.activation(row[0:4, j % 2, :], ps(j, BANK, slice(0, 4)), ACT.Copy)\
                            .then_inc(s["rowc"], 1)
                    lagged(act, high, rows, 2)

                @block.tensor
                def _(pe):
                    pe.wait_ge(s["sill"], 1)

                    def product(i, j):
                        b = j % 2
                        at_least(pe, "rowc", 4 * i + j - 3)
                        for half, name in ((Wh, "high"), (Wl, "low")):
                            pe.wait_ge(s[name], 4 * i + j + 1)
                            for k in range(KT):
                                mm = pe.matmul(ps(j, BANK, slice(0, 4)), sil4[:, k, :], half[b][:, k, :],
                                               start=(half is Wh and k == 0), stop=(half is Wl and k == KT - 1))
                        mm.then_inc(s["rows"], 1)

                    def turn(i, j):
                        pe.wait_ge(s["rowc"], 4 * i + j + 1)
                        at_least(pe, "out", 4 * i + j - 1)
                        for q in range(4):
                            mm = pe.matmul(ps(4 + j % 2, 8)[:, 2 * q:2 * q + 2], row[0:4, j % 2, q * P:(q + 1) * P],
                                           cst[0:4, C_SEL + 64:C_SEL + 66], start=True, stop=True)
                        mm.then_inc(s["cols"], 1)
                    lagged(pe, product, turn, 2)

                @block.vector
                def _(dve):
                    dve.wait_ge(s["silh"], 1)
                    dve.tensor_tensor(sil4[:, :, 2:4], sil[:, :, :], sil4[:, :, 0:2].bitcast(F32), ALU.subtract)\
                        .then_inc(s["sill"], 1)
                    dve.memset(eps[:, :], EPS).then_inc(s["dve"], 1)
                    dve.wait_ge(s["in"], 48)
                    dve.tensor_copy(identb[:, :], ident).then_inc(s["dve"], 1)
                    for n, col in enumerate((C_GE, C_LE)):
                        dve.tensor_copy(maskb[:, n, :], cst[:, col:col + P]).then_inc(s["dve"], 1)
                    for n in range(2):
                        dve.tensor_scalar(rot0[:, n, :], cst[0:A_QK, C_R0:C_R0 + A_QK],
                                          sml[0:A_QK, W_G0 + n:W_G0 + n + 1], None, ALU.mult).then_inc(s["dve"], 1)
                        dve.tensor_scalar(rot1[:, n, :], cst[:, C_R1:C_R1 + P],
                                          sml[:, W_G1 + n:W_G1 + n + 1], None, ALU.mult).then_inc(s["dve"], 1)
                    modb = sml[:, W_MODB:W_MODB + 192].rearrange("p (x y) -> p x y", y=2)

                    def low(i, j):
                        dve.wait_ge(s["high"], 4 * i + j + 1)
                        dve.tensor_tensor(Wl[j % 2][:, :, :], W[j][:, :, :], Wh[j % 2][:, :, :].bitcast(F32),
                                          ALU.subtract).then_inc(s["low"], 1)

                    def add(i, j):
                        dve.wait_ge(s["cols"], 4 * i + j + 1)
                        dve.tensor_tensor(mod[:, ds(16 * i + 4 * j, 4), :],
                                          ps(4 + j % 2, 8).rearrange("p (x y) -> p x y", y=2),
                                          modb[:, ds(16 * i + 4 * j, 4), :], ALU.add).then_inc(s["out"], 1)
                    lagged(dve, low, add, 3)
                    dve.wait_ge(s["out"], NC)
                    for n in range(2 * DEPTH):
                        layer, which = n // 2, 1 + 3 * (n % 2)
                        o = (layer * N_MOD + which) * KT
                        g = sml[:, W_NG + n * 2 * KT:W_NG + (n + 1) * 2 * KT].rearrange("p (x y) -> p x y", y=2)
                        dve.scalar_tensor_tensor(out=gsc[:, n * KT:(n + 1) * KT, :], in0=mod[:, o:o + KT, :],
                                                 scalar=1.0, in1=g, op0=ALU.add, op1=ALU.mult).then_inc(s["dve"], 1)

        def split_norm(tag, layer, which, n, uh, ul, lnb, tt1):
            chunks = [c for c in CH if c[0] < n]
            streams = [x for x in STREAMS if x[0] < n]
            s = {n_: nc.alloc_semaphore(tag + n_) for n_ in ("sq", "sum", "acc", "ln", "rinv", "t", "uh", "ul")}
            acc = big(O_ACC, T)
            sq = [big(O_SQ + b * T, T) for b in range(2)]
            tt = [acc, tt1]

            class parts:
                sems = s
                halves = uh, ul
                first = tag == "n0_"

                def square(act, k):
                    if k == 0:
                        act.preload_act_table_set("natural_log_exp_and_others")
                    if k >= 3:
                        act.wait_ge(s["sum"], k - 2)
                    act.activation((acc if k == 0 else sq[k % 2])[:, :n], X[:, k, 0:n], ACT.Square)\
                        .then_inc(s["sq"], 1)

                def act_apply(act):
                    act.wait_ge(s["acc"], 1)
                    act.activation(lnb[:, :n], PS[:, 0:n], ACT.Ln, bias=eps[:, 0:1], scale=1.0 / D)\
                        .then_inc(s["ln"], 1)
                    act.wait_ge(s["ln"], 1)
                    act.activation(lnb[:, :n], lnb[:, :n], ACT.Exp, scale=-0.5).then_inc(s["rinv"], 1)
                    for k in range(KT):
                        act.wait_ge(s["t"], k + 1)
                        for lo, hi, v in streams:
                            op = act.activation(uh[:, k, lo:hi], tt[k % 2][:, lo:hi], ACT.Identity,
                                                bias=moda(layer, 3 * which, k, v))
                        op.then_inc(s["uh"], 1)

                def pe(pe):
                    pe.wait_ge(s["sum"], KT - 1)
                    for c0, c1 in chunks:
                        mm = pe.matmul(PS[:, c0:c1], ones, acc[:, c0:c1], start=True, stop=True)
                    mm.then_inc(s["acc"], 1)

                def add(dve, k):
                    dve.wait_ge(s["sq"], k + 1)
                    if k >= 2:
                        dve.wait_ge(s["sum"], k - 1)
                    dve.tensor_tensor(acc[:, :n], acc[:, :n], sq[k % 2][:, :n], ALU.add).then_inc(s["sum"], 1)

                def dve_apply(dve):
                    dve.wait_ge(s["rinv"], 1)

                    def rest(k):
                        dve.wait_ge(s["uh"], k + 1)
                        for lo, hi, v in streams:
                            op = dve.scalar_tensor_tensor(
                                out=ul[:, k, lo:hi], in0=tt[k % 2][:, lo:hi], scalar=moda(layer, 3 * which, k, v),
                                in1=uh[:, k, lo:hi].bitcast(F32), op0=ALU.add, op1=ALU.subtract)
                        op.then_inc(s["ul"], 1)
                    for k in range(KT):
                        if k >= 2:
                            dve.wait_ge(s["ul"], k - 1)
                        for lo, hi, v in streams:
                            g = gsc[:, (2 * layer + which) * KT + k, v:v + 1]
                            op = dve.scalar_tensor_tensor(out=tt[k % 2][:, lo:hi], in0=X[:, k, lo:hi], scalar=g,
                                                          in1=lnb[:, lo:hi], op0=ALU.mult, op1=ALU.mult)
                        op.then_inc(s["t"], 1)
                        if k:
                            rest(k - 1)
                    rest(KT - 1)
            return parts

        def linear(tag, w, rhs, tiles, tokens, woff, take, source=None, norm=None, after=None):
            rh, rl = rhs

            @contextmanager
            def each(eng, n):
                if after or n == 0:
                    yield range(n)
                else:
                    with eng.Fori(0, n) as i:
                        yield [i]
            W = [big(woff + b * D, KT, P) for b in range(2)]
            Wh = [place(tag + f"wh{b}", woff + (2 + b) * D, KT, P) for b in range(2)]
            Wl = [place(tag + f"wl{b}", woff + (4 + b) * D, KT, P) for b in range(2)]
            with ExitStack() as c2:
                s = {n: sem(tag + n) for n in
                     ("srch", "srcl") + tuple(f"{n}{b}" for n in ("w", "high", "low", "mm", "taken") for b in range(2))}
                block = c2.enter_context(nc.Block())

                @block.sync
                def _(sp):
                    with sp.Fori(0, tiles // 2) as i:
                        for b in range(2):
                            sp.wait_ge(s[f"low{b}"], i)
                            sp.dma_start(W[b], w[ds(2 * i + b, 1)].rearrange("o p (k n) -> (o p) k n", k=KT))\
                                .then_inc(s[f"w{b}"], 16)

                @block.scalar
                def _(act):
                    def high(b, i):
                        act.wait_ge(s[f"w{b}"], 16 * i + 16)
                        act.wait_ge(s[f"mm{b}"], i)
                        act.activation(Wh[b][:, :, :], W[b], ACT.Copy).then_inc(s[f"high{b}"], 1)
                    if norm and norm.first:
                        for k in range(KT):
                            norm.square(act, k)
                    high(0, 0)
                    if norm:
                        norm.act_apply(act)
                    if source is not None:
                        for k in range(KT):
                            act.activation(rh[:, k, :], source[:, k, :], ACT.Copy).then_inc(s["srch"], 1)

                    def square(m):
                        if after and m >= 0:
                            act.wait_ge(s[f"taken{m % 2}"], m // 2 + 1)
                            after.square(act, m)
                    with each(act, tiles // 2 - 1) as trips:
                        for i in trips:
                            high(1, i)
                            square(2 * i - 1 if after else -1)
                            high(0, i + 1)
                            square(2 * i if after else -1)
                    high(1, tiles // 2 - 1)
                    for m in (tiles - 3, tiles - 2, tiles - 1):
                        square(m)

                @block.tensor
                def _(pe):
                    if norm:
                        norm.pe(pe)
                    ready = norm.sems["ul"] if norm else s["srcl"]
                    with pe.Fori(0, tiles // 2) as i:
                        for b in range(2):
                            chunks = [c for c in CH if c[0] < tokens[b]]
                            pe.wait_ge(s[f"low{b}"], i + 1)
                            pe.wait_ge(s[f"taken{b}"], i)
                            for k in range(KT):
                                if (norm or source is not None) and b == 0:
                                    pe.wait_ge(ready, k + 1)
                                for p_, (left, right) in enumerate(((Wh, rh), (Wh, rl), (Wl, rh))):
                                    for n, (lo, hi) in enumerate(chunks):
                                        mm = pe.matmul(ps(3 * b + n, hi - lo), left[b][:, k, :], right[:, k, lo:hi],
                                                       start=(k == 0 and p_ == 0), stop=(k == KT - 1 and p_ == 2))
                            mm.then_inc(s[f"mm{b}"], 1)

                @block.vector
                def _(dve):
                    def low(b, i):
                        dve.wait_ge(s[f"high{b}"], i + 1)
                        dve.tensor_tensor(Wl[b][:, :, :], W[b], Wh[b][:, :, :].bitcast(F32), ALU.subtract)\
                            .then_inc(s[f"low{b}"], 1)

                    def store(b, i):
                        dve.wait_ge(s[f"mm{b}"], i + 1)
                        take(dve, 2 * i + b, PS[:, 3 * b * BANK:3 * b * BANK + tokens[b]])\
                            .then_inc(s[f"taken{b}"], 1)
                    if norm and norm.first:
                        for k in range(1, KT):
                            norm.add(dve, k)
                    low(0, 0)
                    if norm:
                        norm.dve_apply(dve)
                    if source is not None:
                        for k in range(KT):
                            dve.wait_ge(s["srch"], k + 1)
                            dve.tensor_tensor(rl[:, k, :], source[:, k, :], rh[:, k, :].bitcast(F32), ALU.subtract)\
                                .then_inc(s["srcl"], 1)

                    def add(m):
                        if after and m >= 1:
                            after.add(dve, m)
                    with each(dve, tiles // 2 - 1) as trips:
                        for i in trips:
                            low(1, i)
                            store(0, i)
                            add(2 * i - 1 if after else -1)
                            low(0, i + 1)
                            store(1, i)
                            add(2 * i if after else -1)
                    low(1, tiles // 2 - 1)
                    store(0, tiles // 2 - 1)
                    add(tiles - 3)
                    store(1, tiles // 2 - 1)
                    add(tiles - 2)
                    add(tiles - 1)

        def residual(layer, which, tokens):
            def take(dve, m, y):
                for lo, hi, v in [x for x in STREAMS if x[0] < tokens]:
                    xs = X[:, ds(m, 1), lo:hi].rearrange("p o n -> p (o n)")
                    op = dve.scalar_tensor_tensor(out=xs, in0=y[:, lo:hi], scalar=moda(layer, which, m, v), in1=xs,
                                                  op0=ALU.mult, op1=ALU.add)
                return op
            return take

        O_LNB, O_TT = ARENA - 3 * T, ARENA - 2 * T

        def ffn_norm(layer, n):
            return split_norm(f"s{layer}_", layer, 1, n, place(f"f{layer}_uh", 0, KT, n),
                              place(f"f{layer}_ul", KT * n, KT, n), big(O_LNB, T), big(O_TT, T))

        def ffn(layer, n, norm, after=None):
            tag = f"f{layer}_"
            chunks = [c for c in CH if c[0] < n]
            streams = [x for x in STREAMS if x[0] < n]
            NG = FT // 2
            with ExitStack() as c2:
                o = 2 * KT * n

                def buf(*shape, name=None):
                    nonlocal o
                    v = place(tag + name, o, *shape) if name else big(o, *shape)
                    o += int(np.prod(shape))
                    return v
                uh, ul = norm.halves
                gh = buf(2, n, name="gh")
                gl = buf(2, n, name="gl")
                W = [buf(KT, P) for b in range(2)]
                Wh = [buf(KT, P, name=f"Wh{b}") for b in range(2)]
                Wl = [buf(KT, P, name=f"Wl{b}") for b in range(2)]
                WD = buf(2, D)
                WDh = buf(2, D, name="WDh")
                WDl = buf(2, D, name="WDl")
                cw = buf(2 * FT, 4)
                assert o <= O_SQ
                cg, cv, sg, gp = [big(off, T)[:, :n] for off in (O_SQ, O_LNB, O_TT, O_ACC)]
                s = {n_: sem(tag + n_) for n_ in
                     ("cw", "w0", "w1", "wd", "hi", "lo", "up", "cen", "left", "conv", "silu", "mul", "gh", "gl",
                      "dhi", "dlo", "y", "acc")}
                block = c2.enter_context(nc.Block())
                PLACES = [(0, 0), (0, 1), (1, 0), (1, 1)]
                UPB = [0, 3]
                DNB = [6, 7]
                outs = [(m, c) for m in range(KT) for c in range(len(chunks))]
                NO = len(outs)

                def at_least(eng, name, value):
                    if not (isinstance(value, int) and value <= 0):
                        eng.wait_ge(s[name], value)

                def psv(bank):
                    return PS[:, bank * BANK:bank * BANK + n]

                def groups(eng, group, last):
                    group(0, False, True)
                    with eng.Fori(1, NG - 1) as g:
                        group(g, True, True)
                    group(NG - 1, True, False)
                    last()

                @block.sync
                def _(sp):
                    def load(g, place):
                        t_, kind = PLACES[place % 4]
                        g = g + place // 4
                        at_least(sp, "lo", 4 * g + place % 4 - 1)
                        sp.dma_start(W[place % 2][:, :, :], a["w_up"][layer][ds(kind * FT + 2 * g + t_, 1)]
                                     .rearrange("o p (k n) -> (o p) k n", k=KT)).then_inc(s[f"w{place % 2}"], 16)

                    def group(g, before, after):
                        for place in (1, 2, 3, 4):
                            if place == 3:
                                at_least(sp, "dlo", g)
                                sp.dma_start(WD[:, :, :], a["w_down"][layer][ds(g, 1)]
                                             .rearrange("o p k n -> (o p) k n")).then_inc(s["wd"], 16)
                            if place < 4 or after:
                                load(g, place)
                    sp.dma_start(cw[:, :, :], a["conv"][layer].rearrange("p (k n) -> p k n", n=4)).then_inc(s["cw"], 16)
                    load(0, 0)
                    groups(sp, group, lambda: None)

                @block.tensor
                def _(pe):
                    def three(bank, cs, wh, wl, xh, xl, first, final):
                        for w_, x_, f_, l_ in ((wh, xh, first, False), (wh, xl, False, False), (wl, xh, False, final)):
                            for c, (lo, hi) in enumerate(cs):
                                mm = pe.matmul(ps(bank + c, hi - lo), w_, x_[:, lo:hi], start=f_, stop=l_)
                        return mm

                    def up(g, place):
                        t_, kind = PLACES[place]
                        q = 4 * g + place
                        pe.wait_ge(s["hi"], q + 1)
                        pe.wait_ge(s["lo"], q + 1)
                        at_least(pe, "conv", q - 1)
                        for k in range(KT):
                            if isinstance(g, int) and q == 0:
                                pe.wait_ge(norm.sems["ul"], k + 1)
                            mm = three(UPB[kind], chunks, Wh[place % 2][:, k, :], Wl[place % 2][:, k, :], uh[:, k, :], ul[:, k, :],
                                       k == 0, k == KT - 1)
                        mm.then_inc(s["up"], 1)

                    def down(g):
                        pe.wait_ge(s["dhi"], g + 1)
                        pe.wait_ge(s["dlo"], g + 1)
                        pe.wait_ge(s["gh"], 2 * g + 2)
                        pe.wait_ge(s["gl"], 2 * g + 2)
                        for r, (m, c) in enumerate(outs):
                            at_least(pe, "acc", NO * g + max(r - 1, 0))
                            for k in range(2):
                                mm = three(DNB[r % 2], chunks[c:c + 1], WDh[:, k, m * P:(m + 1) * P], WDl[:, k, m * P:(m + 1) * P],
                                           gh[:, k, :], gl[:, k, :], k == 0, k == 1)
                            mm.then_inc(s["y"], 1)

                    def group(g, before, after):
                        up(g, 0)
                        if before:
                            down(g - 1)
                        for place in (1, 2, 3):
                            up(g, place)
                    norm.pe(pe)
                    groups(pe, group, lambda: down(NG - 1))

                @block.scalar
                def _(act):
                    def high(g, place):
                        g, place = g + place // 4, place % 4
                        q = 4 * g + place
                        act.wait_ge(s[f"w{place % 2}"], 16 * (2 * g + place // 2 + 1))
                        at_least(act, "up", q - 1)
                        act.activation(Wh[place % 2][:, :, :], W[place % 2][:, :, :], ACT.Copy).then_inc(s["hi"], 1)

                    def centre(g, place):
                        t_, kind = PLACES[place]
                        q = 4 * g + place
                        act.wait_ge(s["up"], q + 1)
                        at_least(act, "silu" if kind == 0 else "mul", 2 * g + t_)
                        f = kind * FT + 2 * g + t_
                        act.activation((cg, cv)[kind][:, :], psv(UPB[kind]), ACT.Identity,
                                       scale=cw[:, ds(f, 1), 1], bias=cw[:, ds(f, 1), 3]).then_inc(s["cen"], 1)

                    def silu(g, t_):
                        act.wait_ge(s["conv"], 4 * g + 2 * t_ + 1)
                        at_least(act, "mul", 2 * g + t_)
                        act.activation(sg[:, :], cg[:, :], ACT.Silu).then_inc(s["silu"], 1)

                    def gated_high(g, t_):
                        act.wait_ge(s["mul"], 2 * g + t_ + 1)
                        at_least(act, "y", NO * g)
                        act.activation(gh[:, t_, :], gp[:, :], ACT.Copy).then_inc(s["gh"], 1)

                    def down_high(g):
                        act.wait_ge(s["wd"], 16 * (g + 1))
                        at_least(act, "y", NO * g)
                        act.activation(WDh[:, :, :], WD[:, :, :], ACT.Copy).then_inc(s["dhi"], 1)

                    def group(g, before, after):
                        high(g, 1)
                        centre(g, 0)
                        silu(g, 0)
                        high(g, 2)
                        centre(g, 1)
                        gated_high(g, 0)
                        high(g, 3)
                        down_high(g)
                        centre(g, 2)
                        silu(g, 1)
                        if after:
                            high(g, 4)
                        centre(g, 3)
                        gated_high(g, 1)
                    high(0, 0)
                    norm.act_apply(act)
                    act.preload_act_table_set("silu_and_others")
                    act.wait_ge(s["cw"], 16)

                    def squares():
                        for m in range(KT if after else 0):
                            act.wait_ge(s["acc"], NO * (NG - 1) + len(chunks) * (m + 1))
                            after.square(act, m)
                    groups(act, group, squares)

                @block.vector
                def _(dve):
                    def low(g, place):
                        g, place = g + place // 4, place % 4
                        dve.wait_ge(s["hi"], 4 * g + place + 1)
                        dve.tensor_tensor(Wl[place % 2][:, :, :], W[place % 2][:, :, :],
                                          Wh[place % 2][:, :, :].bitcast(F32), ALU.subtract).then_inc(s["lo"], 1)

                    def sides(g, place):
                        t_, kind = PLACES[place]
                        q = 4 * g + place
                        x = (cg, cv)[kind]
                        h = psv(UPB[kind])
                        f = kind * FT + 2 * g + t_
                        dve.wait_ge(s["cen"], q + 1)
                        for lo, hi, _ in streams:
                            op = dve.scalar_tensor_tensor(out=x[:, lo + 1:hi], in0=h[:, lo:hi - 1],
                                                          scalar=cw[:, ds(f, 1), 0], in1=x[:, lo + 1:hi],
                                                          op0=ALU.mult, op1=ALU.add)
                        op.then_inc(s["left"], 1)
                        dve.wait_ge(s["left"], q + 1)
                        for lo, hi, _ in streams:
                            op = dve.scalar_tensor_tensor(out=x[:, lo:hi - 1], in0=h[:, lo + 1:hi],
                                                          scalar=cw[:, ds(f, 1), 2], in1=x[:, lo:hi - 1],
                                                          op0=ALU.mult, op1=ALU.add)
                        op.then_inc(s["conv"], 1)

                    def product(g, t_):
                        dve.wait_ge(s["conv"], 4 * g + 2 * t_ + 2)
                        dve.wait_ge(s["silu"], 2 * g + t_ + 1)
                        at_least(dve, "gl", 2 * g + t_)
                        dve.tensor_tensor(gp[:, :], sg[:, :], cv[:, :], ALU.mult).then_inc(s["mul"], 1)
                        dve.wait_ge(s["gh"], 2 * g + t_ + 1)
                        dve.tensor_tensor(gl[:, t_, :], gp[:, :], gh[:, t_, :].bitcast(F32), ALU.subtract)\
                            .then_inc(s["gl"], 1)

                    def down_low(g):
                        dve.wait_ge(s["dhi"], g + 1)
                        dve.tensor_tensor(WDl[:, :, :], WD[:, :, :], WDh[:, :, :].bitcast(F32), ALU.subtract)\
                            .then_inc(s["dlo"], 1)

                    def add(g, after=None):
                        at_least(dve, "acc", NO * g)
                        for r, (m, c) in enumerate(outs):
                            lo, hi = chunks[c]
                            dve.wait_ge(s["y"], NO * g + r + 1)
                            dve.scalar_tensor_tensor(out=X[:, m, lo:hi], in0=ps(DNB[r % 2], hi - lo),
                                                     scalar=moda(layer, 5, m, 0 if lo < SEQ else 1), in1=X[:, m, lo:hi],
                                                     op0=ALU.mult, op1=ALU.add).then_inc(s["acc"], 1)
                            if after and c == len(chunks) - 1 and m >= 2:
                                after.add(dve, m - 1)
                        if after:
                            after.add(dve, KT - 1)

                    def group(g, before, after):
                        low(g, 1)
                        if before:
                            add(g - 1)
                        sides(g, 0)
                        low(g, 2)
                        sides(g, 1)
                        product(g, 0)
                        low(g, 3)
                        down_low(g)
                        sides(g, 2)
                        if after:
                            low(g, 4)
                        sides(g, 3)
                        product(g, 1)
                    low(0, 0)
                    norm.dve_apply(dve)
                    dve.wait_ge(s["cw"], 16)
                    groups(dve, group, lambda: add(NG - 1, after))

        mods()
        O_MIX = KT * T
        O_H = O_MIX + KT * T
        O_A = O_H + 6 * T
        U = big(0, KT, T)
        MIX = big(O_MIX, KT, T)
        H = big(O_H, 6, T)

        def copy_take(dst, tokens):
            def take(dve, m, y):
                return dve.tensor_copy(dst[:, ds(m, 1), :tokens].rearrange("p o n -> p (o n)"), y)
            return take

        V0 = U[:, :, :].rearrange("p k n -> p (k n)")[:, 0:10 * A_HEADS * 65]\
            .rearrange("p (t h d) -> p t h d", t=10, h=A_HEADS)

        def latent_norms():
            sq = big(O_A, 2, T)
            lnb = big(O_A + 2 * T, T)
            wv = big(O_A + 3 * T, A_HEADS * 64)
            parts = [((0, 1), 256, W_CQG), ((2,), 128, W_CKVG)]
            with ExitStack() as c2:
                s = {n: sem("ln_" + n) for n in
                     ("w", "sq", "acc", "ln", "rinv", "u", "v", "vc", "one")}
                block = c2.enter_context(nc.Block())

                @block.sync
                def _(sp):
                    sp.dma_start(wv, a["w_v0"]).then_inc(s["w"], 16)

                @block.gpsimd
                def _(pool):
                    pool.memset(V0[:, :, :, 64], 1.0).then_inc(s["one"], 1)

                @block.scalar
                def _(act):
                    act.preload_act_table_set("natural_log_exp_and_others")
                    n = 0
                    for i, (tiles, width, _) in enumerate(parts):
                        for t_ in tiles:
                            if n >= 2:
                                act.wait_ge(s["acc"], n - 1)
                            act.activation(sq[:, n % 2, :], H[:, t_, :], ACT.Square).then_inc(s["sq"], 1)
                            n += 1
                        act.wait_ge(s["acc"], n)
                        if i:
                            act.wait_ge(s["rinv"], 1)
                        act.activation(lnb, PS[:, 3 * i * BANK:3 * i * BANK + T], ACT.Ln, bias=eps[:, 0:1],
                                       scale=1.0 / width).then_inc(s["ln"], 1)
                        act.wait_ge(s["ln"], i + 1)
                        act.activation(PS[:, 3 * i * BANK:3 * i * BANK + T], lnb, ACT.Exp, scale=-0.5)\
                            .then_inc(s["rinv"], 1)
                    for t_ in range(10):
                        act.wait_ge(s["v"], t_ + 1)
                        for h in range(2):
                            op = act.activation(
                                V0[:, t_, 6 * h:6 * h + 6, 0:64],
                                ps(2 * (t_ % 2) + h, 384).rearrange("p (h d) -> p h d", h=6), ACT.Copy)
                        op.then_inc(s["vc"], 1)

                @block.tensor
                def _(pe):
                    n = 0
                    for i, (tiles, _, _) in enumerate(parts):
                        for t_ in tiles:
                            pe.wait_ge(s["sq"], n + 1)
                            for c, (lo, hi) in enumerate(CH):
                                mm = pe.matmul(ps(3 * i + c, hi - lo), ones, sq[:, n % 2, lo:hi],
                                               start=(t_ == tiles[0]), stop=(t_ == tiles[-1]))
                            mm.then_inc(s["acc"], 1)
                            n += 1
                    pe.wait_ge(s["w"], 16)
                    pe.wait_ge(s["u"], 3)
                    for t_ in range(10):
                        if t_ >= 2:
                            pe.wait_ge(s["vc"], t_ - 1)
                        for h in range(2):
                            mm = pe.matmul(ps(2 * (t_ % 2) + h, 384), H[:, 2, t_ * P:(t_ + 1) * P],
                                           wv[:, 384 * h:384 * h + 384], start=True, stop=True)
                        mm.then_inc(s["v"], 1)

                @block.vector
                def _(dve):
                    for i, (tiles, _, g) in enumerate(parts):
                        dve.wait_ge(s["rinv"], i + 1)
                        for t_ in tiles:
                            dve.scalar_tensor_tensor(out=H[:, t_, :], in0=H[:, t_, :],
                                                     scalar=sml[:, g + t_ % 2:g + t_ % 2 + 1],
                                                     in1=PS[:, 3 * i * BANK:3 * i * BANK + T],
                                                     op0=ALU.mult, op1=ALU.mult).then_inc(s["u"], 1)

        def fourier():
            FW = big(O_A, 2, 2 * P)
            AB = big(O_A + 512, 10, 4 * P)
            DF = [big(O_A + 512 + 5120 + b * 2048, 2, SEQ) for b in range(2)]
            DC = big(O_A + 512 + 5120 + 4096, 2, 2, CTX)
            with ExitStack() as c2:
                s = {n: sem("ff_" + n) for n in
                     ("d0", "d1", "dc", "fw", "fwc", "ab", "abc", "l", "y", "yc")}
                block = c2.enter_context(nc.Block())

                @block.sync
                def _(sp):
                    sp.dma_start(DC, a["dftc"].rearrange("t p s n -> p t s n")).then_inc(s["dc"], 16)
                    for t_ in range(8):
                        if t_ >= 2:
                            sp.wait_ge(s["l"], t_ - 1)
                        sp.dma_start(DF[t_ % 2], a["dft"][t_]).then_inc(s[f"d{t_ % 2}"], 16)

                @block.tensor
                def _(pe):
                    for p in range(2):
                        for n, col in enumerate((C_COSC, C_SINC)):
                            mm = pe.matmul(ps(p, 2 * P)[:, n * P:(n + 1) * P], cst[:, col:col + P],
                                           sml[:, W_FN + p * P:W_FN + (p + 1) * P], start=True, stop=True)
                    mm.then_inc(s["fw"], 1)
                    pe.wait_ge(s["fwc"], 1)
                    for t_ in range(10):
                        if t_ >= 2:
                            pe.wait_ge(s["abc"], t_ - 1)
                        for p in range(2):
                            mm = pe.matmul(ps(2 + t_ % 2, 4 * P)[:, 2 * P * p:2 * P * (p + 1)],
                                           H[:, 4 + p, t_ * P:(t_ + 1) * P], FW[:, p, :], start=True, stop=True)
                        mm.then_inc(s["ab"], 1)
                    pe.wait_ge(s["abc"], 10)
                    for t_ in range(8):
                        pe.wait_ge(s[f"d{t_ % 2}"], 16 * (t_ // 2 + 1))
                        for p in range(2):
                            for n in range(2):
                                for c in range(2):
                                    mm = pe.matmul(ps(4 + 2 * p + c, BANK),
                                                   AB[:, t_, (2 * p + n) * P:(2 * p + n + 1) * P],
                                                   DF[t_ % 2][:, n, c * BANK:(c + 1) * BANK],
                                                   start=(t_ == 0 and n == 0), stop=(t_ == 7 and n == 1))
                        mm.then_inc(s["l"], 1)
                    pe.wait_ge(s["dc"], 16)
                    for p in range(2):
                        for t_ in range(2):
                            for n in range(2):
                                mm = pe.matmul(ps(p, CTX), AB[:, 8 + t_, (2 * p + n) * P:(2 * p + n + 1) * P],
                                               DC[:, t_, n, :], start=(t_ == 0 and n == 0),
                                               stop=(t_ == 1 and n == 1))
                    mm.then_inc(s["y"], 1)

                @block.vector
                def _(dve):
                    dve.wait_ge(s["fw"], 1)
                    dve.tensor_copy(FW, PS[:, 0:2 * BANK].rearrange("p (x y) -> p x y", x=2)[:, :, 0:2 * P])\
                        .then_inc(s["fwc"], 1)
                    for t_ in range(10):
                        dve.wait_ge(s["ab"], t_ + 1)
                        dve.tensor_copy(AB[:, t_, :], ps(2 + t_ % 2, BANK)).then_inc(s["abc"], 1)
                    dve.wait_ge(s["l"], 8)
                    for p in range(2):
                        dve.tensor_copy(MIX[:, 6 + p, 0:SEQ], PS[:, (4 + 2 * p) * BANK:(6 + 2 * p) * BANK])\
                            .then_inc(s["yc"], 1)
                    dve.wait_ge(s["y"], 1)
                    for p in range(2):
                        dve.tensor_copy(MIX[:, 6 + p, SEQ:T], ps(p, CTX)).then_inc(s["yc"], 1)

        def heads0():
            o = O_A

            def take(*shape):
                nonlocal o
                v = big(o, *shape)
                o += int(np.prod(shape))
                return v
            qa = [take(T) for _ in range(2)]
            ka = [take(T) for _ in range(2)]
            vs = [take(10, 65) for _ in range(2)]
            wq = [take(256) for _ in range(2)]
            pr = [take(BANK) for _ in range(2)]
            raw = [take(BANK) for _ in range(2)]
            sq = [take(BANK) for _ in range(2)]
            kx = take(T)
            sk = take(T)
            t1 = take(BANK)
            lnb = take(BANK)
            mc = take(26)
            mcb = take(6).bitcast(BF16)
            o65 = take(T)
            rope = H[:, 4:6, :]
            lnr = H[:, 3, :]
            Uf = U[:, :, :].rearrange("p k n -> p (k n)")
            qb = Uf[:, 7800:7800 + T // 2].bitcast(BF16)
            kb = Uf[:, 7800 + T // 2:7800 + T].bitcast(BF16)
            NU = 22
            units = [(kt, c) for kt in range(10) for c in (0, 1)] + [(8, 2), (9, 2)]
            NM = 26
            LAST = A_HEADS - 1
            RB, NB, TB = 5, 6, 7
            with ExitStack() as c2:
                s = {n: sem("h0_" + n) for n in
                     ("tab", "w0", "w1", "one", "zero", "kr", "krc", "krt", "krm", "krp", "krs", "S", "P", "PV", "raw", "rawc",
                      "sq", "nt", "ln", "rinv", "t1", "ts", "ta", "out", "cast", "vs", "mx", "mc", "mn", "mrow",
                      "mr", "o", "bc", "lnr", "rs", "fin")}
                block = c2.enter_context(nc.Block())

                def at_least(eng, name, value):
                    if not (isinstance(value, int) and value <= 0):
                        eng.wait_ge(s[name], value)

                def step_of(u):
                    if 3 <= u <= 9:
                        return "prep", u - 3
                    if 10 <= u <= 18:
                        return "max", u - 10
                    if u == 19:
                        return "row", 0
                    return None, 0

                @block.sync
                def _(sp):
                    sp.dma_start(rope[0:A_QK], a["rope0"]).then_inc(s["tab"], 16)

                    def load(p, b):
                        sp.dma_start(wq[b], a["wqk0"][ds(p, 1)].rearrange("o p n -> (o p) n")).then_inc(s[f"w{b}"], 16)
                    load(0, 0)
                    load(1, 1)
                    with sp.Fori(0, 5) as i:
                        sp.wait_ge(s["raw"], 12 * i + 6)
                        load(2 * i + 2, 0)
                        sp.wait_ge(s["raw"], 12 * i + 12)
                        load(2 * i + 3, 1)

                @block.gpsimd
                def _(pool):
                    pool.memset(sk[0:64, :], 0.0).then_inc(s["zero"], 1)
                    pool.wait_ge(s["zero"], 1)
                    for b in range(2):
                        pool.memset(ka[b][96:97, :], 1.0).then_inc(s["one"], 1)
                    pool.wait_ge(s["one"], 2)
                    for p in range(A_HEADS):
                        b = p % 2
                        at_least(pool, "cast", 6 * p)
                        at_least(pool, "PV", NU * (p - 1))
                        pool.tensor_copy(vs[b], V0[:, :, p, :]).then_inc(s["vs"], 1)
                        at_least(pool, "mx", NM * p)
                        for w in range(6):
                            lo, hi = CH[w % 3]
                            src, dst = (ka[b], kb) if w < 3 else (qa[b], qb)
                            pool.wait_ge(s["out"], 6 * p + w + 1)
                            if w == 0:
                                pool.wait_ge(s["vs"], p + 1)
                            pool.tensor_copy(dst[0:A_QK, lo:hi], src[0:A_QK, lo:hi]).then_inc(s["cast"], 1)

                @block.tensor
                def _(pe):
                    def qk(h, b, u):
                        kt, c = units[u]
                        lo, hi = CH[c]
                        at_least(pe, "P", NU * h + u - 1)
                        if u == 0:
                            pe.wait_ge(s["mr"], h + 1)
                        pe.matmul(ps(u % 2, hi - lo), ka[b][0:97, kt * P:(kt + 1) * P], qa[b][0:97, lo:hi],
                                  start=True, stop=True).then_inc(s["S"], 1)

                    def pv(h, b, u):
                        kt, c = units[u]
                        lo, hi = CH[c]
                        pe.wait_ge(s["P"], NU * h + u + 1)
                        if u == 0:
                            pe.wait_ge(s["vs"], h + 1)
                        if u in (0, 1, 20):
                            at_least(pe, "o", 3 * h - 2 + c)
                        pe.matmul(ps(2 + c, hi - lo, slice(0, 65)), vs[b][:, kt, :], pr[u % 2][:, :hi - lo],
                                  start=(kt == (8 if c == 2 else 0)), stop=(kt == 9)).then_inc(s["PV"], 1)

                    def spread(h):
                        pe.wait_ge(s["o"], 3 * h + 3)
                        for n, (lo, hi) in enumerate(CH):
                            mm = pe.matmul(ps(RB + n, hi - lo, slice(0, 64)), cst[0:65, C_SEL:C_SEL + 64],
                                           o65[0:65, lo:hi], start=True, stop=True)
                        mm.then_inc(s["bc"], 1)

                    def project(p, b, use, w):
                        lo, hi = CH[w % 3]
                        if w == 0:
                            pe.wait_ge(s[f"w{b}"], 16 * use + 16)
                            at_least(pe, "fin", p - 1)
                        at_least(pe, "sq", 6 * p + w)
                        if w < 3:
                            mm = pe.matmul(ps(RB, hi - lo, slice(0, 64)), wq[b][:, 192:256], H[:, 2, lo:hi],
                                           start=True, stop=True)
                        else:
                            for k in range(2):
                                mm = pe.matmul(ps(RB, hi - lo, slice(0, A_QK)), wq[b][:, 96 * k:96 * k + 96],
                                               H[:, k, lo:hi], start=(k == 0), stop=(k == 1))
                        mm.then_inc(s["raw"], 1)

                    def squares(p, w):
                        lo, hi = CH[w % 3]
                        pe.wait_ge(s["sq"], 6 * p + w + 1)
                        at_least(pe, "out", 6 * p + w)
                        src = sk[0:A_QK, lo:hi] if w < 3 else sq[w % 2][0:A_QK, :hi - lo]
                        mm = pe.matmul(ps(NB, hi - lo, slice(0, A_QK)), ones[0:A_QK, 0:A_QK], src,
                                       start=True, stop=True)
                        if 3 <= w < 5:
                            mm = pe.matmul(ps(TB, hi - lo, slice(0, A_QK)), rot0[:, 0, :],
                                           raw[w % 2][0:A_QK, :hi - lo], start=True, stop=True)
                        mm.then_inc(s["nt"], 1)

                    def step(kind, n, p, b, use):
                        if kind == "prep":
                            if n < 6:
                                project(p, b, use, n)
                            if n:
                                squares(p, n - 1)
                        if kind == "max" and n < 8:
                            if n == 0:
                                pe.wait_ge(s["cast"], 6 * p + 6)
                            for c, (lo, hi) in enumerate(CH):
                                at_least(pe, "mc", NM * p + max(3 * n + c - 2, 0))
                                pe.matmul(ps(RB + c, hi - lo), qb[0:A_QK, n * P:(n + 1) * P],
                                          kb[0:A_QK, lo:hi], start=True, stop=True).then_inc(s["mx"], 1)
                        if kind == "max" and n == 8:
                            for c in range(2):
                                pe.wait_ge(s["mc"], NM * p + 3 * n + c - 2)
                                pe.matmul(ps(RB + c, CTX), qb[0:A_QK, SEQ + c * P:SEQ + (c + 1) * P],
                                          kb[0:A_QK, SEQ:T], start=True, stop=True).then_inc(s["mx"], 1)
                        if kind == "row":
                            pe.wait_ge(s["mn"], p + 1)
                            for n in range(10):
                                mm = pe.matmul(ps(RB + n // 4, BANK, slice(96, 97))[:, (n % 4) * P:(n % 4 + 1) * P],
                                               mcb[:, n:n + 1], identb[:, :], start=True, stop=True)
                            mm.then_inc(s["mrow"], 1)

                    def head(h, b, use, prep, before):
                        for u in range(NU):
                            if u + 1 < NU:
                                qk(h, b, u + 1)
                            elif prep:
                                qk(h + 1, 1 - b, 0)
                            if u == 1 and before:
                                spread(h - 1)
                            if prep:
                                step(*step_of(u), h + 1, 1 - b, use)
                            pv(h, b, u)

                    pe.wait_ge(s["tab"], 16)
                    pe.wait_ge(s["one"], 2)
                    for c, (lo, hi) in enumerate(CH):
                        pe.wait_ge(s["kr"], 1)
                        pe.wait_ge(s["zero"], 1)
                        mm = pe.matmul(ps(RB + c, hi - lo, slice(0, A_QK)), rot0[:, 1, :], sk[0:A_QK, lo:hi],
                                       start=True, stop=True)
                    mm.then_inc(s["krm"], 1)
                    pe.wait_ge(s["krc"], 1)
                    pe.wait_ge(s["krs"], 1)
                    for u in range(NU):
                        step(*step_of(u), 0, 0, 0)
                    qk(0, 0, 0)
                    head(0, 0, 0, True, False)
                    with pe.Fori(0, 5) as i:
                        head(2 * i + 1, 1, i + 1, True, True)
                        head(2 * i + 2, 0, i + 1, True, True)
                    head(LAST, 1, 0, False, True)
                    spread(LAST)

                @block.scalar
                def _(act):
                    def project(p, w):
                        lo, hi = CH[w % 3]
                        n = hi - lo
                        act.wait_ge(s["raw"], 6 * p + w + 1)
                        if w < 3:
                            at_least(act, "out", 6 * p)
                            act.activation(kx[0:64, lo:hi], ps(RB, n, slice(0, 64)), ACT.Copy,
                                           scale=sml[0:64, W_G0 + 1:W_G0 + 2]).then_inc(s["rawc"], 1)
                            act.activation(sk[0:64, lo:hi], ps(RB, n, slice(0, 64)), ACT.Square).then_inc(s["sq"], 1)
                        else:
                            at_least(act, "nt", 6 * p + w - 1)
                            if w == 3:
                                at_least(act, "out", 6 * p)
                            if w == 5:
                                act.wait_ge(s["t1"], 2 * p + 1)
                            act.activation(raw[w % 2][0:96, :n], ps(RB, n, slice(0, 96)), ACT.Copy)\
                                .then_inc(s["rawc"], 1)
                            act.activation(sq[w % 2][0:96, :n], ps(RB, n, slice(0, 96)), ACT.Square)\
                                .then_inc(s["sq"], 1)

                    def inverse(p, w):
                        lo, hi = CH[w % 3]
                        n = hi - lo
                        act.wait_ge(s["nt"], 6 * p + w + 1)
                        at_least(act, "rinv", 6 * p + w)
                        act.activation(lnb[0:96, :n], ps(NB, n, slice(0, 96)), ACT.Ln, bias=eps[0:96, 0:1],
                                       scale=1.0 / A_QK).then_inc(s["ln"], 1)
                        act.wait_ge(s["ln"], 6 * p + w + 1)
                        act.activation(ps(NB, n, slice(0, 96)), lnb[0:96, :n], ACT.Exp, scale=-0.5)\
                            .then_inc(s["rinv"], 1)

                    def step(kind, n, p, b):
                        if kind == "prep":
                            if n < 6:
                                project(p, n)
                            if n:
                                inverse(p, n - 1)
                        if kind == "row":
                            act.wait_ge(s["mrow"], p + 1)
                            act.activation(qa[b][96:97, :], PS[96:97, RB * BANK:RB * BANK + T], ACT.Copy)\
                                .then_inc(s["mr"], 1)

                    def exps(h, u):
                        lo, hi = CH[units[u][1]]
                        act.wait_ge(s["S"], NU * h + u + 1)
                        at_least(act, "PV", NU * h + u - 1)
                        act.activation(pr[u % 2][:, :hi - lo], ps(u % 2, hi - lo), ACT.Exp, scale=A_SCALE)\
                            .then_inc(s["P"], 1)

                    def inverse_sum(h):
                        act.wait_ge(s["bc"], h + 1)
                        at_least(act, "rs", h)
                        r = PS[0:64, RB * BANK:RB * BANK + T]
                        act.activation(lnr[0:64, :], r, ACT.Ln).then_inc(s["lnr"], 1)
                        act.wait_ge(s["lnr"], h + 1)
                        act.activation(r, lnr[0:64, :], ACT.Exp, scale=-1.0).then_inc(s["rs"], 1)

                    def head(h, b, prep, before):
                        for u in range(NU):
                            if u + 1 < NU:
                                exps(h, u + 1)
                            elif prep:
                                exps(h + 1, 0)
                            if u == 1 and before:
                                inverse_sum(h - 1)
                            if prep:
                                step(*step_of(u), h + 1, 1 - b)
                        act.wait_ge(s["PV"], NU * h + NU)
                        at_least(act, "fin", h)
                        for c, (lo, hi) in enumerate(CH):
                            act.activation(o65[0:65, lo:hi], ps(2 + c, hi - lo, slice(0, 65)), ACT.Copy)\
                                .then_inc(s["o"], 1)

                    act.wait_ge(s["zero"], 1)
                    act.activation(sk[64:96, :], H[0:32, 3, :], ACT.Copy).then_inc(s["kr"], 1)
                    act.wait_ge(s["krm"], 1)
                    act.wait_ge(s["krt"], 1)
                    act.activation(sk[64:96, :], H[0:32, 3, :], ACT.Square).then_inc(s["krs"], 1)
                    act.wait_ge(s["krs"], 1)
                    for u in range(NU):
                        step(*step_of(u), 0, 0)
                    exps(0, 0)
                    head(0, 0, True, False)
                    with act.Fori(0, 5) as i:
                        head(2 * i + 1, 1, True, True)
                        head(2 * i + 2, 0, True, True)
                    head(LAST, 1, False, True)
                    inverse_sum(LAST)

                @block.vector
                def _(dve):
                    def finish(h, tile, half):
                        dve.wait_ge(s["rs"], h + 1)
                        dve.tensor_tensor(MIX[64 * half:64 * half + 64, ds(tile, 1), :].rearrange("p o n -> p (o n)"),
                                          o65[0:64, :], PS[0:64, RB * BANK:RB * BANK + T], ALU.mult)\
                            .then_inc(s["fin"], 1)

                    def unit(p, b, w):
                        lo, hi = CH[w % 3]
                        n = hi - lo
                        g = sml[0:96, W_G0:W_G0 + 1]
                        norm_ = ps(NB, n, slice(0, 96))
                        if w < 3:
                            dve.wait_ge(s["rinv"], 6 * p + w + 1)
                            dve.tensor_tensor(ka[b][0:96, lo:hi], kx[0:96, lo:hi], norm_, ALU.mult)\
                                .then_inc(s["out"], 1)
                            return
                        x = raw[w % 2][0:96, :n]
                        if w == 5:
                            dve.wait_ge(s["rinv"], 6 * p + w + 1)
                            dve.scalar_tensor_tensor(out=qa[b][0:96, lo:hi], in0=x, scalar=g, in1=norm_,
                                                     op0=ALU.mult, op1=ALU.mult).then_inc(s["out"], 1)
                            return
                        v = 2 * p + w - 3
                        dve.wait_ge(s["sq"], 6 * p + w + 1)
                        at_least(dve, "out", 6 * p + w)
                        dve.scalar_tensor_tensor(out=t1[0:96, :n], in0=x, scalar=g,
                                                 in1=rope[0:96, 0, lo:hi], op0=ALU.mult, op1=ALU.mult)\
                            .then_inc(s["t1"], 1)
                        dve.wait_ge(s["nt"], 6 * p + w + 1)
                        T_ = ps(TB, n, slice(0, 96))
                        dve.tensor_tensor(T_, T_, rope[0:96, 1, lo:hi], ALU.mult).then_inc(s["ts"], 1)
                        dve.wait_ge(s["ts"], v + 1)
                        dve.tensor_tensor(t1[0:96, :n], t1[0:96, :n], T_, ALU.add).then_inc(s["ta"], 1)
                        dve.wait_ge(s["ta"], v + 1)
                        dve.wait_ge(s["rinv"], 6 * p + w + 1)
                        dve.tensor_tensor(qa[b][0:96, lo:hi], t1[0:96, :n], norm_, ALU.mult).then_inc(s["out"], 1)

                    def step(kind, n, p, b):
                        if kind == "prep" and n:
                            unit(p, b, n - 1)
                        if kind == "max":
                            for c, (lo, hi) in enumerate(CH if n < 8 else CH[2:] * 2):
                                r = 3 * n + c
                                dve.wait_ge(s["mx"], NM * p + r + 1)
                                if r == 0:
                                    at_least(dve, "mn", p)
                                dve.reduce_max(mc[:, r:r + 1], ps(RB + c, hi - lo), AX_X).then_inc(s["mc"], 1)
                        if kind == "row":
                            dve.wait_ge(s["mc"], NM * p + NM)
                            at_least(dve, "mrow", p)
                            dve.tensor_reduce(mcb[:, 0:8], mc[:, 0:24].rearrange("p (x y) -> p x y", y=3), AX_X,
                                              ALU.max, negate=True)
                            dve.tensor_scalar(mcb[:, 8:10], mc[:, 24:26], -1.0, None, ALU.mult).then_inc(s["mn"], 1)

                    dve.wait_ge(s["tab"], 16)
                    dve.wait_ge(s["kr"], 1)
                    dve.scalar_tensor_tensor(out=kx[64:96, :], in0=sk[64:96, :], scalar=sml[64:96, W_G0 + 1:W_G0 + 2],
                                             in1=rope[64:96, 0, :], op0=ALU.mult, op1=ALU.mult).then_inc(s["krt"], 1)
                    dve.wait_ge(s["krm"], 1)
                    T_ = PS[64:96, RB * BANK:RB * BANK + T]
                    dve.tensor_tensor(T_, T_, rope[64:96, 1, :], ALU.mult).then_inc(s["krp"], 1)
                    dve.wait_ge(s["krt"], 1)
                    dve.wait_ge(s["krp"], 1)
                    dve.tensor_tensor(kx[64:96, :], kx[64:96, :], T_, ALU.add).then_inc(s["krc"], 1)
                    dve.wait_ge(s["krc"], 1)
                    for u in range(NU):
                        step(*step_of(u), 0, 0)
                    for u in range(NU):
                        step(*step_of(u), 1, 1)
                    with dve.Fori(0, 5) as i:
                        finish(2 * i, i, 0)
                        for u in range(NU):
                            step(*step_of(u), 2 * i + 2, 0)
                        finish(2 * i + 1, i, 1)
                        for u in range(NU):
                            step(*step_of(u), 2 * i + 3, 1)
                    finish(10, 5, 0)
                    finish(LAST, 5, 1)

        halves = place("u0h", 0, KT, T), place("u0l", O_MIX, KT, T)
        linear("in0_", a["w_in0"], halves, 6, (T, T), O_A + 2 * T, copy_take(H, T),
               norm=split_norm("n0_", 0, 0, T, *halves, big(O_A, T), big(O_A + T, T)))
        latent_norms()
        fourier()
        heads0()
        recycle()
        halves = place("mix0h", 0, KT, T), place("mix0l", O_H, KT, T)
        norm0 = ffn_norm(0, T)
        linear("out0_", a["w_out0"], halves, KT, (T, T), O_H + KT * T, residual(0, 2, T), source=MIX,
               after=norm0)

        O_QK1 = 2 * KT * T
        O_V1 = O_QK1 + KT * T
        O_Z = O_V1 + 10 * C_KV * 65
        PAD = 8
        ZW = SEQ + 2 * PAD
        O_B = O_Z + 2 * ZW
        u1h, u1l = place("u1h", 0, KT, T), place("u1l", KT * T, KT, T)
        norm10 = split_norm("n1_", 1, 0, T, u1h, u1l, big(O_QK1, T), big(O_QK1 + T, T))
        ffn(0, T, norm0, after=norm10)
        recycle()
        MIX1 = big(0, KT, SEQ)
        QK1 = big(O_QK1, KT, T)
        V1 = big(O_V1, 10, C_KV, 65)
        Z = big(O_Z, 2, ZW)

        def pool_take(dve, m, y):
            return dve.tensor_copy(Z[:, ds(m, 1), PAD:PAD + SEQ].rearrange("p o n -> p (o n)"), y)

        def values_and_pooling():
            wv = big(O_B, KT, 256)
            wvh = place("wvh", O_B + 256 * KT, KT, 256)
            wvl = place("wvl", O_B + 512 * KT, KT, 256)
            Wd = [big(O_B + 768 * KT + n * ZW, ZW) for n in range(2)]
            inv = X[:, :, SEQ:T]
            with ExitStack() as c2:
                s = {n: sem("v1_" + n) for n in
                     ("w", "wh", "wl", "v", "vc", "one", "inv", "d", "mm", "out")}
                block = c2.enter_context(nc.Block())

                @block.sync
                def _(sp):
                    sp.dma_start(wv, a["w_v1"]).then_inc(s["w"], 16)
                    sp.dma_start(inv, a["pool_inv"].rearrange("p t (q n) -> p (t q) n", n=CTX)).then_inc(s["inv"], 16)

                @block.gpsimd
                def _(pool):
                    pool.memset(V1[:, :, :, 64], 1.0).then_inc(s["one"], 1)

                @block.scalar
                def _(act):
                    act.wait_ge(s["w"], 16)
                    act.activation(wvh[:, :, :], wv, ACT.Copy).then_inc(s["wh"], 1)
                    for t_ in range(10):
                        act.wait_ge(s["v"], t_ + 1)
                        act.activation(V1[:, t_, :, 0:64], ps(t_ % 2, 256).rearrange("p (h d) -> p h d", h=C_KV),
                                       ACT.Copy).then_inc(s["vc"], 1)

                @block.tensor
                def _(pe):
                    pe.wait_ge(s["wl"], 1)
                    for t_ in range(10):
                        if t_ >= 2:
                            pe.wait_ge(s["vc"], t_ - 1)
                        for k in range(KT):
                            for n, (left, right) in enumerate(((u1h, wvh), (u1h, wvl), (u1l, wvh))):
                                mm = pe.matmul(ps(t_ % 2, 256), left[:, k, t_ * P:(t_ + 1) * P], right[:, k, :],
                                               start=(k == 0 and n == 0), stop=(k == KT - 1 and n == 2))
                        mm.then_inc(s["v"], 1)
                    pe.wait_ge(s["d"], 4 + 5 + 7)
                    for t_ in range(2):
                        for c in range(2):
                            mm = pe.matmul(ps(4 + 2 * t_ + c, BANK), sml[:, W_PW + t_ * P:W_PW + (t_ + 1) * P],
                                           Z[:, t_, PAD + c * BANK:PAD + (c + 1) * BANK], start=True, stop=True)
                        mm.then_inc(s["mm"], 1)

                @block.vector
                def _(dve):
                    dve.wait_ge(s["wh"], 1)
                    dve.tensor_tensor(wvl[:, :, :], wv, wvh[:, :, :].bitcast(F32), ALU.subtract).then_inc(s["wl"], 1)
                    n = 0

                    def chained(op):
                        nonlocal n
                        n += 1
                        op.then_inc(s["d"], 1)
                        dve.wait_ge(s["d"], n)

                    for t_ in range(2):
                        for e in (0, PAD + SEQ):
                            chained(dve.memset(Z[:, t_, e:e + PAD], 0.0))
                    dve.wait_ge(s["inv"], 16)
                    for t_ in range(2):
                        z = Z[:, t_, :]
                        chained(dve.tensor_tensor(Wd[0][:, 1:ZW], z[:, 0:ZW - 1], z[:, 1:ZW], ALU.add))
                        chained(dve.tensor_tensor(Wd[1][:, 2:ZW - 1], Wd[0][:, 1:ZW - 2], Wd[0][:, 3:ZW], ALU.add))
                        if t_ == 1:
                            chained(dve.tensor_tensor(Wd[0][:, 4:ZW - 3], Wd[1][:, 2:ZW - 5], Wd[1][:, 6:ZW - 1],
                                                      ALU.add))
                            chained(dve.tensor_tensor(Wd[1][:, PAD:PAD + SEQ], Wd[0][:, PAD - 4:PAD + SEQ - 4],
                                                      Wd[0][:, PAD + 4:PAD + SEQ + 4], ALU.add))
                        mean = Wd[0][:, PAD:PAD + SEQ]
                        for r, src in ((0, Wd[0]), (64, Wd[1])):
                            chained(dve.tensor_tensor(
                                mean[r:r + 64, :].rearrange("p (q n) -> p q n", n=CTX),
                                src[r:r + 64, PAD:PAD + SEQ].rearrange("p (q n) -> p q n", n=CTX),
                                inv[r:r + 64, 4 * t_:4 * t_ + 4, :], ALU.mult))
                        chained(dve.tensor_tensor(z[:, PAD:PAD + SEQ], mean, z[:, PAD:PAD + SEQ], ALU.subtract))
                    for t_ in range(2):
                        dve.wait_ge(s["mm"], t_ + 1)
                        dve.tensor_scalar(MIX1[:, 6 + t_, :], PS[:, (4 + 2 * t_) * BANK:(6 + 2 * t_) * BANK],
                                          sml[:, W_PS + t_:W_PS + t_ + 1], None, ALU.mult).then_inc(s["out"], 1)

        def heads1():
            free = [[KT * SEQ, O_QK1], [O_Z, ARENA]]

            def take(*shape):
                n = int(np.prod(shape))
                part = next(f for f in free if f[1] - f[0] >= n)
                part[0] += n
                return big(part[0] - n, *shape)
            qa = [[take(SEQ) for _ in range(C_GROUP)] for _ in range(2)]
            ka = [take(T) for _ in range(2)]
            pr = [take(BANK) for _ in range(2)]
            sq = [take(BANK) for _ in range(2)]
            t1 = take(BANK)
            lnb = take(BANK)
            rope = take(2, T)
            qb = [take(SEQ // 2).bitcast(BF16) for _ in range(C_GROUP)]
            kb = take(T // 2).bitcast(BF16)
            mc = take(C_GROUP * 8)
            mcb = take(C_GROUP * 4).bitcast(BF16)
            s8 = take(C_HEADS)
            o97 = take(SEQ)
            lnr = take(SEQ)
            SB, TB, RB, NB = 4, 5, 6, 7
            WIN = [(max(t - 1, 0), min(t + 2, 8)) for t in range(8)]
            units = [(8, 0, 4), (8, 4, 8), (9, 0, 4), (9, 4, 8)] + [(t, *WIN[t]) for t in range(8)]
            NU = len(units)
            NS = 6 + 8 * C_GROUP + C_GROUP
            order = [("prep", n, 0) for n in range(6)]
            for j in range(C_GROUP):
                order += [("max", j, t_) for t_ in range(8)]
                if j:
                    order.insert(-7, ("row", j - 1, 0))
            order.append(("row", C_GROUP - 1, 0))
            assert len(order) == NS
            AHEAD = 6 + 9 + 2
            places = [(h, u) for h in range(C_HEADS) for u in range(NU) if u != 2]
            step_at = {pl: AHEAD + n for n, pl in enumerate(places) if AHEAD + n < NS * C_KV}

            def rows_before(idx):
                return [o[0] for o in order[:idx]].count("row")
            prods = [(0, 0), (0, 1), (0, 2), (1, 0), (1, 1)]
            NW = len(prods)
            with ExitStack() as c2:
                s = {n: sem("h1_" + n) for n in
                     ("tab", "one", "s8", "S", "P", "PV", "sq", "nt", "ln", "rinv",
                      "t1", "ts", "ta", "out", "cast", "mx", "mc", "mn", "mrow", "mr", "o", "es", "zero",
                      "bc", "lnr", "rs", "fin")}
                block = c2.enter_context(nc.Block())

                def at_least(eng, name, value):
                    if value > 0:
                        eng.wait_ge(s[name], value)

                def everywhere(stepper, attend, begin, end):
                    for n in range(AHEAD):
                        stepper(n, 0)
                    for g in range(C_KV):
                        for j in range(C_GROUP):
                            for u in range(NU):
                                begin(g, j, u)
                                if (C_GROUP * g + j, u) in step_at:
                                    n = step_at[C_GROUP * g + j, u]
                                    stepper(n % NS, n // NS)
                                attend(g, j, u)
                            end(g, j)

                def following(g, j, u):
                    n = NU * (C_GROUP * g + j) + u + 1
                    return (n // NU // C_GROUP, n // NU % C_GROUP, n % NU) if n < NU * C_HEADS else None

                @block.sync
                def _(sp):
                    sp.dma_start(rope, a["rope1"]).then_inc(s["tab"], 16)

                @block.gpsimd
                def _(pool):
                    pool.memset(o97[64:97, :], 0.0).then_inc(s["zero"], 1)
                    pool.wait_ge(s["zero"], 1)
                    for b in range(2):
                        pool.memset(ka[b][64:65, :], 1.0).then_inc(s["one"], 1)
                    pool.wait_ge(s["one"], 2)
                    for g in range(C_KV):
                        b = g % 2
                        at_least(pool, "mx", 8 * C_GROUP * g)
                        for w, (n, c) in enumerate(prods):
                            lo, hi = CH[c]
                            pool.wait_ge(s["out"], NW * g + w + 1)
                            if n == 0:
                                if c < 2:
                                    pool.tensor_copy(qb[2][0:64, lo:hi], qa[b][2][0:64, lo:hi])
                                op = pool.tensor_copy(kb[0:64, lo:hi], ka[b][0:64, lo:hi])
                            else:
                                pool.tensor_copy(qb[0][0:64, lo:hi], qa[b][0][0:64, lo:hi])
                                op = pool.tensor_copy(qb[1][0:64, lo:hi], qa[b][1][0:64, lo:hi])
                            op.then_inc(s["cast"], 1)

                @block.tensor
                def _(pe):
                    spreads = 0

                    def qk(g, j, u):
                        kt, q0, q1 = units[u]
                        n = (q1 - q0) * P
                        U_ = NU * (C_GROUP * g + j) + u
                        at_least(pe, "P", U_ - 1)
                        if u == 0:
                            pe.wait_ge(s["mr"], C_GROUP * g + j + 1)
                        ends = [(kt - 1 >= q0 and kt < 8, 0, 0), (kt + 1 < q1 and kt < 8, n - P, 1)]
                        last = [e for e in ends if e[0]]
                        mm = pe.matmul(ps(u % 2, n), ka[g % 2][0:65, kt * P:(kt + 1) * P],
                                       qa[g % 2][j][0:65, q0 * P:q1 * P], start=True, stop=not last)
                        for e in last:
                            mm = pe.matmul(ps(u % 2, n)[:, e[1]:e[1] + P], identb[:, :], maskb[:, e[2], :],
                                           start=False, stop=(e is last[-1]))
                        mm.then_inc(s["S"], 1)

                    def pv(g, j, u):
                        kt, q0, q1 = units[u]
                        U_ = NU * (C_GROUP * g + j) + u
                        pe.wait_ge(s["P"], U_ + 1)
                        if u < 2:
                            at_least(pe, "o", 2 * (C_GROUP * g + j) - 1 + u)
                        for c in range(2):
                            lo, hi = max(q0, 4 * c), min(q1, 4 * c + 4)
                            if lo < hi:
                                mm = pe.matmul(ps(2 + c, BANK, slice(0, 65))[:, (lo - 4 * c) * P:(hi - 4 * c) * P],
                                               V1[:, kt, g, :], pr[u % 2][:, (lo - q0) * P:(hi - q0) * P],
                                               start=(kt == 8), stop=(kt == (4 if c == 0 else 7)))
                        mm.then_inc(s["PV"], 1)

                    def spread(idx, G):
                        nonlocal spreads
                        at_least(pe, "out", NW * G + min(max(idx - 1, 0), NW))
                        at_least(pe, "mr", C_GROUP * G + rows_before(idx))
                        pe.wait_ge(s["o"], 2 * spreads + 2)
                        pe.wait_ge(s["es"], spreads + 1)
                        for c in range(2):
                            mm = pe.matmul(ps(SB + c, BANK, slice(0, 64)), cst[0:97, C_SEL:C_SEL + 64],
                                           o97[0:97, c * BANK:(c + 1) * BANK], start=True, stop=True)
                        mm.then_inc(s["bc"], 1)
                        spreads += 1

                    def step(n, G):
                        if 0 < n < NW + 1 or order[n][0] == "row":
                            at_least(pe, "fin", spreads)
                        if 0 < n < NW + 1:
                            w = n - 1
                            lo, hi = CH[prods[w][1]]
                            pe.wait_ge(s["sq"], NW * G + w + 1)
                            at_least(pe, "out", NW * G + w)
                            at_least(pe, "mr", C_GROUP * G)
                            pe.matmul(ps(NB, hi - lo), bones, sq[w % 2][:, :hi - lo], start=True, stop=True)
                            pe.matmul(ps(TB, hi - lo), rot1[:, 1 - prods[w][0], :], QK1[:, 2 * G + prods[w][0], lo:hi],
                                      start=True, stop=True).then_inc(s["nt"], 1)
                        kind, j, qt = order[n]
                        if kind == "max":
                            if n == 6:
                                pe.wait_ge(s["cast"], NW * (G + 1))
                            at_least(pe, "mc", 8 * C_GROUP * G + 8 * j + qt)
                            q = qb[j][0:64, qt * P:(qt + 1) * P]
                            lo, hi = WIN[qt]
                            pe.matmul(ps(RB, BANK)[:, CTX:BANK], q, kb[0:64, SEQ:T], start=True, stop=True)
                            nk = (hi - lo) * P
                            pe.matmul(ps(NB, nk), q, kb[0:64, lo * P:hi * P], start=True, stop=False)
                            if qt > 0:
                                mm = pe.matmul(ps(NB, P), identb[:, :], maskb[:, 0, :], start=False, stop=(qt == 7))
                            if qt < 7:
                                mm = pe.matmul(ps(NB, nk)[:, nk - P:nk], identb[:, :], maskb[:, 1, :],
                                               start=False, stop=True)
                            mm.then_inc(s["mx"], 1)
                        if kind == "row":
                            at_least(pe, "out", NW * (G + 1))
                            pe.wait_ge(s["mn"], C_GROUP * G + j + 1)
                            at_least(pe, "mr", C_GROUP * G + j)
                            for m in range(8):
                                mm = pe.matmul(ps(SB + m // 4, BANK, slice(64, 65))[:, (m % 4) * P:(m % 4 + 1) * P],
                                               mcb[:, 8 * j + m:8 * j + m + 1], identb[:, :], start=True, stop=True)
                            mm.then_inc(s["mrow"], 1)

                    def begin(g, j, u):
                        if (g, j, u) == (0, 0, 0):
                            qk(0, 0, 0)
                        if following(g, j, u):
                            qk(*following(g, j, u))
                        if u == 2 and (g or j):
                            done = AHEAD + sum(pl < (C_GROUP * g + j, u) for pl in places)
                            G, idx = divmod(min(done, NS * C_KV), NS)
                            spread(idx, G)

                    pe.wait_ge(s["tab"], 16)
                    pe.wait_ge(s["one"], 2)
                    everywhere(step, pv, begin, lambda g, j: None)
                    spread(0, C_KV)

                @block.scalar
                def _(act):
                    def step(n, G):
                        if n < NW:
                            lo, hi = CH[prods[n][1]]
                            m = hi - lo
                            at_least(act, "nt", NW * G + n - 1)
                            act.activation(sq[n % 2][:, :m], QK1[:, 2 * G + prods[n][0], lo:hi], ACT.Square)\
                                .then_inc(s["sq"], 1)
                        if 0 < n < NW + 1:
                            w = n - 1
                            lo, hi = CH[prods[w][1]]
                            m = hi - lo
                            act.wait_ge(s["nt"], NW * G + w + 1)
                            at_least(act, "rinv", NW * G + w)
                            act.activation(lnb[:, :m], ps(NB, m), ACT.Ln, bias=eps[:, 0:1], scale=1.0 / C_HD)\
                                .then_inc(s["ln"], 1)
                            act.wait_ge(s["ln"], NW * G + w + 1)
                            act.activation(ps(NB, m), lnb[:, :m], ACT.Exp, scale=-0.5).then_inc(s["rinv"], 1)
                        kind, j, _ = order[n]
                        if kind == "row":
                            act.wait_ge(s["mrow"], C_GROUP * G + j + 1)
                            act.activation(qa[G % 2][j][64:65, :], PS[64:65, SB * BANK:SB * BANK + SEQ], ACT.Copy)\
                                .then_inc(s["mr"], 1)

                    def attend(g, j, u):
                        _, q0, q1 = units[u]
                        n = (q1 - q0) * P
                        U_ = NU * (C_GROUP * g + j) + u
                        act.wait_ge(s["S"], U_ + 1)
                        at_least(act, "PV", U_ - 1)
                        act.activation(pr[u % 2][:, :n], ps(u % 2, n), ACT.Exp, scale=C_SCALE).then_inc(s["P"], 1)

                    def begin(g, j, u):
                        if (g, j, u) == (0, 0, 0):
                            attend(0, 0, 0)
                        if following(g, j, u):
                            attend(*following(g, j, u))
                        if u == 2 and (g or j):
                            inverse_sum(C_GROUP * g + j - 1)

                    def inverse_sum(h):
                        act.wait_ge(s["bc"], h + 1)
                        at_least(act, "rs", h)
                        r = PS[0:64, SB * BANK:SB * BANK + SEQ]
                        act.activation(lnr[0:64, :], r, ACT.Ln).then_inc(s["lnr"], 1)
                        act.wait_ge(s["lnr"], h + 1)
                        act.activation(r, lnr[0:64, :], ACT.Exp, scale=-1.0).then_inc(s["rs"], 1)

                    def end(g, j):
                        h = C_GROUP * g + j
                        act.wait_ge(s["PV"], NU * (h + 1))
                        at_least(act, "fin", h)
                        for c in range(2):
                            act.activation(o97[0:65, c * BANK:(c + 1) * BANK], ps(2 + c, BANK, slice(0, 65)), ACT.Copy)\
                                .then_inc(s["o"], 1)
                        act.activation(o97[96:97, :], qa[g % 2][j][64:65, :], ACT.Exp, scale=C_SCALE,
                                       bias=sml[64:65, W_SINK + h:W_SINK + h + 1]).then_inc(s["es"], 1)

                    act.wait_ge(s["zero"], 1)
                    everywhere(step, lambda g, j, u: None, begin, end)
                    inverse_sum(C_HEADS - 1)

                @block.vector
                def _(dve):
                    heads = 0

                    def finish():
                        nonlocal heads
                        h = heads
                        heads += 1
                        dve.wait_ge(s["rs"], h + 1)
                        half = 64 * (h % 2)
                        dve.tensor_tensor(MIX1[half:half + 64, h // 2, :], o97[0:64, :],
                                          PS[0:64, SB * BANK:SB * BANK + SEQ], ALU.mult).then_inc(s["fin"], 1)

                    def step(n, G):
                        b = G % 2
                        if 0 < n < NW + 1:
                            w = n - 1
                            t_, c = prods[w]
                            lo, hi = CH[c]
                            m = hi - lo
                            q = NW * G + w
                            at_least(dve, "out", q)
                            dve.scalar_tensor_tensor(out=t1[:, :m], in0=QK1[:, 2 * G + t_, lo:hi],
                                                     scalar=sml[:, W_G1 + 1 - t_:W_G1 + 2 - t_],
                                                     in1=rope[:, 0, lo:hi], op0=ALU.mult, op1=ALU.mult)\
                                .then_inc(s["t1"], 1)
                            dve.wait_ge(s["nt"], q + 1)
                            T_ = ps(TB, m)
                            dve.tensor_tensor(T_, T_, rope[:, 1, lo:hi], ALU.mult).then_inc(s["ts"], 1)
                            dve.wait_ge(s["ts"], q + 1)
                            dve.tensor_tensor(t1[:, :m], t1[:, :m], T_, ALU.add).then_inc(s["ta"], 1)
                            dve.wait_ge(s["ta"], q + 1)
                            dve.wait_ge(s["rinv"], q + 1)
                            dsts = [qa[b][2] if c < 2 else None, ka[b]] if t_ == 0 else [qa[b][0], qa[b][1]]
                            for r, dst in enumerate(dsts):
                                if dst is not None:
                                    op = dve.tensor_tensor(dst[0:64, lo:hi], t1[64 * r:64 * r + 64, :m],
                                                           ps(NB, m, slice(64 * r, 64 * r + 64)), ALU.mult)
                            op.then_inc(s["out"], 1)
                        kind, j, qt = order[n]
                        if kind == "max":
                            m = 8 * j + qt
                            dve.wait_ge(s["mx"], 8 * C_GROUP * G + m + 1)
                            if m == 0:
                                at_least(dve, "mn", C_GROUP * G)
                            lo, hi = WIN[m % 8]
                            dve.reduce_max(mc[:, m:m + 1],
                                           PS[:, RB * BANK + CTX:NB * BANK + (hi - lo) * P], AX_X)\
                                .then_inc(s["mc"], 1)
                        if kind == "row":
                            h = C_GROUP * G + j
                            dve.wait_ge(s["mc"], 8 * C_GROUP * G + 8 * (j + 1))
                            at_least(dve, "mrow", C_GROUP * G)
                            dve.tensor_scalar(mcb[:, 8 * j:8 * j + 8], mc[:, 8 * j:8 * j + 8], s8[:, h:h + 1], -1.0,
                                              ALU.max, ALU.mult).then_inc(s["mn"], 1)

                    dve.tensor_scalar(s8, sml[:, W_SINK:W_SINK + C_HEADS], 1 / C_SCALE, None, ALU.mult)\
                        .then_inc(s["s8"], 1)
                    dve.wait_ge(s["s8"], 1)
                    dve.wait_ge(s["tab"], 16)

                    def begin(g, j, u):
                        if u == 2 and (g or j):
                            finish()
                    everywhere(step, lambda g, j, u: None, begin, lambda g, j: None)
                    finish()

        def qk_take(dve, m, y):
            n = y.shape[-1]
            return dve.tensor_copy(QK1[:, ds(m, 1), 0:n].rearrange("p o n -> p (o n)"), y)

        linear("pool_", a["w_pool"], (u1h, u1l), 2, (SEQ, SEQ), O_B, pool_take,
               norm=norm10)
        linear("qk1_", a["wqk1"], (u1h, u1l), KT, (T, SEQ), O_B, qk_take)
        values_and_pooling()
        recycle()
        heads1()
        halves = place("mix1h", KT * SEQ, KT, SEQ), place("mix1l", 2 * KT * SEQ, KT, SEQ)
        norm1 = ffn_norm(1, SEQ)
        linear("out1_", a["w_out1"], halves, KT, (SEQ, SEQ), 3 * KT * SEQ, residual(1, 2, SEQ), source=MIX1,
               after=norm1)
        recycle()
        ffn(1, SEQ, norm1)
        stored = sem("stored")
        with nc.Block() as block:
            @block.sync
            def _(sp):
                sp.dma_start(out, X[:, :, 0:SEQ]).then_inc(stored, 16)
                sp.wait_ge(stored, 16)


def kernel(**inputs):
    import concourse.bacc as bacc
    from concourse.bass_utils import run_bass_kernel_spmd

    f = {k: np.asarray(v) for k, v in inputs.items()}

    def cols(v):
        return v.reshape(-1, P).T

    def rows(m):
        return m.reshape(-1, P, m.shape[-1]).transpose(1, 0, 2)

    def tiles(m, width=P):
        k, n = m.shape
        return m.reshape(k // P, P, n // width, width).transpose(2, 1, 0, 3).reshape(n // width, P, -1)

    def twice(v):
        return np.repeat(v[..., None], 2, axis=-1).reshape(v.shape[0], -1)

    z = {"xT": rows(np.concatenate([f["x"][0], f["ctx"][0]], 0).T),
         "cT": np.stack([cols(f["c"][0]), cols(f["c_ctx"])], -1)}
    z["mod_w"] = f["mod_w"].reshape(DEPTH, KT, P, -1, BANK).transpose(0, 3, 2, 1, 4).reshape(-1, P, KT, BANK)
    small = np.zeros((P, N_SMALL), np.float32)

    def put(col, v, r=0):
        small[r:r + v.shape[0], col:col + v.shape[1]] = v
    put(W_MODB, twice(cols(f["mod_b"].reshape(-1))))
    for layer in range(DEPTH):
        for n, g in enumerate((f["norm1_g"], f["norm2_g"])):
            put(W_NG + (2 * layer + n) * 2 * KT, twice(cols(g[layer])))
    put(W_CQG, cols(f["mla_cq_g"][0]))
    put(W_CKVG, cols(f["mla_ckv_g"][0]))
    put(W_G0, f["mla_q_g"].T)
    put(W_G0 + 1, f["mla_k_g"].T)
    q, k = f["win_q_g"].T, f["win_k_g"].T
    put(W_G1, np.concatenate([q, q]))
    put(W_G1 + 1, np.concatenate([q, k]))
    put(W_SINK, np.tile(f["win_sink"].reshape(1, -1), (P, 1)))
    put(W_PS, cols(f["pool_scale"][0]))
    for p in range(2):
        for i in range(2):
            put(W_FN + p * P + 64 * i, f["fnet_w"][0, 2 * p + i], 64 * i)
            put(W_PW + p * P + 64 * i, f["pool_w"][0, 2 * p + i], 64 * i)
    z["small"] = small
    w = f["mla_w_in"][0]
    pad = np.zeros((D, 96), np.float32)
    z["w_in0"] = tiles(np.concatenate([w[:, :416], pad, w[:, 416:]], 1))
    uq = f["mla_w_uq"][0].reshape(2, P, A_HEADS, A_QK).transpose(2, 1, 0, 3).reshape(A_HEADS, P, -1)
    ukv = f["mla_w_ukv"][0].reshape(P, A_HEADS, 128)
    z["wqk0"] = np.concatenate([uq, ukv[:, :, :64].transpose(1, 0, 2)], -1)
    z["w_v0"] = ukv[:, :, 64:].reshape(P, -1)
    z["w_out0"] = tiles(f["even_w_out"][0])
    w = f["win_w_in"][0]
    qs = w[:, :768].reshape(D, C_KV, C_GROUP, 64)
    ks = w[:, 768:1024].reshape(D, C_KV, 64)
    z["wqk1"] = np.concatenate([t for g in range(C_KV) for t in (
        tiles(np.concatenate([qs[:, g, 2], ks[:, g]], 1)), tiles(np.concatenate([qs[:, g, 0], qs[:, g, 1]], 1)))])
    z["w_v1"] = rows(w[:, 1024:1280])
    z["w_pool"] = tiles(w[:, 1280:])
    z["w_out1"] = tiles(f["odd_w_out"][0])
    z["w_up"] = np.stack([tiles(m) for m in f["ffn_up"]])
    z["w_down"] = f["ffn_down"].reshape(DEPTH, FT // 2, 2, P, D).transpose(0, 1, 3, 2, 4)
    conv = np.concatenate([f["ffn_conv_w"], f["ffn_conv_b"][:, None]], 1)
    z["conv"] = conv.reshape(DEPTH, 4, 2 * FT, P).transpose(0, 3, 2, 1).reshape(DEPTH, P, -1)
    z.update(constants())

    nc = bacc.Bacc("TRN2", target_bir_lowering=False, num_devices=1,
                   dynamic_dma_scratch_size=1024)
    arrays, args = {}, {}
    for name, v in z.items():
        v = np.ascontiguousarray(v)
        arrays["in_" + name] = v
        args[name] = nc.dram_tensor("in_" + name, v.shape, F32, kind="ExternalInput").ap()
    out = nc.dram_tensor("out", (P, KT, SEQ), F32, kind="ExternalOutput").ap()
    program(nc, args, out)
    r = run_bass_kernel_spmd(nc, [arrays], core_ids=[0])
    y = np.asarray(r.results[0]["out"])
    return y.transpose(2, 1, 0).reshape(1, SEQ, D)
```
